# Optimizing a Trainium2 kernel written in Bass

```python
import math
import functools
import jax
import jax.numpy as jnp
from jax import lax
import numpy as np

D_MODEL = 1024
BATCH = 1
SEQ = 1024
DEPTH = 1
DEC_BATCH = 8
DEC_SEQ = 1
PAST_LEN = 8192
PAGE_SIZE = 128

EPS = 1e-6
Q_BLOCK = 128
MLA_HEADS = 8
MLA_NOPE = 64
MLA_ROPE = 32
MLA_V = 64
Q_LORA = 256
KV_LORA = 128
ROPE_BASE = 10000.0
MLA_SCALE = (MLA_NOPE + MLA_ROPE) ** -0.5
DSA_HEADS = 8
DSA_HEAD_DIM = 64
DSA_SCALE = DSA_HEAD_DIM ** -0.5
IDX_HEADS = 8
IDX_DIM = 64
IDX_TOPK_MAX = 256
REL_BUCKETS = 32
REL_MAX_DIST = 128
N_EXPERTS = 64
TOP_K = 6
N_GROUPS = 8
TOPK_GROUPS = 4
D_EXPERT = 256
D_SHARED = 256
ROUTED_SCALE = 2.5
EXPERT_BLOCK = 128

MLA_OUT = MLA_HEADS * MLA_V
DSA_OUT = DSA_HEADS * DSA_HEAD_DIM
MIX_WIDTH = MLA_OUT + DSA_OUT
IN_SIZES = (Q_LORA, KV_LORA, MLA_ROPE, DSA_OUT, DSA_OUT, DSA_OUT, IDX_HEADS * IDX_DIM, IDX_DIM, IDX_HEADS)
D_IN = Q_LORA + KV_LORA + MLA_ROPE + 3 * DSA_OUT + IDX_HEADS * IDX_DIM + IDX_DIM + IDX_HEADS

kernel_name = 'hymba_mla_dsa_moe_adaln_step'

def rms_norm(x, g):
    xf = x.astype(jnp.float32)
    y = xf * lax.rsqrt(jnp.mean(xf * xf, axis=-1, keepdims=True) + EPS)
    return (y * g.astype(jnp.float32)).astype(x.dtype)

def adaln(c, w_ada, b_ada):
    mod = (jax.nn.silu(c) @ w_ada + b_ada)[:, None, :]
    return jnp.split(mod, 6, axis=-1)

def rope(x, pos):
    half = x.shape[-1] // 2
    inv = ROPE_BASE ** (-jnp.arange(half, dtype=jnp.float32) / half)
    ang = pos.astype(jnp.float32)[..., None] * inv
    cos, sin = jnp.cos(ang), jnp.sin(ang)
    x1 = x[..., :half].astype(jnp.float32)
    x2 = x[..., half:].astype(jnp.float32)
    return jnp.concatenate([x1 * cos - x2 * sin, x2 * cos + x1 * sin], axis=-1).astype(x.dtype)

def t5_bucket(dist):
    exact = REL_BUCKETS // 2
    d = jnp.maximum(dist, 0)
    logd = jnp.log(jnp.maximum(d, 1).astype(jnp.float32) / exact) / math.log(REL_MAX_DIST / exact)
    far = jnp.minimum(exact + (logd * (REL_BUCKETS - exact)).astype(jnp.int32), REL_BUCKETS - 1)
    return jnp.where(d < exact, d, far)

def project_mixers(h, pos, w_in, g_q_lora, w_q_up, g_kv_lora, g_mla_qn, g_mla_qr, g_mla_kr, g_dsa_q, g_dsa_k):
    B, T, _ = h.shape
    q_lat, kv_lat, kr_raw, q_d, k_d, v_d, q_i, k_i, w_i = jnp.split(
        h @ w_in, np.cumsum(IN_SIZES)[:-1].tolist(), axis=-1)
    q = (rms_norm(q_lat, g_q_lora) @ w_q_up).reshape(B, T, MLA_HEADS, MLA_NOPE + MLA_ROPE)
    q_nope = rms_norm(q[..., :MLA_NOPE], g_mla_qn)
    q_rope = rope(rms_norm(q[..., MLA_NOPE:], g_mla_qr), pos[..., None])
    c_kv = rms_norm(kv_lat, g_kv_lora)
    k_rope = rope(rms_norm(kr_raw, g_mla_kr), pos)
    q_d = rms_norm(q_d.reshape(B, T, DSA_HEADS, DSA_HEAD_DIM), g_dsa_q)
    k_d = rms_norm(k_d.reshape(B, T, DSA_HEADS, DSA_HEAD_DIM), g_dsa_k)
    v_d = v_d.reshape(B, T, DSA_HEADS, DSA_HEAD_DIM)
    q_i = q_i.reshape(B, T, IDX_HEADS, IDX_DIM)
    w_i = w_i * IDX_HEADS ** -0.5
    return (q_nope, q_rope, c_kv, k_rope, q_d, k_d, v_d, q_i, k_i, w_i)

def split_kv_up(w_kv_up):
    w = w_kv_up.reshape(KV_LORA, MLA_HEADS, MLA_NOPE + MLA_V)
    return w[..., :MLA_NOPE], w[..., MLA_NOPE:]

def mla_keys(c_kv, w_uk, g_kn):
    return rms_norm(jnp.einsum('...c,chd->...hd', c_kv, w_uk), g_kn)

def mla_attend(q_nope, q_rope, k_nope, k_rope, c_kv, key_pos, q_pos, w_uv):
    s = (jnp.einsum('qhd,shd->hqs', q_nope, k_nope).astype(jnp.float32)
         + jnp.einsum('qhr,sr->hqs', q_rope, k_rope).astype(jnp.float32)) * MLA_SCALE
    s = jnp.where((key_pos[None, :] <= q_pos[:, None])[None], s, -jnp.inf)
    p = jax.nn.softmax(s, axis=-1).astype(c_kv.dtype)
    o_lat = jnp.einsum('hqs,sc->qhc', p, c_kv)
    return jnp.einsum('qhc,chv->qhv', o_lat, w_uv).reshape(q_nope.shape[0], MLA_OUT)

def indexer_select(q_idx, w_idx, k_idx, key_pos, q_pos, n_sel):
    r = jax.nn.relu(jnp.einsum('qhd,sd->qhs', q_idx, k_idx).astype(jnp.float32) * IDX_DIM ** -0.5)
    score = jnp.einsum('qh,qhs->qs', w_idx.astype(jnp.float32), r)
    causal = key_pos[None, :] <= q_pos[:, None]
    _, sel = lax.top_k(jnp.where(causal, score, -jnp.inf), n_sel)
    return sel, key_pos[sel] <= q_pos[:, None]

def dsa_attend(q, k_sel, v_sel, sel_pos, valid, q_pos, rel_bias):
    s = jnp.einsum('qhd,qkhd->hqk', q, k_sel).astype(jnp.float32) * DSA_SCALE
    bias = rel_bias[t5_bucket(q_pos[:, None] - sel_pos)].astype(jnp.float32)
    s = jnp.where(valid[None], s + jnp.transpose(bias, (2, 0, 1)), -jnp.inf)
    p = jax.nn.softmax(s, axis=-1).astype(v_sel.dtype)
    return jnp.einsum('hqk,qkhd->qhd', p, v_sel).reshape(q.shape[0], DSA_OUT)

def gather_rows(cache, pages, new, idx, past):
    p = jnp.minimum(idx, past - 1)
    old = cache[pages[p // PAGE_SIZE], p % PAGE_SIZE]
    fresh = new[jnp.clip(idx - past, 0, new.shape[0] - 1)]
    in_past = (idx < past).reshape(idx.shape + (1,) * (old.ndim - idx.ndim))
    return jnp.where(in_past, old, fresh)

def mixers_prompt(m, w_uk, w_uv, g_mla_kn, rel_bias):
    q_nope, q_rope, c_kv, k_rope, q_d, k_d, v_d, q_i, k_i, w_i = m
    B, T = c_kv.shape[:2]
    n_blocks = T // Q_BLOCK
    n_sel = min(IDX_TOPK_MAX, T // 4)
    key_pos = jnp.arange(T)
    k_nope = mla_keys(c_kv, w_uk, g_mla_kn)

    def mla_block(i):
        q0 = i * Q_BLOCK
        q_pos = q0 + jnp.arange(Q_BLOCK)
        qn = lax.dynamic_slice_in_dim(q_nope, q0, Q_BLOCK, axis=1)
        qr = lax.dynamic_slice_in_dim(q_rope, q0, Q_BLOCK, axis=1)
        return jax.vmap(mla_attend, in_axes=(0, 0, 0, 0, 0, None, None, None))(
            qn, qr, k_nope, k_rope, c_kv, key_pos, q_pos, w_uv)

    o_mla = lax.map(mla_block, jnp.arange(n_blocks))
    o_mla = jnp.moveaxis(o_mla, 0, 1).reshape(B, T, MLA_OUT)

    def dsa_block(j):
        b, i = j // n_blocks, j % n_blocks
        q0 = i * Q_BLOCK
        q_pos = q0 + jnp.arange(Q_BLOCK)
        sl = lambda a: lax.dynamic_slice_in_dim(a[b], q0, Q_BLOCK, axis=0)
        sel, valid = indexer_select(sl(q_i), sl(w_i), k_i[b], key_pos, q_pos, n_sel)
        return dsa_attend(sl(q_d), k_d[b][sel], v_d[b][sel], key_pos[sel], valid, q_pos, rel_bias)

    o_dsa = lax.map(dsa_block, jnp.arange(B * n_blocks)).reshape(B, T, DSA_OUT)
    return jnp.concatenate([o_mla, o_dsa], axis=-1)

def mixers_sample(m, cache_lat, cache_kr, cache_k, cache_v, cache_idx, page_table,
                  w_uk, w_uv, g_mla_kn, rel_bias):
    q_nope, q_rope, c_kv, k_rope, q_d, k_d, v_d, q_i, k_i, w_i = m
    T = c_kv.shape[1]
    past = page_table.shape[1] * PAGE_SIZE
    L = past + T
    key_pos = jnp.arange(L)
    q_pos = past + jnp.arange(T)
    n_sel = min(IDX_TOPK_MAX, L // 4)

    def past_rows(cache, pages):
        return cache[pages].reshape((past,) + cache.shape[2:])

    def mla_seq(args):
        qn, qr, cn, krn, pages = args
        lat = jnp.concatenate([past_rows(cache_lat, pages), cn], axis=0)
        kr = jnp.concatenate([past_rows(cache_kr, pages), krn], axis=0)
        return mla_attend(qn, qr, mla_keys(lat, w_uk, g_mla_kn), kr, lat, key_pos, q_pos, w_uv)

    o_mla = lax.map(mla_seq, (q_nope, q_rope, c_kv, k_rope, page_table))

    def dsa_seq(qd, kd, vd, qi, ki, wi, pages):
        keys_idx = jnp.concatenate([past_rows(cache_idx, pages), ki], axis=0)
        sel, valid = indexer_select(qi, wi, keys_idx, key_pos, q_pos, n_sel)
        k_sel = gather_rows(cache_k, pages, kd, sel, past)
        v_sel = gather_rows(cache_v, pages, vd, sel, past)
        return dsa_attend(qd, k_sel, v_sel, sel, valid, q_pos, rel_bias)

    o_dsa = jax.vmap(dsa_seq)(q_d, k_d, v_d, q_i, k_i, w_i, page_table)
    return jnp.concatenate([o_mla, o_dsa], axis=-1)

def swiglu(x, w_gu, w_down):
    g, u = jnp.split(x @ w_gu, 2, axis=-1)
    return (jax.nn.silu(g) * u) @ w_down

def routed_experts(x, eidx, gate, w_e_gu, w_e_down):
    N, D = x.shape
    A = N * TOP_K
    blk = int(min(EXPERT_BLOCK, max(8, A // N_EXPERTS)))
    flat_e = eidx.reshape(-1)
    order = jnp.argsort(flat_e)
    e_sorted = flat_e[order]
    counts = jnp.zeros((N_EXPERTS,), jnp.int32).at[flat_e].add(1)
    start = jnp.cumsum(counts) - counts
    padded = (counts + blk - 1) // blk * blk
    pad_end = jnp.cumsum(padded)
    slot = (pad_end - padded)[e_sorted] + jnp.arange(A) - start[e_sorted]
    n_blocks = -(-(A + N_EXPERTS * (blk - 1)) // blk)
    n_slots = n_blocks * blk
    slot_token = jnp.full((n_slots,), N, jnp.int32).at[slot].set((order // TOP_K).astype(jnp.int32))
    slot_gate = jnp.zeros((n_slots,), x.dtype).at[slot].set(gate.reshape(-1)[order])
    block_expert = jnp.minimum(
        jnp.searchsorted(pad_end, jnp.arange(n_blocks) * blk, side='right'), N_EXPERTS - 1)
    x_pad = jnp.concatenate([x, jnp.zeros((1, D), x.dtype)], axis=0)
    xb = x_pad[slot_token].reshape(n_blocks, blk, D)
    yb = lax.map(lambda a: swiglu(a[0], w_e_gu[a[1]], w_e_down[a[1]]), (xb, block_expert))
    y = jnp.zeros((N + 1, D), x.dtype).at[slot_token].add(yb.reshape(n_slots, D) * slot_gate[:, None])
    return y[:N]

def moe(h, w_router, b_router, w_e_gu, w_e_down, w_s_gu, w_s_down):
    B, T, D = h.shape
    xt = h.reshape(B * T, D)
    N = xt.shape[0]
    scores = jax.nn.sigmoid((xt @ w_router).astype(jnp.float32))
    biased = scores + b_router.astype(jnp.float32)
    grp_score = lax.top_k(biased.reshape(N, N_GROUPS, N_EXPERTS // N_GROUPS), 2)[0].sum(-1)
    _, top_g = lax.top_k(grp_score, TOPK_GROUPS)
    gmask = jnp.any(top_g[..., None] == jnp.arange(N_GROUPS), axis=1)
    masked = jnp.where(jnp.repeat(gmask, N_EXPERTS // N_GROUPS, axis=1), biased, -jnp.inf)
    _, eidx = lax.top_k(masked, TOP_K)
    w = jnp.take_along_axis(scores, eidx, axis=1)
    w = w / jnp.sum(w, axis=-1, keepdims=True) * ROUTED_SCALE
    routed = routed_experts(xt, eidx, w.astype(xt.dtype), w_e_gu, w_e_down)
    return (routed + swiglu(xt, w_s_gu, w_s_down)).reshape(B, T, D)

def setup_inputs(seed: int = 0) -> dict:
    key = jax.random.key(seed)
    ks = iter(jax.random.split(key, 48))
    nrm = lambda shape, scale=1.0: jax.random.normal(next(ks), shape, jnp.float32) * scale
    gain = lambda shape: 1.0 + 0.05 * jax.random.normal(next(ks), shape, jnp.float32)
    n_pages = PAST_LEN // PAGE_SIZE
    n_used = DEC_BATCH * n_pages
    n_pool = n_used + max(1, n_used // 4)
    pool = lambda *tail: nrm((DEPTH, n_pool, PAGE_SIZE) + tail)
    return {
        'x_prompt': nrm((BATCH, SEQ, D_MODEL)),
        'x_sample': nrm((DEC_BATCH, DEC_SEQ, D_MODEL)),
        'cache_mla_latent': pool(KV_LORA),
        'cache_mla_krope': pool(MLA_ROPE),
        'cache_dsa_k': pool(DSA_HEADS, DSA_HEAD_DIM),
        'cache_dsa_v': pool(DSA_HEADS, DSA_HEAD_DIM),
        'cache_idx_k': pool(IDX_DIM),
        'page_table': jax.random.permutation(next(ks), n_pool)[:n_used].reshape(DEC_BATCH, n_pages).astype(jnp.int32),
        'c_prompt': nrm((BATCH, D_MODEL)),
        'c_sample': nrm((DEC_BATCH, D_MODEL)),
        'rel_bias': nrm((REL_BUCKETS, DSA_HEADS), 0.5),
        'w_ada': nrm((DEPTH, D_MODEL, 6 * D_MODEL), 0.5 * D_MODEL ** -0.5),
        'b_ada': nrm((DEPTH, 6 * D_MODEL), 0.02),
        'g_attn_norm': gain((DEPTH, D_MODEL)),
        'w_in': nrm((DEPTH, D_MODEL, D_IN), D_MODEL ** -0.5),
        'g_q_lora': gain((DEPTH, Q_LORA)),
        'w_q_up': nrm((DEPTH, Q_LORA, MLA_HEADS * (MLA_NOPE + MLA_ROPE)), Q_LORA ** -0.5),
        'g_kv_lora': gain((DEPTH, KV_LORA)),
        'w_kv_up': nrm((DEPTH, KV_LORA, MLA_HEADS * (MLA_NOPE + MLA_V)), KV_LORA ** -0.5),
        'g_mla_qn': gain((DEPTH, MLA_NOPE)),
        'g_mla_qr': gain((DEPTH, MLA_ROPE)),
        'g_mla_kn': gain((DEPTH, MLA_NOPE)),
        'g_mla_kr': gain((DEPTH, MLA_ROPE)),
        'g_dsa_q': gain((DEPTH, DSA_HEAD_DIM)),
        'g_dsa_k': gain((DEPTH, DSA_HEAD_DIM)),
        'w_out': nrm((DEPTH, MIX_WIDTH, D_MODEL), MIX_WIDTH ** -0.5),
        'g_ffn_norm': gain((DEPTH, D_MODEL)),
        'w_router': nrm((DEPTH, D_MODEL, N_EXPERTS), D_MODEL ** -0.5),
        'b_router': nrm((DEPTH, N_EXPERTS), 0.01),
        'w_e_gu': nrm((DEPTH, N_EXPERTS, D_MODEL, 2 * D_EXPERT), D_MODEL ** -0.5),
        'w_e_down': nrm((DEPTH, N_EXPERTS, D_EXPERT, D_MODEL), D_EXPERT ** -0.5),
        'w_s_gu': nrm((DEPTH, D_MODEL, 2 * D_SHARED), D_MODEL ** -0.5),
        'w_s_down': nrm((DEPTH, D_SHARED, D_MODEL), D_SHARED ** -0.5),
    }

def reference(x_prompt, x_sample, cache_mla_latent, cache_mla_krope, cache_dsa_k, cache_dsa_v,
              cache_idx_k, page_table, c_prompt, c_sample, rel_bias, w_ada, b_ada, g_attn_norm,
              w_in, g_q_lora, w_q_up, g_kv_lora, w_kv_up, g_mla_qn, g_mla_qr, g_mla_kn, g_mla_kr,
              g_dsa_q, g_dsa_k, w_out, g_ffn_norm, w_router, b_router, w_e_gu, w_e_down,
              w_s_gu, w_s_down):
    past = page_table.shape[1] * PAGE_SIZE
    pos_p = jnp.arange(x_prompt.shape[1])[None, :]
    pos_s = past + jnp.arange(x_sample.shape[1])[None, :]
    xp, xs = x_prompt, x_sample
    new_p, new_s = [], []
    for l in range(DEPTH):
        w_uk, w_uv = split_kv_up(w_kv_up[l])
        proj = functools.partial(
            project_mixers, w_in=w_in[l], g_q_lora=g_q_lora[l], w_q_up=w_q_up[l], g_kv_lora=g_kv_lora[l],
            g_mla_qn=g_mla_qn[l], g_mla_qr=g_mla_qr[l], g_mla_kr=g_mla_kr[l],
            g_dsa_q=g_dsa_q[l], g_dsa_k=g_dsa_k[l])
        ffn = functools.partial(
            moe, w_router=w_router[l], b_router=b_router[l], w_e_gu=w_e_gu[l], w_e_down=w_e_down[l],
            w_s_gu=w_s_gu[l], w_s_down=w_s_down[l])
        sa_p, ca_p, ga_p, sf_p, cf_p, gf_p = adaln(c_prompt, w_ada[l], b_ada[l])
        sa_s, ca_s, ga_s, sf_s, cf_s, gf_s = adaln(c_sample, w_ada[l], b_ada[l])
        mp = proj(rms_norm(xp, g_attn_norm[l]) * (1 + ca_p) + sa_p, pos_p)
        ms = proj(rms_norm(xs, g_attn_norm[l]) * (1 + ca_s) + sa_s, pos_s)
        o_p = mixers_prompt(mp, w_uk, w_uv, g_mla_kn[l], rel_bias)
        o_s = mixers_sample(ms, cache_mla_latent[l], cache_mla_krope[l], cache_dsa_k[l], cache_dsa_v[l],
                            cache_idx_k[l], page_table, w_uk, w_uv, g_mla_kn[l], rel_bias)
        xp = xp + ga_p * (o_p @ w_out[l])
        xs = xs + ga_s * (o_s @ w_out[l])
        xp = xp + gf_p * ffn(rms_norm(xp, g_ffn_norm[l]) * (1 + cf_p) + sf_p)
        xs = xs + gf_s * ffn(rms_norm(xs, g_ffn_norm[l]) * (1 + cf_s) + sf_s)
        new_p.append((mp[2], mp[3], mp[5], mp[6], mp[8]))
        new_s.append((ms[2], ms[3], ms[5], ms[6], ms[8]))
    sp = [jnp.stack(a) for a in zip(*new_p)]
    ss = [jnp.stack(a) for a in zip(*new_s)]
    return (xp, xs, sp[0], sp[1], sp[2], sp[3], sp[4], ss[0], ss[1], ss[2], ss[3], ss[4])


_drawn_inputs = setup_inputs


def setup_inputs(seed=0):
    import zlib

    import numpy as np

    out = dict(_drawn_inputs(seed))
    spreads = {}
    factors = {'cache_mla_latent': 8.0,
     'cache_mla_krope': 8.0,
     'g_q_lora': 8.0,
     'g_mla_qn': 8.0,
     'g_mla_qr': 8.0,
     'g_mla_kn': 7.918,
     'g_dsa_q': 6.49}
    for name, (base, spread) in spreads.items():
        noise = np.random.default_rng([zlib.crc32(name.encode()), seed]).standard_normal(out[name].shape)
        drawn = base * np.exp(spread * noise) if base else spread * noise
        out[name] = jnp.asarray(drawn.astype(out[name].dtype))
    for name, factor in factors.items():
        out[name] = (out[name] * factor).astype(out[name].dtype)
    return out
```

```python
import math
from contextlib import ExitStack

import numpy as np
import concourse.bass as bass
from concourse import mybir

F32 = mybir.dt.float32
I32 = mybir.dt.int32
U32 = mybir.dt.uint32
BF16 = mybir.dt.bfloat16
ALU = mybir.AluOpType
ACT = mybir.ActivationFunctionType
AX = mybir.AxisListType
RMAX = bass.bass_isa.ReduceOp.max

P = 128
D = 1024
KD = D // P
SEQ, NS, PAST, PAGE = 1024, 8, 8192, 128
NT = SEQ // P
NTOK = SEQ + NS
NPG = PAST // PAGE
EPS = 1e-6
H, NOPE, ROPE, VD = 8, 64, 32, 64
QK = NOPE + ROPE
QL, KVL, IDX = 256, 128, 64
MLA_SCALE = QK ** -0.5
DSA_SCALE = 64 ** -0.5
TOPK = 256
NB_REL = 32
NE, TK, NG, TKG, DE = 64, 6, 8, 4, 256
ROUTED_SCALE = 2.5
C_Q, C_KV, C_KR = 0, 256, 384
C_QD, C_KD, C_VD, C_QI, C_KI, C_WI = 416, 928, 1440, 1952, 2464, 2528
D_IN = 2536
NEG = -3.0e38
NC9 = NS + 1
NBLK = NE + (NTOK * TK - NE) // P
NBLK += NBLK % 2
SLOTS = NBLK * P
BIGM = 1.0e9


def t5_bucket(d):
    exact = NB_REL // 2
    if d < exact:
        return max(d, 0)
    return min(exact + int(math.log(d / exact) / math.log(128 / exact) * (NB_REL - exact) + 1e-9), NB_REL - 1)


def shape_constants():
    c = {}
    i, j = np.arange(P)[:, None], np.arange(P)[None, :]
    c["ident"] = (i == j)
    c["causal"] = np.where(j <= i, 0.0, NEG)
    c["before"] = (i < j)
    c["ones"] = np.ones((P, P))
    c["same_half"] = (i // 64 == j // 64)
    c["before_half"] = (i < j) & (i // 64 == j // 64)
    c["iota"] = np.arange(P)[None, :] + np.zeros((P, 1))
    c["part"] = i
    c["page_of"] = i % 64
    c["half32"] = 16.0 * (i // 64)
    c["half_neg"] = np.where(np.stack([i[:, 0] < 64, i[:, 0] >= 64], 1), 0.0, NEG)
    c["half_one"] = np.stack([i[:, 0] < 64, i[:, 0] >= 64], 1)
    c["fresh_neg"] = np.where(i % 64 == 63, 0.0, NEG)
    dist = np.arange(384) - 127
    b = np.array([t5_bucket(int(x)) for x in dist])
    c["rel_onehot"] = np.concatenate([b[None, :] == np.arange(NB_REL)[:, None], np.zeros((P - NB_REL, 384))])
    thr = [min(x for x in range(0, 200) if t5_bucket(x) >= k) for k in range(1, NB_REL)]
    c["rel_from"] = np.array(thr)[None, :] + np.zeros((P, 1))
    c["row8"] = np.where(i == NS, 1.0, 0.0) + np.zeros((1, P))
    hb = np.zeros((P, H, 64))
    for p in range(16):
        hb[p, p % 8] = 1.0
    c["own_head"] = hb.reshape(P, 512)
    es = np.zeros((P, NS, NS))
    for p in range(16):
        for s in range(NS):
            es[p, s, s] = p < 8
    c["to_row"] = es.reshape(P, NS * NS)
    ep = np.zeros((P, NS // 2, NS))
    for p in range(16):
        for s in range(NS // 2):
            ep[p, s, 2 * s + p // 8] = 1.0
    c["to_pair"] = ep.reshape(P, NS // 2 * NS)
    c["lower8"] = np.tile((np.arange(8)[None, :] < np.arange(8)[:, None]).reshape(1, 64), (P, 1))
    c["is_token"] = np.stack([np.ones(P)] * NT + [np.arange(P) < NS], 1)
    c = {k: np.asarray(v, np.float32) for k, v in c.items()}
    b = np.empty((P, 31), np.int32)
    b[:] = np.int32(1) << np.arange(30, -1, -1, dtype=np.int32)
    c["bits"] = b.view(np.float32)
    at, cols, n = {}, [], 0
    for k, v in c.items():
        at[k] = (n, v.shape[1])
        cols.append(v)
        n += v.shape[1]
    return at, np.ascontiguousarray(np.concatenate(cols, 1))


def rope_table():
    half = ROPE // 2
    inv = (np.float32(10000.0) ** (-np.arange(half, dtype=np.float32) / np.float32(half))).astype(np.float32)
    pos = np.concatenate([np.arange(SEQ), np.full(NS, PAST)]).astype(np.float32)
    a = (pos[:, None] * inv[None, :]).astype(np.float32)
    return np.concatenate([np.cos(a), np.sin(a)], 1).astype(np.float32)


CONST_AT, CONST = shape_constants()


def build(nc, T):
    root = ExitStack()
    with root:
        sem_cache = {}

        def sem(name):
            if name not in sem_cache:
                sem_cache[name] = nc.alloc_semaphore(name)
            return sem_cache[name]

        stage_name = [""]

        def alloc(ctx):
            def sb(name, shape, dt=F32):
                return ctx.enter_context(nc.sbuf_tensor(stage_name[0] + name, shape, dt))

            def ps(name, dt=F32):
                return ctx.enter_context(nc.psum_tensor(stage_name[0] + name, [P, 512], dt))
            return sb, ps

        sb, _ = alloc(root)
        K = sb("K", [P, CONST.shape[1]])
        G = {"K": K, "c": lambda k: K[:, CONST_AT[k][0]:CONST_AT[k][0] + CONST_AT[k][1]]}
        for n in ("Aa", "Ba", "Af", "Bf"):
            G[n] = sb(n, [P, KD, NC9])
        G["lg"] = sb("lg", [P, NT + 1, NE])
        G["gate"] = sb("gate", [P, NT + 1, TK])
        G["slot"] = sb("slot", [P, NT + 1, 8], I32)
        G["expert"] = sb("expert", [2, P], I32)
        G["nblk"] = sb("nblk", [1, 1], I32)
        G["list"] = sb("list", [P, NBLK], I32)
        for st in (stage_ada, stage_in, stage_mix, stage_prompt, stage_sample, stage_out, stage_dispatch, stage_shared, stage_routed,
                   stage_combine):
            stage_name[0] = st.__name__[6:] + "_"
            with ExitStack() as ctx:
                st(nc, T, G, sem, *alloc(ctx))
            nc.clear_and_free_semaphores(list(sem_cache.values()))
            nc.all_engine_barrier()
            sem_cache.clear()


def serial(eng, s):
    n = [0]

    def link(ins):
        n[0] += 1
        ins.then_inc(s, 1)
        eng.wait_ge(s, n[0])
    return link


def stage_ada(nc, T, G, sem, sb, ps):
    K, c = G["K"], G["c"]
    NCH = 6 * D // 512
    cs = sb("cs", [NC9, D])
    sc = sb("sc", [NC9, D])
    cT = sb("cT", [P, KD, NC9])
    W = [sb(f"Wada{i}", [P, KD, 512]) for i in range(3)]
    mod = sb("mod", [NC9, 6 * D])
    badd = sb("badd", [NC9, 6 * D])
    gr = sb("gr", [2 * KD, P])
    gT = sb("gT", [P, 2 * KD])
    one = sb("one", [P, KD * NC9])
    pt, pg, pm = ps("pt"), ps("pg"), [ps("pm0"), ps("pm1")]
    s_k, s_c, s_w = sem("ada_const"), sem("ada_c"), [sem(f"ada_w{i}") for i in range(3)]
    s_sc, s_cT, s_cTs, s_mm, s_mod, s_out = (sem("ada_" + n) for n in ("silu", "cT", "cTs", "mm", "mod", "out"))
    s_tr, s_gt, s_v = sem("ada_tr"), sem("ada_gt"), sem("ada_v")
    with nc.Block() as block:
        @block.sync
        def _(sp):
            sp.dma_start(K[:, :], T["const"]).then_inc(s_k, 16)
            sp.dma_start(cs[0:NS, :], T["c_sample"]).then_inc(s_c, 16)
            sp.dma_start(cs[NS:NC9, :], T["c_prompt"]).then_inc(s_c, 16)
            sp.dma_start(gr[0:KD, :], T["g_attn_norm"][0].rearrange("(k p) -> k p", p=P)).then_inc(s_c, 16)
            sp.dma_start(gr[KD:2 * KD, :], T["g_ffn_norm"][0].rearrange("(k p) -> k p", p=P)).then_inc(s_c, 16)
            sp.dma_start(badd[:, :], T["b_ada"].to_broadcast([NC9, 6 * D])).then_inc(s_c, 16)
            for g in range(NCH):
                if g >= 3:
                    sp.wait_ge(s_mm, g - 2)
                sp.dma_start(W[g % 3][:, :, :], T["w_ada"][0, :, 512 * g:512 * g + 512]
                             .rearrange("(k p) n -> p k n", p=P)).then_inc(s_w[g % 3], 16)
            sp.wait_ge(s_mod, NCH)
            sp.dma_start(T["mod"], mod[:, :]).then_inc(s_out, 16)
            sp.wait_ge(s_out, 16)

        @block.scalar
        def _(act):
            act.wait_ge(s_c, 80)
            act.activation(sc[:, :], cs[:, :], ACT.Sigmoid).then_inc(s_sc, 1)

        @block.tensor
        def _(pe):
            pe.wait_ge(s_k, 16)
            pe.wait_ge(s_sc, 2)
            for k in range(KD):
                m = pe.transpose(pt[:, k * NC9:(k + 1) * NC9], sc[:, k * P:(k + 1) * P], c("ident")[0:NC9, 0:NC9])
            m.then_inc(s_cT, 1)
            pe.transpose(pg[:, 0:2 * KD], gr[:, :], c("ident")[0:2 * KD, 0:2 * KD]).then_inc(s_gt, 1)
            pe.wait_ge(s_cTs, 1)
            for g in range(NCH):
                pe.wait_ge(s_w[g % 3], 16 * (g // 3 + 1))
                if g >= 2:
                    pe.wait_ge(s_mod, g - 1)
                for k in range(KD):
                    m = pe.matmul(pm[g % 2][0:NC9, :], cT[:, k, :], W[g % 3][:, k, :], start=(k == 0), stop=(k == KD - 1))
                m.then_inc(s_mm, 1)
            pe.wait_ge(s_mod, NCH)
            pe.wait_ge(s_gt, 2)
            for j, part in enumerate((0, 1, 3, 4)):
                for k in range(KD):
                    a = part * D + k * P
                    m = pe.transpose(pg[:, (j * KD + k) * NC9:(j * KD + k + 1) * NC9], mod[:, a:a + P],
                                     c("ident")[0:NC9, 0:NC9])
            m.then_inc(s_tr, 1)

        @block.vector
        def _(dve):
            link = serial(dve, s_v)
            dve.wait_ge(s_sc, 1)
            dve.tensor_tensor(sc[:, :], sc[:, :], cs[:, :], ALU.mult).then_inc(s_sc, 1)
            link(dve.memset(one[:, :], 1.0))
            dve.wait_ge(s_cT, 1)
            dve.tensor_copy(cT[:, :, :].rearrange("p k n -> p (k n)"), pt[:, 0:KD * NC9]).then_inc(s_cTs, 1)
            dve.wait_ge(s_gt, 1)
            dve.tensor_copy(gT[:, :], pg[:, 0:2 * KD]).then_inc(s_gt, 1)
            for g in range(NCH):
                dve.wait_ge(s_mm, g + 1)
                dve.tensor_tensor(mod[:, 512 * g:512 * g + 512], pm[g % 2][0:NC9, :],
                                  badd[:, 512 * g:512 * g + 512], ALU.add).then_inc(s_mod, 1)
            dve.wait_ge(s_tr, 1)
            for j, (a, b) in enumerate((("Aa", "Ba"), ("Af", "Bf"))):
                n = KD * NC9
                link(dve.tensor_copy(G[b][:, :, :].rearrange("p k n -> p (k n)"), pg[:, 2 * j * n:(2 * j + 1) * n]))
                link(dve.tensor_tensor(G[a][:, :, :].rearrange("p k n -> p (k n)"),
                                       pg[:, (2 * j + 1) * n:(2 * j + 2) * n], one[:, :], ALU.add))
                link(dve.tensor_tensor(G[a][:, :, :], G[a][:, :, :],
                                       gT[:, j * KD:(j + 1) * KD].unsqueeze(2).to_broadcast([P, KD, NC9]), ALU.mult))


def tiles():
    return [(t, P if t < NT else NS) for t in range(NT + 1)]


def token_rows(prompt, sample, t):
    return prompt[t * P:(t + 1) * P, :] if t < NT else sample


def stage_in(nc, T, G, sem, sb, ps):
    c = G["c"]
    Win = sb("Win", [P, KD, D_IN])
    x = [sb(f"x{i}", [P, D]) for i in range(2)]
    xn = [sb(f"xn{i}", [P, D]) for i in range(2)]
    hT = [sb(f"hT{i}", [P, KD, P]) for i in range(2)]
    pr = [sb(f"pr{i}", [P, D_IN]) for i in range(2)]
    junk, st = sb("junk", [P, D]), sb("st", [P, 4, NT + 1])
    epst = sb("epst", [P, 1])
    pt = [ps("pt0"), ps("pt1")]
    pp = [ps(f"pp{i}") for i in range(5)]
    cols = [(0, 512), (512, 1024), (1024, 1536), (1536, 2048), (2048, D_IN)]
    s_w, s_x, s_ss, s_rs, s_xn, s_t, s_h, s_p, s_e, s_o, s_eps, s_b = (
        sem("in_" + n) for n in ("w", "x", "ss", "rstd", "xn", "t", "h", "p", "evac", "out", "eps", "b"))
    s_xs, s_wc = [sem("in_x0"), sem("in_x1")], [sem(f"in_w{g}") for g in range(5)]
    s_os = [sem("in_o0"), sem("in_o1")]
    xp, xs = T["x_prompt"][0], T["x_sample"].rearrange("b s d -> (b s) d")
    with nc.Block() as block:
        @block.sync
        def _(sp):
            for t, R in tiles():
                if t >= 2:
                    sp.wait_ge(s_xn, t - 1)
                sp.dma_start(x[t % 2][0:R, :], token_rows(xp, xs, t)).then_inc(s_xs[t % 2], 16)
                if t == 0:
                    for g, (a, b) in enumerate(cols):
                        sp.dma_start(Win[:, :, a:b], T["w_in"][0, :, a:b].rearrange("(k p) n -> p k n", p=P)).then_inc(s_wc[g], 16)

        def evac(eng, t, groups):
            R = P if t < NT else NS
            for g in groups:
                a, b = cols[g]
                if t >= 2:
                    eng.wait_ge(s_os[t % 2], 16 * (t // 2))
                eng.wait_ge(s_p, 5 * t + g + 1)
                if g in (1, 3):
                    eng.activation(pr[t % 2][0:R, a:b], pp[g][0:R, 0:b - a], ACT.Copy).then_inc(s_e, 1)
                else:
                    eng.tensor_copy(pr[t % 2][0:R, a:b], pp[g][0:R, 0:b - a]).then_inc(s_e, 1)

        @block.scalar
        def _(act):
            act.wait_ge(s_eps, 1)
            for t, R in tiles():
                act.wait_ge(s_xs[t % 2], 16 * (t // 2 + 1))
                if t >= 1:
                    act.wait_ge(s_rs, 2 * t)
                act.activation(junk[0:R, :], x[t % 2][0:R, :], ACT.Square, accum_out=st[0:R, 0, t:t + 1]).then_inc(s_ss, 1)
                act.wait_ge(s_ss, t + 1)
                act.activation(st[0:R, 1, t:t + 1], st[0:R, 0, t:t + 1], ACT.Sqrt, scale=1.0 / D, bias=epst[0:R, 0:1]).then_inc(s_rs, 1)
                act.wait_ge(s_rs, 2 * t + 2)
                if t >= 2:
                    act.wait_ge(s_t, t - 1)
                act.activation(xn[t % 2][0:R, :], x[t % 2][0:R, :], ACT.Copy, scale=st[0:R, 2, t:t + 1]).then_inc(s_xn, 1)
                if t >= 1:
                    evac(act, t - 1, (1, 3))
            evac(act, NT, (1, 3))

        @block.gpsimd
        def _(pool):
            for t, R in tiles():
                pool.wait_ge(s_e, 5 * t + 5)
                pool.dma_start(T["p"][t * P:t * P + R, :], pr[t % 2][0:R, :]).then_inc(s_os[t % 2], 16)
            pool.wait_ge(s_os[0], 16 * 5)
            pool.wait_ge(s_os[1], 16 * 4)

        @block.tensor
        def _(pe):
            def turn(t, R):
                pe.wait_ge(s_xn, t + 1)
                if t >= 1:
                    pe.wait_ge(s_h, 8 * t)
                for k in range(KD):
                    m = pe.transpose(pt[k // 4][:, (k % 4) * P:(k % 4) * P + R], xn[t % 2][0:R, k * P:(k + 1) * P],
                                     c("ident")[0:R, 0:R])
                m.then_inc(s_t, 1)

            turn(*tiles()[0])
            for t, R in tiles():
                if t < NT:
                    turn(*tiles()[t + 1])
                pe.wait_ge(s_h, 8 * (t + 1))
                for g, (a, b) in enumerate(cols):
                    if t == 0:
                        pe.wait_ge(s_wc[g], 16)
                    else:
                        pe.wait_ge(s_e, 5 * t)
                    for k in range(KD):
                        m = pe.matmul(pp[g][0:R, 0:b - a], hT[t % 2][:, k, 0:R], Win[:, k, a:b],
                                      start=(k == 0), stop=(k == KD - 1))
                    m.then_inc(s_p, 1)

        @block.vector
        def _(dve):
            dve.memset(epst[:, :], EPS).then_inc(s_eps, 1)
            for t, R in tiles():
                dve.wait_ge(s_rs, 2 * t + 1)
                dve.reciprocal(st[0:R, 2, t:t + 1], st[0:R, 1, t:t + 1]).then_inc(s_rs, 1)
                dve.wait_ge(s_t, t + 1)
                if t >= 2:
                    dve.wait_ge(s_p, 5 * (t - 1))
                for k in range(KD):
                    src = pt[k // 4][:, (k % 4) * P:(k % 4) * P + R]
                    if t < NT:
                        dve.tensor_scalar(hT[t % 2][:, k, :], src, G["Aa"][:, k, NS:NC9], G["Ba"][:, k, NS:NC9],
                                          ALU.mult, ALU.add).then_inc(s_h, 1)
                    else:
                        dve.tensor_tensor(hT[t % 2][:, k, 0:R], src, G["Aa"][:, k, 0:NS], ALU.mult).then_inc(s_b, 1)
                        dve.wait_ge(s_b, k + 1)
                        dve.tensor_tensor(hT[t % 2][:, k, 0:R], hT[t % 2][:, k, 0:R], G["Ba"][:, k, 0:NS],
                                          ALU.add).then_inc(s_h, 1)
                if t >= 1:
                    evac(dve, t - 1, (0, 2, 4))
            evac(dve, NT, (0, 2, 4))


def stage_mix(nc, T, G, sem, sb, ps):
    c = G["c"]
    Wq = sb("Wq", [P, 2, H * QK])
    Wkv = sb("Wkv", [P, H, NOPE + VD])
    gains = {n: sb("m_" + n, [P, w]) for n, w in (("g_q_lora", QL), ("g_kv_lora", KVL), ("g_mla_qn", NOPE), ("g_mla_qr", ROPE),
                                                  ("g_mla_kn", NOPE), ("g_mla_kr", ROPE), ("g_dsa_q", 64), ("g_dsa_k", 64))}
    pr = [sb(f"mp{i}", [P, D_IN]) for i in range(2)]
    cs = [sb(f"mcs{i}", [P, ROPE]) for i in range(2)]
    ql = sb("ql", [P, QL])
    ckv = sb("ckv", [P, KVL])
    krr = sb("krr", [P, ROPE])
    qd, kd = sb("qd", [P, 512]), sb("kd", [P, 512])
    qm, km = sb("qm", [P, H, QK]), sb("km", [P, H, QK])
    vm = sb("vm", [P, 512])
    kir = sb("kir", [P, 2 * IDX])
    qlT, ckvT = sb("qlT", [P, 2, P]), sb("ckvT", [P, P])
    tq = sb("tq", [P, 16, P])
    td = sb("td", [P, 13, P])
    sq = sb("sq", [P, 768])
    r8 = sb("r8", [P, 3, 8])
    rt = sb("rt", [P, H, ROPE])
    eps = sb("meps", [P, 1])
    pA, pq, pk, pv = ps("mA"), [ps("mq0"), ps("mq1")], ps("mk"), ps("mv")
    pT = [ps("mT0"), ps("mT1"), ps("mT2")]
    s_w, s_v, s_pr, s_o, s_tr, s_qT, s_ckT, s_q, s_kv = (sem("mx_" + n) for n in
                                                         ("w", "v", "p", "o", "tr", "qT", "ckT", "q", "kv"))
    s_in = [sem("mx_in0"), sem("mx_in1")]
    s_root, s_rooted, s_vm, s_rows, s_lat, s_tT, s_te = (sem("mx_" + n) for n in
                                                         ("root", "rooted", "vm", "rows", "lat", "tT", "te"))
    s_rd = sem("mx_read")
    NR = 8
    with nc.Block() as block:
        @block.sync
        def _(sp):
            sp.dma_start(Wq[:, :, :], T["w_q_up"][0].rearrange("(k p) n -> p k n", p=P)).then_inc(s_w, 16)
            sp.dma_start(Wkv[:, :, :], T["w_kv_up"][0].rearrange("p (h n) -> p h n", h=H)).then_inc(s_w, 16)
            for n, g in gains.items():
                sp.dma_start(g[:, :], T[n].to_broadcast([P, g.shape[1]])).then_inc(s_w, 16)
            for t, R in tiles():
                if t >= 2:
                    sp.wait_ge(s_rd, 2 * (t - 1))
                sp.dma_start(pr[t % 2][0:R, :], T["p"][t * P:t * P + R, :]).then_inc(s_in[t % 2], 16)
                sp.dma_start(cs[t % 2][0:R, :], T["rope"][t * P:t * P + R, :]).then_inc(s_in[t % 2], 16)

        @block.scalar
        def _(act):
            act.wait_ge(s_vm, 1)
            n = 0
            for t, R in tiles():
                for j, (w, cnt) in enumerate(((QL, 1), (KVL, 1), (ROPE, 1), (64, 8), (64, 8), (64, 8), (32, 8), (64, 8))):
                    n += 1
                    act.wait_ge(s_root, n)
                    act.activation(r8[0:R, 1, 0:cnt], r8[0:R, 0, 0:cnt], ACT.Sqrt, scale=1.0 / w,
                                   bias=eps[0:R, 0:1]).then_inc(s_rooted, 1)
                for b in range(8):
                    act.wait_ge(s_tT, 8 * t + b + 1)
                    if t >= 1:
                        act.wait_ge(s_o, 16 * 14 * t)
                    if b < 4:
                        act.activation(tq[0:QK, 4 * b:4 * b + 4, :], pT[(8 * t + b) % 3][0:QK, :].rearrange("p (a q) -> p a q", a=4),
                                       ACT.Copy).then_inc(s_te, 1)
                    else:
                        m = 4 if b < 7 else 1
                        act.activation(td[:, 4 * (b - 4):4 * (b - 4) + m, :], pT[(8 * t + b) % 3][:, 0:m * P].rearrange("p (a q) -> p a q", a=m),
                                       ACT.Copy).then_inc(s_te, 1)

        @block.gpsimd
        def _(pool):
            for t, R in tiles():
                pool.wait_ge(s_in[t % 2], 32 * (t // 2 + 1))
                pool.wait_ge(s_rows, t + 1)
                rs = slice(t * P, t * P + R)
                if t < NT:
                    outs = [T["o2"][0, 0, rs, :], T["o3"][0, 0, rs, :], T["o4"][0, 0, rs].rearrange("r h d -> r (h d)"),
                            T["o5"][0, 0, rs].rearrange("r h d -> r (h d)"), T["o6"][0, 0, rs, :]]
                else:
                    outs = [T["o7"].rearrange("l b s d -> (l b s) d"), T["o8"].rearrange("l b s d -> (l b s) d"),
                            T["o9"].rearrange("l b s h d -> (l b s) (h d)"), T["o10"].rearrange("l b s h d -> (l b s) (h d)"),
                            T["o11"].rearrange("l b s d -> (l b s) d")]
                p_ = pr[t % 2]
                for o, s in zip(outs, (ckv[0:R, :], krr[0:R, :], kd[0:R, :], p_[0:R, C_VD:C_VD + 512], p_[0:R, C_KI:C_KI + IDX])):
                    pool.dma_start(o, s).then_inc(s_o, 16)
                pool.dma_start(T["wi"][rs, :], p_[0:R, C_WI:C_WI + H]).then_inc(s_o, 16)
                pool.dma_start(T["vm"][rs, :], vm[0:R, :]).then_inc(s_o, 16)
                pool.dma_start(T["qm"][rs, :], qm[0:R, :, :].rearrange("p h d -> p (h d)")).then_inc(s_o, 16)
                pool.dma_start(T["qd"][rs, :], qd[0:R, :]).then_inc(s_o, 16)
                pool.dma_start(T["vd"][rs, :], p_[0:R, C_VD:C_VD + 512]).then_inc(s_o, 16)
                pool.wait_ge(s_te, 8 * t + 8)
                cols = slice(t * P, t * P + R)
                pool.dma_start(T["qmT"][:, :, cols].rearrange("h d s -> d h s"), tq[0:QK, 0:8, 0:R]).then_inc(s_o, 16)
                pool.dma_start(T["kmT"][:, :, cols].rearrange("h d s -> d h s"), tq[0:QK, 8:16, 0:R]).then_inc(s_o, 16)
                pool.dma_start(T["tdT"][0:7, :, cols].rearrange("h d s -> d h s"), td[:, 0:7, 0:R]).then_inc(s_o, 16)
                pool.dma_start(T["tdT"][7:13, :, cols].rearrange("h d s -> d h s"), td[:, 7:13, 0:R]).then_inc(s_o, 16)
                pool.wait_ge(s_o, 16 * 14 * (t + 1))
                pool.sem_inc(s_rd, 1)

        @block.tensor
        def _(pe):
            pe.wait_ge(s_w, 160)
            nb = [0]

            def turn(srcs, R):
                n = nb[0]
                if n >= 3:
                    pe.wait_ge(s_te, n - 2)
                for a, s in enumerate(srcs):
                    m = pe.transpose(pT[n % 3][0:s.shape[1], a * P:a * P + R], s, c("ident")[0:R, 0:R])
                m.then_inc(s_tT, 1)
                nb[0] += 1

            for t, R in tiles():
                I = c("ident")[0:R, 0:R]
                pe.wait_ge(s_qT, 4 * t + 1)
                for k in range(2):
                    pe.transpose(pA[:, k * P:k * P + R], ql[0:R, k * P:(k + 1) * P], I)
                pe.wait_ge(s_qT, 4 * t + 2)
                pe.transpose(pA[:, 256:256 + R], ckv[0:R, :], I).then_inc(s_ckT, 1)
                pe.wait_ge(s_qT, 4 * t + 3)
                for n in range(2):
                    for k in range(2):
                        m = pe.matmul(pq[n][0:R, 0:384], qlT[:, k, 0:R], Wq[:, k, 384 * n:384 * n + 384], start=(k == 0), stop=(k == 1))
                pe.matmul(pk[0:R, :], ckvT[:, 0:R], Wkv[:, :, 0:NOPE], start=True, stop=True)
                pe.matmul(pv[0:R, :], ckvT[:, 0:R], Wkv[:, :, NOPE:], start=True, stop=True).then_inc(s_q, 1)
                pe.wait_ge(s_rows, t + 1)
                nb[0] = 8 * t
                p_ = pr[t % 2]
                for b in range(2):
                    turn([qm[0:R, 4 * b + a, :] for a in range(4)], R)
                for b in range(2):
                    turn([km[0:R, 4 * b + a, :] for a in range(4)], R)
                turn([qd[0:R, a * P:(a + 1) * P] for a in range(4)], R)
                turn([kd[0:R, a * P:(a + 1) * P] for a in range(4)], R)
                turn([p_[0:R, C_QI + a * P:C_QI + (a + 1) * P] for a in range(4)], R)
                turn([kir[0:R, :]], R)

        @block.vector
        def _(dve):
            link = serial(dve, s_v)
            dve.memset(eps[:, :], EPS).then_inc(s_vm, 1)
            dve.wait_ge(s_w, 160)
            n = [0]

            def norm(dst, src, cnt, w, gain, R):
                s3 = sq[0:R, 0:cnt * w].rearrange("p (c w) -> p c w", c=cnt)
                link(dve.tensor_tensor(s3, src, src, ALU.mult))
                dve.tensor_reduce(r8[0:R, 0, 0:cnt], s3, AX.X, ALU.add).then_inc(s_root, 1)
                n[0] += 1
                dve.wait_ge(s_rooted, n[0])
                link(dve.reciprocal(r8[0:R, 2, 0:cnt], r8[0:R, 1, 0:cnt]))
                link(dve.tensor_tensor(s3, src, r8[0:R, 2, 0:cnt].unsqueeze(2).to_broadcast([R, cnt, w]), ALU.mult))
                link(dve.tensor_tensor(dst, s3, gain[0:R, :].unsqueeze(1).to_broadcast([R, cnt, w]), ALU.mult))

            def rotate(dst, src, cnt, R, table):
                co = table[0:R, 0:16].unsqueeze(1).to_broadcast([R, cnt, 16])
                si = table[0:R, 16:32].unsqueeze(1).to_broadcast([R, cnt, 16])
                a, b = sq[0:R, 0:cnt * 16].rearrange("p (c w) -> p c w", c=cnt), sq[0:R, 256:256 + cnt * 16].rearrange("p (c w) -> p c w", c=cnt)
                link(dve.tensor_tensor(a, src[:, :, 0:16], co, ALU.mult))
                link(dve.tensor_tensor(b, src[:, :, 16:32], si, ALU.mult))
                link(dve.tensor_tensor(dst[:, :, 0:16], a, b, ALU.subtract))
                link(dve.tensor_tensor(a, src[:, :, 16:32], co, ALU.mult))
                link(dve.tensor_tensor(b, src[:, :, 0:16], si, ALU.mult))
                link(dve.tensor_tensor(dst[:, :, 16:32], a, b, ALU.add))

            for t, R in tiles():
                p_, tb = pr[t % 2], cs[t % 2]
                dve.wait_ge(s_in[t % 2], 32 * (t // 2 + 1))
                if t >= 1:
                    dve.wait_ge(s_rd, 2 * t)
                    dve.wait_ge(s_tT, 8 * t)
                u = lambda ap: ap.unsqueeze(1)
                norm(u(ql[0:R, :]), u(p_[0:R, C_Q:C_Q + QL]), 1, QL, gains["g_q_lora"], R)
                dve.sem_inc(s_qT, 1)
                norm(u(ckv[0:R, :]), u(p_[0:R, C_KV:C_KV + KVL]), 1, KVL, gains["g_kv_lora"], R)
                dve.sem_inc(s_qT, 1)
                dve.wait_ge(s_ckT, t + 1)
                link(dve.tensor_copy(qlT[:, :, 0:R], pA[:, 0:256].rearrange("p (k r) -> p k r", k=2)[:, :, 0:R]))
                link(dve.tensor_copy(ckvT[:, 0:R], pA[:, 256:256 + R]))
                dve.sem_inc(s_qT, 2)
                norm(u(rt[0:R, 0, :]), u(p_[0:R, C_KR:C_KR + ROPE]), 1, ROPE, gains["g_mla_kr"], R)
                rotate(u(krr[0:R, :]), u(rt[0:R, 0, :]), 1, R, tb)
                v3 = lambda ap: ap.rearrange("p (h d) -> p h d", h=H)
                norm(v3(qd[0:R, :]), v3(p_[0:R, C_QD:C_QD + 512]), 8, 64, gains["g_dsa_q"], R)
                norm(v3(kd[0:R, :]), v3(p_[0:R, C_KD:C_KD + 512]), 8, 64, gains["g_dsa_k"], R)
                for a in range(2):
                    link(dve.tensor_copy(kir[0:R, a * IDX:(a + 1) * IDX], p_[0:R, C_KI:C_KI + IDX]))
                dve.wait_ge(s_q, t + 1)
                for a in range(2):
                    link(dve.tensor_copy(qm[0:R, 4 * a:4 * a + 4, :], pq[a][0:R, 0:384].rearrange("p (h d) -> p h d", h=4)))
                link(dve.tensor_copy(vm[0:R, :], pv[0:R, :]))
                link(dve.tensor_copy(km[0:R, :, 0:NOPE], v3(pk[0:R, :])))
                norm(qm[0:R, :, 0:NOPE], qm[0:R, :, 0:NOPE], 8, 64, gains["g_mla_qn"], R)
                norm(rt[0:R, :, :], qm[0:R, :, NOPE:QK], 8, 32, gains["g_mla_qr"], R)
                rotate(qm[0:R, :, NOPE:QK], rt[0:R, :, :], 8, R, tb)
                norm(km[0:R, :, 0:NOPE], km[0:R, :, 0:NOPE], 8, 64, gains["g_mla_kn"], R)
                link(dve.tensor_copy(km[0:R, :, NOPE:QK], u(krr[0:R, :]).to_broadcast([R, H, ROPE])))
                dve.sem_inc(s_rows, 1)
                dve.sem_inc(s_rd, 1)


def stage_prompt(nc, T, G, sem, sb, ps):
    c = G["c"]
    FIRST = TOPK // P
    widths = [(i + 1) * P for i in range(NT)]
    at = [sum(widths[FIRST:i]) for i in range(NT)]
    kiT = sb("kiT", [P, SEQ])
    U = sb("U", [P, sum(widths[FIRST:])])
    bias = sb("bias", [P, H, 2 * P])
    sel_phase = ExitStack()
    with sel_phase as ctx:
        def sb1(name, shape, dt=F32):
            return ctx.enter_context(nc.sbuf_tensor(name, shape, dt))

        def ps1(name):
            return ctx.enter_context(nc.psum_tensor(name, [P, 512], F32))
        index_and_select(nc, T, G, sem, sb1, ps1, kiT, U, bias, FIRST, widths, at)
    with ExitStack() as ctx:
        def sb2(name, shape, dt=F32):
            return ctx.enter_context(nc.sbuf_tensor(name, shape, dt))

        def ps2(name):
            return ctx.enter_context(nc.psum_tensor(name, [P, 512], F32))
        attend(nc, T, G, sem, sb2, ps2, U, bias, FIRST, widths, at)


def index_and_select(nc, T, G, sem, sb, ps, kiT, U, bias, FIRST, widths, at):
    c = G["c"]
    NSEL = NT - FIRST
    qi = [sb(f"qi{i}", [P, 4, P]) for i in range(2)]
    wi = sb("wiall", [P, NSEL, H])
    rl = [sb(f"rl{i}", [P, SEQ]) for i in range(2)]
    junk = sb("sjunk", [P, U.shape[1]], BF16)
    eq, rank = sb("eq", [P, SEQ]), sb("rank", [P, SEQ])
    ones = sb("onesrow", [P, SEQ])
    cand, best = sb("cand", [P, NSEL], I32), sb("best", [P, NSEL], I32)
    cnt, goal, pos, sgn = (sb(n, [P, NSEL]) for n in ("cnt", "goal", "pos", "sgn"))
    ncol, thr, keep = sb("ncol", [P, NSEL]), sb("thr", [P, NSEL]), sb("keep", [P, NSEL], I32)
    rb, rb31 = sb("rb", [NB_REL, H]), sb("rb31", [NB_REL, H])
    pS = [[ps(f"iS{a}{b}") for b in range(2)] for a in range(2)]
    pB = [ps(f"iB{a}") for a in range(4)]
    s_k, s_wi, s_q, s_s, s_r, s_a, s_v, s_b, s_bd = (sem("ix_" + n) for n in ("k", "wi", "q", "s", "relu", "acc", "v", "bias", "biasd"))
    s_bit = sem("ix_bit")
    with nc.Block() as block:
        @block.sync
        def _(sp):
            sp.dma_start(kiT[:, :], T["tdT"][12, :, 0:SEQ]).then_inc(s_k, 16)
            sp.dma_start(wi[:, :, :], T["wi"][FIRST * P:SEQ, :].rearrange("(t p) h -> p t h", p=P)).then_inc(s_wi, 16)
            sp.dma_start(rb[:, :], T["rel_bias"]).then_inc(s_wi, 16)
            sp.dma_start(rb31[:, :], T["rel_bias"][NB_REL - 1:NB_REL, :].to_broadcast([NB_REL, H])).then_inc(s_wi, 16)
            for j in range(NSEL):
                i = FIRST + j
                if j >= 2:
                    sp.wait_ge(s_s, 8 * (j - 1))
                sp.wait_ge(s_q, 16 * j)
                sp.dma_start(qi[j % 2][:, :, :], T["tdT"][8:12, :, i * P:(i + 1) * P].rearrange("h d s -> d h s")).then_inc(s_q, 16)

        @block.tensor
        def _(pe):
            pe.wait_ge(s_k, 16)
            n = 0
            for j in range(NSEL):
                pe.wait_ge(s_q, 16 * (j + 1))
                for h in range(H):
                    b = 64 * (h % 2)
                    if n >= 2:
                        pe.wait_ge(s_r, n - 1)
                    w = widths[FIRST + j]
                    for z in range(0, w, 512):
                        m = pe.matmul(pS[n % 2][z // 512][:, 0:min(512, w - z)], qi[j % 2][b:b + 64, h // 2, :],
                                      kiT[b:b + 64, z:min(z + 512, w)], start=True, stop=True)
                    m.then_inc(s_s, 1)
                    n += 1
            pe.wait_ge(s_bd, 1)
            for k in range(2 * P):
                m = pe.matmul(pB[k // 64][:, (k % 64) * H:(k % 64 + 1) * H], c("rel_onehot")[0:NB_REL, 255 - k:255 - k + P],
                              rb[:, :], start=True, stop=True)
            m.then_inc(s_b, 1)

        @block.scalar
        def _(act):
            n = 0
            for j in range(NSEL):
                for h in range(H):
                    w = widths[FIRST + j]
                    act.wait_ge(s_s, n + 1)
                    if n >= 2:
                        act.wait_ge(s_a, n - 1)
                    for z in range(0, w, 512):
                        a = act.activation(rl[n % 2][:, z:min(z + 512, w)], pS[n % 2][z // 512][:, 0:min(512, w - z)],
                                           ACT.Relu, scale=IDX ** -0.5)
                    a.then_inc(s_r, 1)
                    n += 1

        @block.vector
        def _(dve):
            link = serial(dve, s_v)
            dve.wait_ge(s_wi, 48)
            link(dve.tensor_scalar(wi[:, :, :], wi[:, :, :], H ** -0.5, None, ALU.mult))
            link(dve.tensor_tensor(rb[:, :], rb[:, :], rb31[:, :], ALU.subtract))
            dve.tensor_scalar(rb[:, :], rb[:, :], 1.0 / DSA_SCALE, None, ALU.mult).then_inc(s_bd, 1)
            n = 0
            for j in range(NSEL):
                w = widths[FIRST + j]
                u = U[:, at[FIRST + j]:at[FIRST + j] + w]
                for h in range(H):
                    dve.wait_ge(s_r, n + 1)
                    if n:
                        dve.wait_ge(s_a, n)
                    if h == 0:
                        dve.tensor_scalar(u, rl[n % 2][:, 0:w], wi[:, j, h:h + 1], None, ALU.mult).then_inc(s_a, 1)
                    else:
                        dve.scalar_tensor_tensor(out=u, in0=rl[n % 2][:, 0:w], scalar=wi[:, j, h:h + 1], in1=u,
                                                 op0=ALU.mult, op1=ALU.add).then_inc(s_a, 1)
                    n += 1
            dve.wait_ge(s_a, n)
            tiles_ = [(j, widths[FIRST + j], at[FIRST + j]) for j in range(NSEL)]
            for j, w, a in tiles_:
                link(dve.tensor_tensor(U[:, a + w - P:a + w], U[:, a + w - P:a + w], c("causal"), ALU.add))
                link(dve.memset(ncol[:, j:j + 1], float(w - TOPK + 1)))
            link(dve.memset(best[:, :], 0))
            link(dve.memset(ones[:, :], 1.0))
            for j, w, a in tiles_:
                link(dve.tensor_scalar(junk[:, a:a + w], U[:, a:a + w], 0.0, 0.0, ALU.is_ge, ALU.add, accum_out=cnt[:, j:j + 1]))
            link(dve.tensor_scalar(pos[:, :], cnt[:, :], float(TOPK), None, ALU.is_ge))
            link(dve.tensor_scalar(sgn[:, :], pos[:, :], 2.0, -1.0, ALU.mult, ALU.add))
            link(dve.tensor_scalar(goal[:, :], ncol[:, :], -1.0, float(TOPK), ALU.mult, ALU.add))
            link(dve.tensor_tensor(goal[:, :], goal[:, :], pos[:, :], ALU.mult))
            link(dve.tensor_tensor(goal[:, :], goal[:, :], ncol[:, :], ALU.add))
            for j, w, a in tiles_:
                link(dve.tensor_scalar(U[:, a:a + w], U[:, a:a + w], sgn[:, j:j + 1], None, ALU.mult))
            link(dve.tensor_scalar(goal[:, :], goal[:, :], -1.0, None, ALU.add))
            bits = c("bits").bitcast(I32)
            dve.sem_inc(s_bit, 1)
            per = NSEL + 4
            with dve.Fori(0, 31) as k:
                dve.wait_ge(s_bit, k * per + 1)
                dve.tensor_tensor(cand[:, :], best[:, :], bits[:, bass.ds(k, 1)].to_broadcast([P, NSEL]),
                                  ALU.bitwise_or).then_inc(s_bit, 1)
                dve.wait_ge(s_bit, k * per + 2)
                for j, w, a in tiles_:
                    dve.tensor_scalar(junk[:, a:a + w], U[:, a:a + w], cand[:, j:j + 1].bitcast(F32), 0.0, ALU.is_ge, ALU.add,
                                      accum_out=cnt[:, j:j + 1]).then_inc(s_bit, 1)
                dve.wait_ge(s_bit, k * per + 2 + NSEL)
                dve.tensor_tensor(keep[:, :], goal[:, :], cnt[:, :], ALU.subtract).then_inc(s_bit, 1)
                dve.wait_ge(s_bit, k * per + 3 + NSEL)
                dve.tensor_scalar(keep[:, :], keep[:, :], 31, bits[:, bass.ds(k, 1)], ALU.arith_shift_right,
                                  ALU.bitwise_and).then_inc(s_bit, 1)
                dve.wait_ge(s_bit, k * per + 4 + NSEL)
                dve.tensor_tensor(best[:, :], best[:, :], keep[:, :], ALU.bitwise_or).then_inc(s_bit, 1)
            dve.wait_ge(s_bit, 31 * per + 1)
            link(dve.tensor_tensor(thr[:, :], best[:, :].bitcast(F32), sgn[:, :], ALU.mult))
            for j, w, a in tiles_:
                u = U[:, a:a + w]
                link(dve.tensor_scalar(u, u, sgn[:, j:j + 1], None, ALU.mult))
                link(dve.tensor_scalar(junk[:, a:a + w], u, thr[:, j:j + 1], 0.0, ALU.is_gt, ALU.add, accum_out=cnt[:, j:j + 1]))
                link(dve.tensor_scalar(cnt[:, j:j + 1], cnt[:, j:j + 1], -1.0, float(TOPK), ALU.mult, ALU.add))
                link(dve.tensor_scalar(eq[:, 0:w], u, thr[:, j:j + 1], None, ALU.is_equal))
                link(dve.tensor_tensor_scan(rank[:, 0:w], ones[:, 0:w], eq[:, 0:w], 0.0, ALU.mult, ALU.add))
                link(dve.scalar_tensor_tensor(out=eq[:, 0:w], in0=rank[:, 0:w], scalar=cnt[:, j:j + 1], in1=eq[:, 0:w],
                                              op0=ALU.is_le, op1=ALU.mult))
                link(dve.scalar_tensor_tensor(out=u, in0=u, scalar=thr[:, j:j + 1], in1=eq[:, 0:w], op0=ALU.is_gt, op1=ALU.add))
                link(dve.tensor_scalar(u, u, -NEG, NEG, ALU.mult, ALU.add))
            dve.wait_ge(s_b, 1)
            for g in range(4):
                link(dve.tensor_copy(bias[:, :, 64 * g:64 * g + 64], pB[g][:, :].rearrange("p (k h) -> p h k", h=H)))


def attend(nc, T, G, sem, sb, ps, U, bias, FIRST, widths, at):
    c = G["c"]
    kmT = sb("kmTs", [P, H, SEQ])
    kdT = sb("kdTs", [P, 4, SEQ])
    V = [sb("vmS", [P, NT, 512]), sb("vdS", [P, NT, 512])]
    qm = [sb(f"qmt{i}", [P, H, P]) for i in range(2)]
    qd = [sb(f"qdt{i}", [P, 4, P]) for i in range(2)]
    open_row = sb("open_row", [P, SEQ])
    mb = [sb(f"mb{i}", [P, H, 2 * P]) for i in range(2)]
    S = [sb(f"S{i}", [P, SEQ]) for i in range(2)]
    Pr = [sb(f"Pr{i}", [P, SEQ]) for i in range(2)]
    PT = [sb(f"PT{i}", [P, NT, P]) for i in range(2)]
    O = [sb(f"O{i}", [P, D]) for i in range(2)]
    mx = sb("mx", [P, 2, 4])
    rs = sb("rs", [P, 2])
    mxp = sb("mxp", [P, 2, 4])
    pS = [[ps(f"aS{a}{b}") for b in range(2)] for a in range(2)]
    pT = [ps("aT0"), ps("aT1")]
    pO = [ps("aO0"), ps("aO1")]
    names = ("k", "v", "S", "nm", "P", "T", "evd", "eva", "O", "on", "row", "mb", "st", "mx")
    s_k, s_vv, s_S, s_nm, s_P, s_T, s_evd, s_eva, s_O, s_on, s_row, s_mb, s_st, s_mx = (sem("at_" + n) for n in names)
    s_q, s_out = [sem("at_q0"), sem("at_q1")], [sem("at_o0"), sem("at_o1")]
    items = [(i, g, h) for i in range(NT) for g in range(2) for h in range(H)]
    groups, gfirst = [], []
    for n, (i, g, h) in enumerate(items):
        gfirst.append(len(groups))
        groups += [(n, b, min(4, i + 1 - b)) for b in range(0, i + 1, 4)]
    gfirst.append(len(groups))

    def by_dve(upto):
        return (upto + 1) // 2

    with nc.Block() as block:
        @block.sync
        def _(sp):
            def store(i):
                sp.wait_ge(s_on, 16 * (i + 1))
                sp.dma_start(T["omix"][i * P:(i + 1) * P, :], O[i % 2][:, :]).then_inc(s_out[i % 2], 16)

            for i in range(NT):
                if i >= 2:
                    sp.wait_ge(s_S, 16 * (i - 1))
                sl = slice(i * P, (i + 1) * P)
                sp.dma_start(qm[i % 2][0:QK, :, :], T["qmT"][:, :, sl].rearrange("h d s -> d h s")).then_inc(s_q[i % 2], 16)
                sp.dma_start(qd[i % 2][:, :, :], T["tdT"][0:4, :, sl].rearrange("h d s -> d h s")).then_inc(s_q[i % 2], 16)
                if i == 0:
                    sp.dma_start(kmT[0:QK, :, :], T["kmT"][:, :, 0:SEQ].rearrange("h d s -> d h s")).then_inc(s_k, 16)
                    sp.dma_start(kdT[:, :, :], T["tdT"][4:8, :, 0:SEQ].rearrange("h d s -> d h s")).then_inc(s_k, 16)
                    for g, n in enumerate(("vm", "vd")):
                        sp.dma_start(V[g][:, :, :], T[n][0:SEQ, :].rearrange("(t p) d -> p t d", p=P)).then_inc(s_vv, 16)
                if i >= 2:
                    store(i - 2)
            store(NT - 2)
            store(NT - 1)
            for s in s_out:
                sp.wait_ge(s, 16 * NT // 2)

        @block.gpsimd
        def _(pool):
            pool.memset(open_row[:, 0:SEQ - P], 0.0).then_inc(s_row, 1)
            pool.tensor_copy(open_row[:, SEQ - P:SEQ], c("causal")).then_inc(s_row, 1)
            pool.wait_ge(s_row, 2)
            for i in range(NT):
                if i >= 2:
                    pool.wait_ge(s_nm, 16 * (i - 1))
                w = min(2 * P, widths[i])
                m = U[:, at[i] + widths[i] - w:at[i] + widths[i]] if i >= FIRST else open_row[:, SEQ - w:SEQ]
                pool.tensor_tensor(mb[i % 2][:, :, 2 * P - w:2 * P], bias[:, :, 2 * P - w:2 * P],
                                   m.unsqueeze(1).to_broadcast([P, H, w]), ALU.add).then_inc(s_mb, 1)

        @block.tensor
        def _(pe):
            def scores(n):
                i, g, h = items[n]
                if n == 0:
                    pe.wait_ge(s_k, 32)
                if g == 0 and h == 0:
                    pe.wait_ge(s_q[i % 2], 32 * (i // 2 + 1))
                if n >= 2:
                    pe.wait_ge(s_nm, n - 1)
                w = widths[i]
                b = 64 * (h % 2)
                q = qm[i % 2][0:QK, h, :] if g == 0 else qd[i % 2][b:b + 64, h // 2, :]
                for z in range(0, w, 512):
                    e = min(z + 512, w)
                    k = kmT[0:QK, h, z:e] if g == 0 else kdT[b:b + 64, h // 2, z:e]
                    m = pe.matmul(pS[n % 2][z // 512][:, 0:e - z], q, k, start=True, stop=True)
                m.then_inc(s_S, 1)

            def turn(n):
                pe.wait_ge(s_P, n + 1)
                for gi in range(gfirst[n], gfirst[n + 1]):
                    _, b0, cnt = groups[gi]
                    if gi >= 2:
                        pe.wait_ge(s_evd if gi % 2 == 0 else s_eva, gi // 2)
                    for b in range(cnt):
                        m = pe.transpose(pT[gi % 2][:, b * P:(b + 1) * P], Pr[n % 2][:, (b0 + b) * P:(b0 + b + 1) * P], c("ident"))
                    m.then_inc(s_T, 1)

            def pv(n):
                i, g, h = items[n]
                if n == 0:
                    pe.wait_ge(s_vv, 32)
                pe.wait_ge(s_evd, by_dve(gfirst[n + 1]))
                if gfirst[n + 1] >= 2:
                    pe.wait_ge(s_eva, gfirst[n + 1] // 2)
                if n >= 2:
                    pe.wait_ge(s_on, n - 1)
                for j in range(i + 1):
                    m = pe.matmul(pO[n % 2][:, 0:64], PT[n % 2][:, j, :], V[g][:, j, h * 64:h * 64 + 64], start=(j == 0), stop=(j == i))
                m.then_inc(s_O, 1)

            scores(0)
            for n in range(len(items)):
                if n + 1 < len(items):
                    scores(n + 1)
                turn(n)
                if n:
                    pv(n - 1)
            pv(len(items) - 1)

        def evac(eng, n, odd):
            for gi in range(gfirst[n], gfirst[n + 1]):
                if gi % 2 == odd:
                    _, b0, cnt = groups[gi]
                    eng.wait_ge(s_T, gi + 1)
                    if n >= 2:
                        eng.wait_ge(s_O, n - 1)
                    dst = PT[n % 2][:, b0:b0 + cnt, :].rearrange("p a q -> p (a q)")
                    if odd:
                        eng.activation(dst, pT[1][:, 0:cnt * P], ACT.Copy).then_inc(s_eva, 1)
                    else:
                        eng.tensor_copy(dst, pT[0][:, 0:cnt * P]).then_inc(s_evd, 1)

        @block.scalar
        def _(act):
            def exps(n):
                w = widths[items[n][0]]
                act.wait_ge(s_nm, n + 1)
                if n >= 2:
                    act.wait_ge(s_T, gfirst[n - 1])
                    act.wait_ge(s_on, n - 1)
                act.activation(Pr[n % 2][:, 0:w], S[n % 2][:, 0:w], ACT.Exp, bias=mx[:, n % 2, 2:3],
                               accum_out=mx[:, n % 2, 3:4]).then_inc(s_P, 1)
            exps(0)
            for n in range(len(items)):
                if n + 1 < len(items):
                    exps(n + 1)
                evac(act, n, 1)

        @block.vector
        def _(dve):
            dve.wait_ge(s_row, 2)
            nmx = [0]

            def scale_and_max(n):
                i, g, h = items[n]
                w, k = widths[i], n % 2
                dve.wait_ge(s_S, n + 1)
                if n >= 2:
                    dve.wait_ge(s_P, n - 1)
                near = min(w, 2 * P) if g else 0
                parts = []
                cuts = sorted({0, w} | {x for x in (512, w - near) if 0 < x < w})
                parts = list(zip(cuts, cuts[1:]))
                for a, (z, e) in enumerate(parts):
                    if g == 0:
                        m = open_row[:, SEQ - w + z:SEQ - w + e]
                    elif z >= w - near:
                        dve.wait_ge(s_mb, i + 1)
                        m = mb[i % 2][:, h, 2 * P - w + z:2 * P - w + e]
                    else:
                        m = U[:, at[i] + z:at[i] + e]
                    zb = z // 512
                    dve.tensor_tensor_reduce(out=S[k][:, z:e], in0=pS[k][zb][:, z - 512 * zb:e - 512 * zb], in1=m,
                                             scale=MLA_SCALE if g == 0 else DSA_SCALE, scalar=NEG, op0=ALU.add, op1=ALU.max,
                                             accum_out=mxp[:, k, a:a + 1]).then_inc(s_mx, 1)
                    nmx[0] += 1
                dve.wait_ge(s_mx, nmx[0])
                dve.tensor_reduce(mx[:, k, 2:3], mxp[:, k, 0:len(parts)], AX.X, ALU.max, negate=True).then_inc(s_nm, 1)

            def norm(n):
                i, g, h = items[n]
                dve.wait_ge(s_O, n + 1)
                dve.reciprocal(rs[:, n % 2:n % 2 + 1], mx[:, n % 2, 3:4]).then_inc(s_st, 1)
                dve.wait_ge(s_st, n + 1)
                if g == 0 and h == 0 and i >= 2:
                    dve.wait_ge(s_out[i % 2], 16 * (i // 2))
                dve.tensor_scalar(O[i % 2][:, g * 512 + h * 64:g * 512 + h * 64 + 64], pO[n % 2][:, 0:64], rs[:, n % 2:n % 2 + 1],
                                  None, ALU.mult).then_inc(s_on, 1)

            scale_and_max(0)
            for n in range(len(items)):
                if n + 1 < len(items):
                    scale_and_max(n + 1)
                evac(dve, n, 0)
                if n:
                    norm(n - 1)
            norm(len(items) - 1)


def scoped(nc):
    ctx = ExitStack()

    def sb(name, shape, dt=F32):
        return ctx.enter_context(nc.sbuf_tensor(name, shape, dt))

    def ps(name):
        return ctx.enter_context(nc.psum_tensor(name, [P, 512], F32))
    return ctx, sb, ps


def stage_sample(nc, T, G, sem, sb, ps):
    pages = sb("pages", [P, NS // 2], I32)
    pagef = sb("pagef", [P, NS // 2])
    SD = sb("SD", [P, NS // 2, PAGE + 1])
    ctx, sb1, ps1 = scoped(nc)
    with ctx:
        sample_index(nc, T, G, sem, sb1, ps1, pages, pagef, SD)
    ctx, sb1, ps1 = scoped(nc)
    with ctx:
        sample_mla(nc, T, G, sem, sb1, ps1, pagef)
    gpos, grow = sb("gpos", [P, 16]), sb("grow", [P, 16], I32)
    ctx, sb1, ps1 = scoped(nc)
    with ctx:
        sample_select(nc, T, G, sem, sb1, ps1, pagef, SD, gpos, grow)
    ctx, sb1, ps1 = scoped(nc)
    with ctx:
        sample_dsa(nc, T, G, sem, sb1, ps1, gpos, grow)


def sample_index(nc, T, G, sem, sb, ps, pages, pagef, SD):
    c = G["c"]
    NP2 = NS // 2
    KI = [sb(f"KI{i}", [P, PAGE + 1, IDX]) for i in range(2)]
    qr = sb("dqr", [NS, H, 2, IDX])
    QB = sb("QB", [P, NS, 2, H])
    KT = [sb(f"KT{i}", [P, 512]) for i in range(2)]
    WB = sb("WB", [P, NP2, H])
    RL = [sb(f"RL{i}", [P, 32, H]) for i in range(2)]
    pT, pS, pq = [ps("dT0"), ps("dT1")], [ps("dS0"), ps("dS1")], ps("dq0")
    s_pg, s_q, s_w, s_pi, s_z, s_qt, s_qb, s_T, s_evd, s_eva, s_u, s_S, s_R, s_v, s_a = (
        sem("di_" + n) for n in ("pg", "q", "w", "pi", "z", "qt", "qb", "T", "evd", "eva", "use", "S", "R", "v", "add"))
    s_k = [sem("di_k0"), sem("di_k1")]
    s_f = [sem("di_f0"), sem("di_f1")]
    idx_pages = T["cache_idx_k"][0].rearrange("n s d -> n (s d)")
    fresh = T["o11"].rearrange("l b s d -> (l b s) d")
    uses = [(pr, k) for pr in range(NP2) for k in range(17)]
    nb = lambda u: (u // 17) * 5 + (u % 17) // 4
    with nc.Block() as block:
        @block.sync
        def _(sp):
            sp.dma_start(pages[:, :], T["page_table"].rearrange("(a b) p -> (b p) a", b=2), allow_slow_non_contiguous=True).then_inc(s_pg, 16)
            qi = T["p"][SEQ:NTOK, C_QI:C_QI + 512].rearrange("b (h d) -> b h d", h=H)
            for a in range(2):
                sp.dma_start(qr[:, :, a, :], qi).then_inc(s_q, 16)
            for b in range(NS):
                sp.dma_start(WB[64 * (b % 2):64 * (b % 2) + 64, b // 2, :],
                             T["wi"][SEQ + b:SEQ + b + 1, :].to_broadcast([64, H])).then_inc(s_w, 16)
            sp.wait_ge(s_z, 1)
            for pr in range(NP2):
                if pr >= 2:
                    sp.wait_ge(s_T, 17 * (pr - 1))
                for a in range(2):
                    sp.dma_start(KI[pr % 2][64 * a + 63:64 * a + 64, PAGE, :], fresh[2 * pr + a:2 * pr + a + 1, :]).then_inc(s_f[pr % 2], 16)

        @block.gpsimd
        def _(pool):
            pool.memset(KI[0][:, PAGE, :], 0.0).then_inc(s_pi, 1)
            pool.memset(KI[1][:, PAGE, :], 0.0).then_inc(s_pi, 1)
            pool.wait_ge(s_pi, 2)
            pool.sem_inc(s_z, 1)
            pool.wait_ge(s_pg, 16)
            for pr in range(NP2):
                if pr >= 2:
                    pool.wait_ge(s_T, 17 * (pr - 1))
                pool.indirect_dma_start(out=KI[pr % 2][:, 0:PAGE, :].rearrange("p s d -> p (s d)"), out_offset=None, in_=idx_pages,
                                        in_offset=bass.IndirectOffsetOnAxis(ap=pages[:, pr:pr + 1], axis=0)).then_inc(s_k[pr % 2], 16)

        @block.tensor
        def _(pe):
            pe.wait_ge(s_q, 32)
            for h in range(H):
                m = pe.transpose(pq[:, h * NS:(h + 1) * NS], qr[:, h, :, :].rearrange("b a d -> b (a d)"), c("ident")[0:NS, 0:NS])
            m.then_inc(s_qt, 1)

            def turn(u):
                pr, k = uses[u]
                if k == 0:
                    pe.wait_ge(s_k[pr % 2], 16 * (pr // 2 + 1))
                    pe.wait_ge(s_f[pr % 2], 32 * (pr // 2 + 1))
                if u >= 2:
                    pe.wait_ge(s_eva if u % 2 else s_evd, u // 2)
                for a in range(4 if k < 16 else 1):
                    s = 8 * k + 2 * a
                    src = KI[pr % 2][:, s:min(s + 2, PAGE + 1), :].rearrange("p s d -> p (s d)")
                    m = pe.transpose(pT[u % 2][0:src.shape[1], a * P:(a + 1) * P], src, c("ident"))
                m.then_inc(s_T, 1)

            def product(u):
                pr, k = uses[u]
                pe.wait_ge(s_eva if u % 2 else s_evd, u // 2 + 1)
                b = nb(u)
                if k % 4 == 0 and b >= 2:
                    pe.wait_ge(s_R, 2 * (b - 1))
                if k < 16:
                    for a in range(4):
                        o = ((k % 4) * 4 + a) * 32
                        m = pe.matmul(pS[b % 2][:, o:o + 32], KT[u % 2][:, a * P:(a + 1) * P], QB[:, 2 * pr:2 * pr + 2, :, :],
                                      start=True, stop=True)
                else:
                    m = pe.matmul(pS[b % 2][:, 0:32], KT[u % 2][0:64, 0:P], QB[0:64, 2 * pr:2 * pr + 2, :, :], start=True, stop=True)
                m.then_inc(s_S, 1)

            turn(0)
            pe.wait_ge(s_qb, 1)
            for u in range(len(uses)):
                if u + 1 < len(uses):
                    turn(u + 1)
                product(u)

        def evac(eng, u):
            if u < len(uses):
                eng.wait_ge(s_T, u + 1)
                if u >= 2:
                    eng.wait_ge(s_S, u - 1)
                r = P if uses[u][1] < 16 else 64
                w = 512 if uses[u][1] < 16 else P
                if u % 2:
                    eng.activation(KT[1][0:r, 0:w], pT[1][0:r, 0:w], ACT.Copy).then_inc(s_eva, 1)
                else:
                    eng.tensor_copy(KT[0][0:r, 0:w], pT[0][0:r, 0:w]).then_inc(s_evd, 1)

        @block.scalar
        def _(act):
            for u, (pr, k) in enumerate(uses):
                if u % 2 == 0:
                    evac(act, u + 1)
                if k % 4 == 3 or k == 16:
                    b = nb(u)
                    act.wait_ge(s_S, u + 1)
                    if b >= 2:
                        act.wait_ge(s_a, b - 1)
                    n = 16 if k < 16 else 1
                    for half in range(2):
                        src = pS[b % 2][64 * half:64 * half + 64, 0:n * 32].rearrange("p (n q s h) -> p n q s h", q=2, s=2, h=H)
                        src = src[:, :, half, :, :] if k < 16 else src[:, :, half, 0:1, :]
                        m = 2 * n if k < 16 else 1
                        dst = RL[b % 2][64 * half:64 * half + 64, 0:m, :].rearrange("p (n s) h -> p n s h", n=n)
                        act.activation(dst, src, ACT.Relu, scale=IDX ** -0.5).then_inc(s_R, 1)

        @block.vector
        def _(dve):
            link = serial(dve, s_v)
            link(dve.memset(QB[:, :, :, :], 0.0))
            dve.wait_ge(s_pg, 16)
            link(dve.tensor_copy(pagef[:, :], pages[:, :]))
            dve.wait_ge(s_w, 16 * NS)
            link(dve.tensor_scalar(WB[:, :, :], WB[:, :, :], H ** -0.5, None, ALU.mult))
            dve.wait_ge(s_qt, 1)
            for a in range(2):
                link(dve.tensor_copy(QB[64 * a:64 * a + 64, :, a, :], pq[64 * a:64 * a + 64, 0:64].rearrange("p (h b) -> p b h", h=H)))
            dve.sem_inc(s_qb, 1)
            evac(dve, 0)
            for u, (pr, k) in enumerate(uses):
                if u % 2:
                    evac(dve, u + 1)
                if k % 4 == 3 or k == 16:
                    b = nb(u)
                    dve.wait_ge(s_R, 2 * (b + 1))
                    m = 32 if k < 16 else 1
                    r = RL[b % 2][:, 0:m, :]
                    link(dve.tensor_tensor(r, r, WB[:, pr, :].unsqueeze(1).to_broadcast([P, m, H]), ALU.mult))
                    s0 = 32 * (k // 4) if k < 16 else PAGE
                    dve.tensor_reduce(SD[:, pr, s0:s0 + m], r, AX.X, ALU.add).then_inc(s_a, 1)
            dve.wait_ge(s_a, 5 * NP2)
            link(dve.tensor_tensor(SD[:, :, PAGE], SD[:, :, PAGE], c("fresh_neg").to_broadcast([P, NP2]), ALU.add))


def sample_mla(nc, T, G, sem, sb, ps, pagef):
    c = G["c"]
    NP2, NSL = NS // 2, PAGE + 1
    Wkv = sb("dWkv", [P, H, NOPE + VD])
    L = sb("L", [P, NSL, KVL])
    KR = sb("KR", [P, NSL, ROPE])
    LT = [sb(f"LT{i}", [P, 512]) for i in range(3)]
    SQ = [sb(f"SQ{i}", [P, 512]) for i in range(2)]
    ssq, num, rop = sb("ssq", [P, NSL, H]), sb("num", [P, NSL, H]), sb("rop", [P, NSL, H])
    P16 = sb("P16", [P, NSL, 16])
    qs = sb("qs", [NS, H, QK])
    gkn = sb("gkn", [NS, NOPE])
    qr4 = sb("qr4", [NS, H, 4, ROPE])
    QG = sb("QG", [64, H, NS])
    WT = sb("WT", [64, H, P])
    QT = sb("QT", [P, NS, H])
    QR = sb("QR", [P, NP2, 4, 2, H])
    idx = sb("latidx", [P, NP2, 8], I32)
    idxf = sb("latidxf", [P, NP2, 8])
    kidx = sb("kidx", [P, NP2], I32)
    m8, m16, d16, o16 = sb("m8", [P, H]), sb("m16", [P, 2, H]), sb("d16", [P, 16]), sb("o16", [P, 16])
    M16, sums = sb("M16", [P, 2, H]), sb("sums", [P, 2, H])
    tmp = sb("dtmp", [16, 512])
    orow = sb("orow", [NS, 512])
    epst = sb("deps", [P, 1])
    pT, pK, pN, pO, pR = [ps("eT0"), ps("eT1")], [ps("eK0"), ps("eK1")], [ps("eN0"), ps("eN1")], ps("eO"), ps("eR")
    names = ("in", "idx", "v", "pp", "qt", "T", "evd", "eva", "use", "KN", "sq", "red", "NR", "nrc", "z", "f", "zi",
             "S", "rt", "mx", "am", "M", "ex", "pv", "on", "o2", "tm", "out", "den", "g", "rr")
    (s_in, s_idx, s_v, s_pp, s_qt, s_T, s_evd, s_eva, s_use, s_KN, s_sq, s_red, s_NR, s_nrc, s_z, s_f, s_zi,
     s_S, s_rt, s_mx, s_am, s_M, s_ex, s_pv, s_on, s_o2, s_tm, s_out, s_den, s_g, s_rr) = (sem("dm_" + n) for n in names)
    s_l = [sem(f"dm_l{j}") for j in range(8)]
    s_kr = sem("dm_kr")
    lat_rows = T["cache_mla_latent"][0].rearrange("n (j s) c -> (n j) (s c)", j=8)
    kr_rows = T["cache_mla_krope"][0].rearrange("n s c -> n (s c)")
    uses, chunk_end, kn0 = [], {}, []
    nk = 0
    for pr in range(NP2):
        for ch in range(9):
            uses.append((pr, ch, -1, 4 if ch < 8 else 1))
            kn0.append(nk)
            for k in range(4 if ch < 8 else 1):
                uses.append((pr, ch, k, 4 if ch < 8 else 1))
                kn0.append(nk)
                nk += uses[-1][3]
            chunk_end[len(uses) - 1] = pr * 9 + ch
    last_use = [max(u for u in range(len(uses)) if uses[u][0] == pr) for pr in range(NP2)]

    with nc.Block() as block:
        @block.sync
        def _(sp):
            sp.dma_start(Wkv[:, :, :], T["w_kv_up"][0].rearrange("p (h n) -> p h n", h=H)).then_inc(s_in, 16)
            qsrc = T["qm"][SEQ:NTOK, :].rearrange("b (h d) -> b h d", h=H)
            sp.dma_start(qs[:, :, :], qsrc).then_inc(s_in, 16)
            sp.dma_start(gkn[:, :], T["g_mla_kn"].to_broadcast([NS, NOPE])).then_inc(s_in, 16)
            for a in range(4):
                sp.dma_start(qr4[:, :, a, :], qsrc[:, :, NOPE:QK]).then_inc(s_in, 16)
            sp.wait_ge(s_z, 1)
            lat = T["o7"].rearrange("l b s d -> (l b s) d")
            krf = T["o8"].rearrange("l b s d -> (l b s) d")
            for pr in range(NP2):
                if pr:
                    sp.wait_ge(s_pv, pr)
                for a in range(2):
                    sp.dma_start(L[64 * a + 63:64 * a + 64, PAGE, :], lat[2 * pr + a:2 * pr + a + 1, :]).then_inc(s_f, 16)
                    sp.dma_start(KR[64 * a + 63:64 * a + 64, PAGE, :], krf[2 * pr + a:2 * pr + a + 1, :]).then_inc(s_f, 16)
            sp.wait_ge(s_out, 1)
            sp.dma_start(T["omix"][SEQ:NTOK, 0:512], orow[:, :]).then_inc(s_g, 16)
            sp.wait_ge(s_g, 16)

        @block.gpsimd
        def _(pool):
            pool.memset(L[:, PAGE, :], 0.0).then_inc(s_zi, 1)
            pool.memset(KR[:, PAGE, :], 0.0).then_inc(s_zi, 1)
            pool.memset(P16[:, :, :], 0.0).then_inc(s_zi, 1)
            pool.wait_ge(s_zi, 3)
            pool.sem_inc(s_z, 1)
            pool.wait_ge(s_idx, 1)
            for pr in range(NP2):
                if pr:
                    pool.wait_ge(s_pv, pr)
                pool.indirect_dma_start(out=KR[:, 0:PAGE, :].rearrange("p s d -> p (s d)"), out_offset=None, in_=kr_rows,
                                        in_offset=bass.IndirectOffsetOnAxis(ap=kidx[:, pr:pr + 1], axis=0)).then_inc(s_kr, 16)
                for j in range(8):
                    pool.indirect_dma_start(out=L[:, 16 * j:16 * j + 16, :].rearrange("p s d -> p (s d)"), out_offset=None, in_=lat_rows,
                                            in_offset=bass.IndirectOffsetOnAxis(ap=idx[:, pr, j:j + 1], axis=0)).then_inc(s_l[j], 16)
                pool.wait_ge(s_am, pr + 1)
                pool.partition_all_reduce(M16[:, :, :].rearrange("p a h -> p (a h)"), m16[:, :, :].rearrange("p a h -> p (a h)"),
                                          P, RMAX).then_inc(s_M, 1)

        @block.tensor
        def _(pe):
            I8 = c("ident")[0:NS, 0:NS]
            pe.wait_ge(s_qt, 1)
            pe.wait_ge(s_in, 112)
            for h in range(H):
                pe.transpose(pT[0][0:64, h * NS:(h + 1) * NS], qs[:, h, 0:NOPE], I8)
                pe.transpose(pT[1][:, h * NS:(h + 1) * NS], qr4[:, h, :, :].rearrange("b a r -> b (a r)"), I8)
            for h in range(4):
                pe.transpose(pK[0][0:64, h * P:(h + 1) * P], Wkv[:, h, 0:NOPE], c("ident"))
                m = pe.transpose(pK[1][0:64, h * P:(h + 1) * P], Wkv[:, 4 + h, 0:NOPE], c("ident"))
            m.then_inc(s_pp, 1)
            pe.wait_ge(s_qt, 2)
            for h in range(H):
                m = pe.matmul(pN[0][:, h * NS:(h + 1) * NS], WT[:, h, :], QG[:, h, :], start=True, stop=True)
            m.then_inc(s_pp, 1)
            pe.wait_ge(s_qt, 3)

            def turn(u):
                if u >= len(uses):
                    return
                pr, ch, k, cnt = uses[u]
                if k < 0 and ch == 0:
                    pe.wait_ge(s_kr, 16 * (pr + 1))
                    pe.wait_ge(s_f, 64 * (pr + 1))
                if k == 0 and ch < 8:
                    pe.wait_ge(s_l[ch], 16 * (pr + 1))
                if u >= 2:
                    pe.wait_ge(s_eva if u % 2 else s_evd, u // 2)
                for a in range(cnt):
                    if k < 0:
                        src = KR[:, 16 * ch + 4 * a:min(16 * ch + 4 * a + 4, NSL), :].rearrange("p s r -> p (s r)")
                    else:
                        src = L[:, 16 * ch + 4 * k + a, :]
                    m = pe.transpose(pT[u % 2][0:src.shape[1], a * P:(a + 1) * P], src, c("ident"))
                m.then_inc(s_T, 1)

            def products(u):
                pr, ch, k, cnt = uses[u]
                pe.wait_ge(s_eva if u % 2 else s_evd, u // 2 + 1)
                cg = pr * 9 + ch
                N = pN[cg % 2][:, :].rearrange("p (s w) -> p s w", w=32)
                if k < 0:
                    if cg >= 2:
                        pe.wait_ge(s_nrc, cg - 1)
                    for a in range(cnt):
                        if ch < 8:
                            m = pe.matmul(N[:, 4 * a:4 * a + 4, 16:32], LT[u % 3][:, a * P:(a + 1) * P],
                                          QR[:, pr, :, :, :].rearrange("p s q h -> p (s q h)"), start=True, stop=True)
                        else:
                            m = pe.matmul(N[:, 0, 16:32], LT[u % 3][0:ROPE, 0:P],
                                          QR[0:ROPE, pr, 0, :, :].rearrange("p q h -> p (q h)"), start=True, stop=True)
                else:
                    for a in range(cnt):
                        kn = kn0[u] + a
                        if kn >= 2:
                            pe.wait_ge(s_sq, kn - 1)
                        m = pe.matmul(N[:, 4 * k + a, 0:16], LT[u % 3][:, a * P:(a + 1) * P],
                                      QT[:, 2 * pr:2 * pr + 2, :].rearrange("p b h -> p (b h)"), start=True, stop=True)
                        pe.matmul(pK[kn % 2][:, :], LT[u % 3][:, a * P:(a + 1) * P], Wkv[:, :, 0:NOPE],
                                  start=True, stop=True).then_inc(s_KN, 1)
                        m = None
                if k < 0:
                    m.then_inc(s_rr, 1)

            for u in range(len(uses)):
                if u == 0:
                    turn(0)
                pr = uses[u][0]
                if u not in last_use:
                    turn(u + 1)
                products(u)
                if u in last_use:
                    pe.wait_ge(s_ex, 2 * (pr + 1))
                    for s in range(NSL):
                        m = pe.matmul(pO[:, 0:16], L[:, s, :], P16[:, s, :], start=(s == 0), stop=(s == NSL - 1))
                    m.then_inc(s_pv, 1)
                    pe.wait_ge(s_mx, 3 * pr + 3)
                    pe.matmul(pO[:, 16:32], c("ones"), sums[:, :, :].rearrange("p a h -> p (a h)"), start=True, stop=True).then_inc(s_den, 1)
                    pe.wait_ge(s_on, pr + 1)
                    pe.matmul(pO[0:16, :], o16[:, :], Wkv[:, :, NOPE:], start=True, stop=True).then_inc(s_o2, 1)
                    pe.wait_ge(s_tm, pr + 1)
                    pe.matmul(pR[0:NS, :], c("to_pair")[0:16, pr * NS:(pr + 1) * NS], tmp[:, :], start=(pr == 0), stop=(pr == NP2 - 1)).then_inc(s_rt, 1)
                    turn(u + 1)

        def evac(eng, u):
            if u >= len(uses):
                return
            pr, ch, k, cnt = uses[u]
            eng.wait_ge(s_T, u + 1)
            if u >= 3:
                v = u - 3
                if uses[v][2] < 0:
                    eng.wait_ge(s_rr, sum(1 for x in uses[:v + 1] if x[2] < 0))
                else:
                    eng.wait_ge(s_KN, kn0[v] + uses[v][3])
            r = ROPE if (k < 0 and ch == 8) else P
            if u % 2:
                eng.activation(LT[u % 3][0:r, 0:cnt * P], pT[1][0:r, 0:cnt * P], ACT.Copy).then_inc(s_eva, 1)
            else:
                eng.tensor_copy(LT[u % 3][0:r, 0:cnt * P], pT[0][0:r, 0:cnt * P]).then_inc(s_evd, 1)

        @block.scalar
        def _(act):
            act.wait_ge(s_qt, 3)
            for u, (pr, ch, k, cnt) in enumerate(uses):
                if u % 2 == 0 and u not in last_use:
                    evac(act, u + 1)
                if k >= 0:
                    for a in range(cnt):
                        kn = kn0[u] + a
                        act.wait_ge(s_KN, kn + 1)
                        if kn >= 2:
                            act.wait_ge(s_red, kn - 1)
                        act.activation(SQ[kn % 2][:, :], pK[kn % 2][:, :], ACT.Square).then_inc(s_sq, 1)
                if u in last_use:
                    act.wait_ge(s_red, kn0[u] + cnt)
                    act.activation(ssq[:, :, :], ssq[:, :, :], ACT.Sqrt, scale=1.0 / NOPE, bias=epst[:, 0:1]).then_inc(s_S, 1)
                    act.wait_ge(s_mx, 3 * pr + 2)
                    for a in range(2):
                        r = slice(64 * a, 64 * a + 64)
                        act.activation(P16[r, :, 8 * a:8 * a + 8], num[r, :, :], ACT.Exp).then_inc(s_ex, 1)
                    if u % 2 == 0:
                        evac(act, u + 1)

        @block.vector
        def _(dve):
            link = serial(dve, s_v)
            dve.wait_ge(s_in, 112)
            link(dve.memset(epst[:, :], EPS))
            link(dve.memset(sums[:, :, :], 0.0))
            link(dve.tensor_scalar(idxf[:, :, :], pagef[:, :].unsqueeze(2).to_broadcast([P, NP2, 8]), 8.0, None, ALU.mult))
            link(dve.tensor_tensor(idx[:, :, :], idxf[:, :, :], c("iota")[:, 0:8].unsqueeze(1).to_broadcast([P, NP2, 8]), ALU.add))
            link(dve.tensor_copy(kidx[:, :], pagef[:, :]))
            dve.sem_inc(s_idx, 1)
            link(dve.tensor_tensor(qs[:, :, 0:NOPE], qs[:, :, 0:NOPE], gkn[:, :].unsqueeze(1).to_broadcast([NS, H, NOPE]), ALU.mult))
            dve.sem_inc(s_qt, 1)
            link(dve.memset(QR[:, :, :, :, :], 0.0))
            dve.wait_ge(s_pp, 1)
            link(dve.tensor_copy(QG[:, :, :], pT[0][0:64, 0:64].rearrange("p (h b) -> p h b", h=H)))
            for a in range(4):
                r = slice(32 * a, 32 * a + 32)
                link(dve.tensor_copy(QR[r, :, a, :, :], pT[1][r, 0:64].rearrange("p (h n q) -> p n q h", h=H, q=2)))
            for a in range(2):
                link(dve.tensor_copy(WT[:, 4 * a:4 * a + 4, :], pK[a][0:64, :].rearrange("p (h c) -> p h c", h=4)))
            dve.sem_inc(s_qt, 1)
            dve.wait_ge(s_pp, 2)
            link(dve.tensor_copy(QT[:, :, :], pN[0][:, 0:64].rearrange("p (h b) -> p b h", h=H)))
            dve.sem_inc(s_qt, 1)
            evac(dve, 0)
            for u, (pr, ch, k, cnt) in enumerate(uses):
                if u % 2 == 1 and u not in last_use:
                    evac(dve, u + 1)
                if k >= 0:
                    for a in range(cnt):
                        kn = kn0[u] + a
                        dve.wait_ge(s_sq, kn + 1)
                        dve.tensor_reduce(ssq[:, 16 * ch + 4 * k + a, :], SQ[kn % 2][:, :].rearrange("p (h d) -> p h d", h=H),
                                          AX.X, ALU.add).then_inc(s_red, 1)
                if u in chunk_end:
                    cg = chunk_end[u]
                    n = 16 if ch < 8 else 1
                    dve.wait_ge(s_KN, kn0[u] + cnt)
                    dve.wait_ge(s_rr, cg + 1)
                    N = pN[cg % 2][:, :].rearrange("p (s w) -> p s w", w=32)
                    for a in range(2):
                        r = slice(64 * a, 64 * a + 64)
                        link(dve.tensor_copy(num[r, 16 * ch:16 * ch + n, :], N[r, 0:n, 8 * a:8 * a + 8]))
                        link(dve.tensor_copy(rop[r, 16 * ch:16 * ch + n, :], N[r, 0:n, 16 + 8 * a:24 + 8 * a]))
                    dve.sem_inc(s_nrc, 1)
                if u in last_use:
                    dve.wait_ge(s_S, pr + 1)
                    link(dve.reciprocal(ssq[:, :, :], ssq[:, :, :]))
                    link(dve.tensor_tensor(num[:, :, :], num[:, :, :], ssq[:, :, :], ALU.mult))
                    link(dve.tensor_tensor(num[:, :, :], num[:, :, :], rop[:, :, :], ALU.add))
                    link(dve.tensor_scalar(num[:, :, :], num[:, :, :], MLA_SCALE, None, ALU.mult))
                    link(dve.tensor_scalar(num[:, PAGE, :], num[:, PAGE, :], c("fresh_neg"), None, ALU.add))
                    dve.tensor_reduce(m8[:, :], num[:, :, :].rearrange("p s h -> p h s"), AX.X, ALU.max).then_inc(s_mx, 1)
                    dve.wait_ge(s_mx, 3 * pr + 1)
                    for a in range(2):
                        link(dve.tensor_scalar(m16[:, a, :], m8[:, :], c("half_neg")[:, a:a + 1], None, ALU.add))
                    dve.sem_inc(s_am, 1)
                    dve.wait_ge(s_M, pr + 1)
                    for a in range(2):
                        r = slice(64 * a, 64 * a + 64)
                        m = dve.tensor_tensor(num[r, :, :], num[r, :, :], M16[r, a, :].unsqueeze(1).to_broadcast([64, NSL, H]), ALU.subtract)
                        if a == 0:
                            link(m)
                        else:
                            m.then_inc(s_mx, 1)
                    dve.wait_ge(s_ex, 2 * (pr + 1))
                    for a in range(2):
                        r = slice(64 * a, 64 * a + 64)
                        link(dve.tensor_reduce(sums[r, a, :], P16[r, :, 8 * a:8 * a + 8].rearrange("p s h -> p h s"), AX.X, ALU.add))
                    dve.sem_inc(s_mx, 1)
                    dve.wait_ge(s_den, pr + 1)
                    link(dve.reciprocal(d16[:, :], pO[:, 16:32]))
                    dve.tensor_tensor(o16[:, :], pO[:, 0:16], d16[:, :], ALU.mult).then_inc(s_on, 1)
                    dve.wait_ge(s_o2, pr + 1)
                    dve.tensor_tensor(tmp[:, :], pO[0:16, :], c("own_head")[0:16, :], ALU.mult).then_inc(s_tm, 1)
                    dve.wait_ge(s_rt, pr + 1)
                    if pr == NP2 - 1:
                        dve.tensor_copy(orow[:, :], pR[0:NS, :]).then_inc(s_out, 1)
                    if u % 2 == 1:
                        evac(dve, u + 1)


def sample_select(nc, T, G, sem, sb, ps, pagef, SD, gpos, grow):
    c = G["c"]
    NP2, NSL = NS // 2, PAGE + 1
    N_ALL = 64 * NSL
    NPOOL = T["cache_idx_k"].shape[1]
    junk = sb("zj", [P, NP2, NSL], BF16)
    cnt, goal, pos, sgn, thr, need, pre = (sb("z" + n, [P, NP2]) for n in ("cnt", "goal", "pos", "sgn", "thr", "need", "pre"))
    cand, best, keep = (sb("z" + n, [P, NP2], I32) for n in ("cand", "best", "keep"))
    eq, rank, ones = sb("zeq", [P, NP2, NSL]), sb("zrank", [P, NP2, NSL]), sb("zones", [P, NSL])
    hi, lo = sb("zhi", [P, NP2, NSL]), sb("zlo", [P, NP2, NSL])
    ri, rj = sb("zri", [P, NP2, NSL], I32), sb("zrj", [P, NP2, NSL], I32)
    A = sb("zA", [P, NSL, 32])
    B = sb("zB", [P, NSL, 2, 16])
    key, row = sb("zkey", [P, NSL]), sb("zrow", [P, NSL])
    lst = sb("zlst", [32, NP2, 32])
    ld = [sb("zld0", [16, P]), sb("zld1", [16, P])]
    gr = sb("zgr", [P, 16])
    pC, pL, pG = ps("zC"), ps("zL"), ps("zG")
    s_v, s_c, s_p, s_bit, s_bp, s_ab, s_l, s_lc, s_o, s_i, s_t = (sem("dz_" + n) for n in ("v", "c", "p", "bit", "bp", "ab", "l", "lc", "o", "i", "t"))
    per = NP2 + 4
    with nc.Block() as block:
        @block.tensor
        def _(pe):
            def total(n, w):
                pe.wait_ge(s_c, n + 1)
                pe.matmul(pC[:, 0:NP2], c(w), cnt[:, :], start=True, stop=True).then_inc(s_p, 1)
            total(0, "same_half")
            with pe.Fori(0, 31) as k:
                pe.wait_ge(s_bit, k * per + 2 + NP2)
                pe.matmul(pC[:, 0:NP2], c("same_half"), cnt[:, :], start=True, stop=True).then_inc(s_bp, 1)
            total(1, "same_half")
            total(2, "before_half")
            total(3, "before_half")
            for pr in range(NP2):
                pe.wait_ge(s_ab, pr + 1)
                for s in range(NSL):
                    m = pe.matmul(pL[0:32, pr * 32:(pr + 1) * 32], A[:, s, :], B[:, s, :, :].rearrange("p a b -> p (a b)"),
                                  start=(s == 0), stop=(s == NSL - 1))
                m.then_inc(s_l, 1)
            pe.wait_ge(s_i, 32)
            pe.transpose(pG[:, 0:16], ld[0][:, :], c("ident")[0:16, 0:16])
            pe.transpose(pG[:, 16:32], ld[1][:, :], c("ident")[0:16, 0:16]).then_inc(s_t, 1)

        @block.sync
        def _(sp):
            sp.wait_ge(s_lc, NP2)
            for a, n in enumerate(("dpos", "drow")):
                sp.dma_start(T[n].rearrange("n a b -> a n b"), lst[:, :, 16 * a:16 * a + 16]).then_inc(s_o, 16)
            sp.wait_ge(s_o, 32)
            for a, n in enumerate(("dpos", "drow")):
                sp.dma_start(ld[a][:, :], T[n].rearrange("n (s h a) b -> (n s h) (a b)", s=2, h=2)).then_inc(s_i, 16)

        @block.vector
        def _(dve):
            link = serial(dve, s_v)

            def count(op, by):
                for pr in range(NP2):
                    x = by if isinstance(by, float) else by[:, pr:pr + 1]
                    link(dve.tensor_scalar(junk[:, pr, :], SD[:, pr, :], x, 0.0, op, ALU.add, accum_out=cnt[:, pr:pr + 1]))

            link(dve.memset(best[:, :], 0))
            link(dve.memset(ones[:, :], 1.0))
            count(ALU.is_ge, 0.0)
            dve.sem_inc(s_c, 1)
            dve.wait_ge(s_p, 1)
            link(dve.tensor_scalar(pos[:, :], pC[:, 0:NP2], float(TOPK), None, ALU.is_ge))
            link(dve.tensor_scalar(sgn[:, :], pos[:, :], 2.0, -1.0, ALU.mult, ALU.add))
            n1 = float(N_ALL - TOPK + 1)
            link(dve.tensor_scalar(goal[:, :], pos[:, :], float(TOPK) - n1, n1 - 1.0, ALU.mult, ALU.add))
            for pr in range(NP2):
                link(dve.tensor_scalar(SD[:, pr, :], SD[:, pr, :], sgn[:, pr:pr + 1], None, ALU.mult))
            bits = c("bits").bitcast(I32)
            dve.sem_inc(s_bit, 1)
            with dve.Fori(0, 31) as k:
                dve.wait_ge(s_bit, k * per + 1)
                dve.tensor_tensor(cand[:, :], best[:, :], bits[:, bass.ds(k, 1)].to_broadcast([P, NP2]),
                                  ALU.bitwise_or).then_inc(s_bit, 1)
                dve.wait_ge(s_bit, k * per + 2)
                for pr in range(NP2):
                    dve.tensor_scalar(junk[:, pr, :], SD[:, pr, :], cand[:, pr:pr + 1].bitcast(F32), 0.0, ALU.is_ge, ALU.add,
                                      accum_out=cnt[:, pr:pr + 1]).then_inc(s_bit, 1)
                dve.wait_ge(s_bp, k + 1)
                dve.tensor_tensor(keep[:, :], goal[:, :], pC[:, 0:NP2], ALU.subtract).then_inc(s_bit, 1)
                dve.wait_ge(s_bit, k * per + 3 + NP2)
                dve.tensor_scalar(keep[:, :], keep[:, :], 31, bits[:, bass.ds(k, 1)], ALU.arith_shift_right,
                                  ALU.bitwise_and).then_inc(s_bit, 1)
                dve.wait_ge(s_bit, k * per + 4 + NP2)
                dve.tensor_tensor(best[:, :], best[:, :], keep[:, :], ALU.bitwise_or).then_inc(s_bit, 1)
            dve.wait_ge(s_bit, 31 * per + 1)
            link(dve.tensor_tensor(thr[:, :], best[:, :].bitcast(F32), sgn[:, :], ALU.mult))
            for pr in range(NP2):
                link(dve.tensor_scalar(SD[:, pr, :], SD[:, pr, :], sgn[:, pr:pr + 1], None, ALU.mult))
            count(ALU.is_gt, thr)
            dve.sem_inc(s_c, 1)
            dve.wait_ge(s_p, 2)
            link(dve.tensor_scalar(need[:, :], pC[:, 0:NP2], -1.0, float(TOPK), ALU.mult, ALU.add))
            for pr in range(NP2):
                link(dve.tensor_scalar(eq[:, pr, :], SD[:, pr, :], thr[:, pr:pr + 1], None, ALU.is_equal))
                link(dve.tensor_tensor_scan(rank[:, pr, :], ones[:, :], eq[:, pr, :], 0.0, ALU.mult, ALU.add))
            link(dve.tensor_copy(cnt[:, :], rank[:, :, NSL - 1]))
            dve.sem_inc(s_c, 1)
            dve.wait_ge(s_p, 3)
            link(dve.tensor_tensor(need[:, :], need[:, :], pC[:, 0:NP2], ALU.subtract))
            for pr in range(NP2):
                link(dve.scalar_tensor_tensor(out=eq[:, pr, :], in0=rank[:, pr, :], scalar=need[:, pr:pr + 1], in1=eq[:, pr, :],
                                              op0=ALU.is_le, op1=ALU.mult))
                link(dve.scalar_tensor_tensor(out=eq[:, pr, :], in0=SD[:, pr, :], scalar=thr[:, pr:pr + 1], in1=eq[:, pr, :],
                                              op0=ALU.is_gt, op1=ALU.add))
                link(dve.tensor_tensor_scan(rank[:, pr, :], ones[:, :], eq[:, pr, :], 0.0, ALU.mult, ALU.add))
            link(dve.tensor_copy(cnt[:, :], rank[:, :, NSL - 1]))
            dve.sem_inc(s_c, 1)
            dve.wait_ge(s_p, 4)
            link(dve.tensor_copy(pre[:, :], pC[:, 0:NP2]))
            link(dve.tensor_scalar(pre[:, :], pre[:, :], 1023.0, None, ALU.add))
            for pr in range(NP2):
                link(dve.scalar_tensor_tensor(out=rank[:, pr, :], in0=rank[:, pr, :], scalar=pre[:, pr:pr + 1], in1=eq[:, pr, :],
                                              op0=ALU.add, op1=ALU.mult))
            link(dve.tensor_scalar(ri[:, :, :], rank[:, :, :], -1024.0, None, ALU.add))
            link(dve.tensor_scalar(rj[:, :, :], ri[:, :, :], 4, None, ALU.arith_shift_right))
            link(dve.tensor_copy(hi[:, :, :], rj[:, :, :]))
            link(dve.tensor_scalar(hi[:, :, :], hi[:, :, :], c("half32"), None, ALU.add))
            link(dve.tensor_scalar(rj[:, :, :], ri[:, :, :], 15, None, ALU.bitwise_and))
            link(dve.tensor_copy(lo[:, :, :], rj[:, :, :]))
            link(dve.memset(key[:, :], float(PAGE)))
            link(dve.tensor_copy(key[:, 0:PAGE], c("iota")))
            for pr in range(NP2):
                link(dve.scalar_tensor_tensor(out=row[:, :], in0=ones[:, :], scalar=pagef[:, pr:pr + 1], in1=ones[:, :], op0=ALU.mult, op1=ALU.mult))
                link(dve.tensor_scalar(row[:, :], row[:, :], float(PAGE), None, ALU.mult))
                link(dve.tensor_tensor(row[:, :], row[:, :], key[:, :], ALU.add))
                if pr:
                    dve.wait_ge(s_l, pr)
                link(dve.tensor_tensor(A[:, :, :], hi[:, pr, :].unsqueeze(2).to_broadcast([P, NSL, 32]),
                                       c("iota")[:, 0:32].unsqueeze(1).to_broadcast([P, NSL, 32]), ALU.is_equal))
                link(dve.tensor_tensor(B[:, :, 0, :], lo[:, pr, :].unsqueeze(2).to_broadcast([P, NSL, 16]),
                                       c("iota")[:, 0:16].unsqueeze(1).to_broadcast([P, NSL, 16]), ALU.is_equal))
                link(dve.tensor_tensor(B[:, :, 1, :], B[:, :, 0, :], row[:, :].unsqueeze(2).to_broadcast([P, NSL, 16]), ALU.mult))
                link(dve.tensor_scalar(row[:, :], c("page_of").to_broadcast([P, NSL]), float(PAGE), None, ALU.mult))
                link(dve.tensor_tensor(row[:, :], row[:, :], key[:, :], ALU.add))
                link(dve.tensor_tensor(B[:, :, 0, :], B[:, :, 0, :], row[:, :].unsqueeze(2).to_broadcast([P, NSL, 16]), ALU.mult))
                dve.sem_inc(s_ab, 1)
                dve.wait_ge(s_l, pr + 1)
                dve.tensor_copy(lst[:, pr, :], pL[0:32, pr * 32:(pr + 1) * 32]).then_inc(s_lc, 1)
            dve.wait_ge(s_t, 1)
            link(dve.tensor_copy(gpos[:, :], pG[:, 0:16]))
            link(dve.tensor_scalar(gr[:, :], pG[:, 16:32], float(NPOOL * PAGE - 1), None, ALU.min))
            link(dve.tensor_copy(grow[:, :], gr[:, :]))


def sample_dsa(nc, T, G, sem, sb, ps, gpos, grow):
    c = G["c"]
    KS, VS = sb("KS", [P, 16, 512]), sb("VS", [P, 16, 512])
    qb, kb, vb = sb("qb", [P, NS, 512]), sb("kb", [P, NS, 512]), sb("vb", [P, NS, 512])
    rel = sb("rel", [P, NB_REL, H])
    rd = sb("rdd", [P, NB_REL - 1, H])
    M = sb("yM", [P, 16, NB_REL - 1])
    M2 = sb("yM2", [P, 16, NB_REL - 1])
    dist, isf, notf = sb("dist", [P, 16]), sb("isf", [P, 16]), sb("notf", [P, 16])
    S, sf = sb("yS", [P, 16, H]), sb("sf", [P, NS, H])
    PN, PF = sb("PN", [P, 16, H]), sb("PF", [P, 16, H])
    mx, mh = sb("ymx", [P, 16, H]), sb("ymh", [P, NS, H])
    prod = [sb("prod0", [P, 512]), sb("prod1", [P, 512])]
    tmp = [sb("ytmp0", [H, 512]), sb("ytmp1", [H, 512])]
    den = sb("yden", [H, NS])
    orow = sb("yorow", [NS, 512])
    pO, pD, pR = [ps("yO0"), ps("yO1")], ps("yD"), ps("yR")
    s_b, s_kk, s_vv, s_v, s_m, s_M, s_p, s_e, s_o, s_n, s_r, s_c, s_st, s_dn = (
        sem("dy_" + n) for n in ("b", "k", "vv", "v", "m", "M", "p", "e", "o", "n", "r", "c", "st", "dn"))
    s_k1 = [sem(f"dy_k{j}") for j in range(16)]
    k_rows = T["cache_dsa_k"][0].rearrange("n s h d -> (n s) (h d)")
    v_rows = T["cache_dsa_v"][0].rearrange("n s h d -> (n s) (h d)")
    with nc.Block() as block:
        @block.sync
        def _(sp):
            kf, vf = T["o9"].rearrange("l b s h d -> (l b s) (h d)"), T["o10"].rearrange("l b s h d -> (l b s) (h d)")
            for src, dst in ((T["qd"][SEQ:NTOK, :], qb), (kf, kb), (vf, vb)):
                for b in range(NS):
                    sp.dma_start(dst[:, b, :], src[b:b + 1, :].to_broadcast([P, 512])).then_inc(s_b, 16)
            sp.dma_start(rel[:, :, :].rearrange("p k h -> p (k h)"),
                         T["rel_bias"].rearrange("(o k) h -> o (k h)", o=1).to_broadcast([P, NB_REL * H])).then_inc(s_b, 16)
            sp.wait_ge(s_c, 1)
            sp.dma_start(T["omix"][SEQ:NTOK, 512:1024], orow[:, :]).then_inc(s_st, 16)
            sp.wait_ge(s_st, 16)

        @block.gpsimd
        def _(pool):
            for j in range(16):
                pool.indirect_dma_start(out=KS[:, j, :], out_offset=None, in_=k_rows,
                                        in_offset=bass.IndirectOffsetOnAxis(ap=grow[:, j:j + 1], axis=0)).then_inc(s_k1[j], 16)
            for j in range(16):
                pool.indirect_dma_start(out=VS[:, j, :], out_offset=None, in_=v_rows,
                                        in_offset=bass.IndirectOffsetOnAxis(ap=grow[:, j:j + 1], axis=0)).then_inc(s_vv, 16)
            pool.wait_ge(s_m, 1)
            pool.partition_all_reduce(mx[:, :, :].rearrange("p j h -> p (j h)"), S[:, :, :].rearrange("p j h -> p (j h)"), P, RMAX).then_inc(s_M, 1)

        @block.scalar
        def _(act):
            act.wait_ge(s_m, 2)
            act.activation(S[:, :, :], S[:, :, :], ACT.Exp).then_inc(s_e, 1)

        @block.vector
        def _(dve):
            link = serial(dve, s_v)
            dve.wait_ge(s_b, 16 * 25)
            link(dve.tensor_scalar(dist[:, :], gpos[:, :], -1.0, float(PAST), ALU.mult, ALU.add))
            link(dve.tensor_scalar(isf[:, :], gpos[:, :], float(PAST), None, ALU.is_equal))
            link(dve.tensor_scalar(notf[:, :], isf[:, :], -1.0, 1.0, ALU.mult, ALU.add))
            link(dve.tensor_tensor(rd[:, :, :], rel[:, 1:NB_REL, :], rel[:, 0:NB_REL - 1, :], ALU.subtract))
            n = NB_REL - 1
            link(dve.tensor_tensor(M[:, :, :], dist[:, :].unsqueeze(2).to_broadcast([P, 16, n]),
                                   c("rel_from").unsqueeze(1).to_broadcast([P, 16, n]), ALU.is_ge))
            for h in range(H):
                link(dve.tensor_tensor(M2[:, :, :], M[:, :, :], rd[:, :, h].unsqueeze(1).to_broadcast([P, 16, n]), ALU.mult))
                link(dve.tensor_reduce(mx[:, :, h], M2[:, :, :], AX.X, ALU.add))
            link(dve.tensor_tensor(mx[:, :, :], mx[:, :, :], rel[:, 0, :].unsqueeze(1).to_broadcast([P, 16, H]), ALU.add))
            for b in range(NS):
                link(dve.tensor_tensor(prod[0][:, :], kb[:, b, :], qb[:, b, :], ALU.mult))
                link(dve.tensor_reduce(sf[:, b, :], prod[0][:, :].rearrange("p (h d) -> p h d", h=H), AX.X, ALU.add))
            for j in range(16):
                dve.wait_ge(s_k1[j], 16)
                link(dve.tensor_tensor(prod[j % 2][:, :], KS[:, j, :], qb[:, j // 2, :], ALU.mult))
                link(dve.tensor_reduce(S[:, j, :], prod[j % 2][:, :].rearrange("p (h d) -> p h d", h=H), AX.X, ALU.add))
                link(dve.tensor_scalar(S[:, j, :], S[:, j, :], notf[:, j:j + 1], None, ALU.mult))
                link(dve.scalar_tensor_tensor(out=S[:, j, :], in0=sf[:, j // 2, :], scalar=isf[:, j:j + 1], in1=S[:, j, :],
                                              op0=ALU.mult, op1=ALU.add))
            link(dve.scalar_tensor_tensor(out=S[:, :, :], in0=S[:, :, :], scalar=DSA_SCALE, in1=mx[:, :, :], op0=ALU.mult, op1=ALU.add))
            dve.sem_inc(s_m, 1)
            dve.wait_ge(s_M, 1)
            m4 = mx[:, :, :].rearrange("p (b a) h -> p b a h", a=2)
            link(dve.tensor_tensor(mh[:, :, :], m4[:, :, 0, :], m4[:, :, 1, :], ALU.max))
            s4 = S[:, :, :].rearrange("p (b a) h -> p b a h", a=2)
            link(dve.tensor_tensor(s4, s4, mh[:, :, :].unsqueeze(2).to_broadcast([P, NS, 2, H]), ALU.subtract))
            dve.sem_inc(s_m, 1)
            dve.wait_ge(s_e, 1)
            link(dve.tensor_tensor(PN[:, :, :], S[:, :, :], notf[:, :].unsqueeze(2).to_broadcast([P, 16, H]), ALU.mult))
            link(dve.tensor_tensor(PF[:, :, :], S[:, :, :], isf[:, :].unsqueeze(2).to_broadcast([P, 16, H]), ALU.mult))
            dve.sem_inc(s_p, 1)
            dve.wait_ge(s_dn, 1)
            link(dve.reciprocal(den[:, :], pD[0:H, 0:NS]))
            for b in range(NS):
                dve.wait_ge(s_o, b + 1)
                if b >= 2:
                    dve.wait_ge(s_r, b - 1)
                dve.scalar_tensor_tensor(out=tmp[b % 2][:, :], in0=pO[b % 2][0:H, :], scalar=den[:, b:b + 1], in1=c("own_head")[0:H, :],
                                         op0=ALU.mult, op1=ALU.mult).then_inc(s_n, 1)
            dve.wait_ge(s_r, NS)
            dve.tensor_copy(orow[:, :], pR[0:NS, :]).then_inc(s_c, 1)

        @block.tensor
        def _(pe):
            pe.wait_ge(s_p, 1)
            for b in range(NS):
                for a in range(2):
                    m = pe.matmul(pD[0:H, b:b + 1], S[:, 2 * b + a, :], c("ones")[:, 0:1], start=(a == 0), stop=(a == 1))
            m.then_inc(s_dn, 1)
            pe.wait_ge(s_vv, 256)

            def fold(b):
                pe.wait_ge(s_n, b + 1)
                pe.matmul(pR[0:NS, :], c("to_row")[0:H, b * NS:(b + 1) * NS], tmp[b % 2][:, :], start=(b == 0), stop=(b == NS - 1)).then_inc(s_r, 1)

            for b in range(NS):
                if b >= 2:
                    pe.wait_ge(s_n, b - 1)
                for a in range(2):
                    j = 2 * b + a
                    pe.matmul(pO[b % 2][0:H, :], PN[:, j, :], VS[:, j, :], start=(a == 0), stop=False)
                    m = pe.matmul(pO[b % 2][0:H, :], PF[:, j, :], vb[:, b, :], start=False, stop=(a == 1))
                m.then_inc(s_o, 1)
                if b:
                    fold(b - 1)
            fold(NS - 1)


TOKP = (NT + 1) * P


def stage_out(nc, T, G, sem, sb, ps):
    c = G["c"]
    Wo = sb("Wo", [P, KD, D])
    Wr = sb("Wr", [P, KD, NE])
    mod = {n: (sb("r_" + n, [P, D]), sb("rs_" + n, [NS, D])) for n in ("ga", "sf", "cf")}
    gf = sb("gfr", [P, D])
    mi = [sb(f"mi{i}", [P, D]) for i in range(2)]
    xi = [sb(f"xi{i}", [P, D]) for i in range(2)]
    x1 = [sb(f"x1{i}", [P, D]) for i in range(2)]
    h2 = [sb(f"h2{i}", [P, D]) for i in range(2)]
    mT = [sb(f"mT{i}", [P, KD, P]) for i in range(2)]
    hT = sb("hT", [P, KD, P])
    junk, st, epst = sb("ojunk", [P, D]), sb("ost", [P, 3, NT + 1]), sb("oeps", [P, 1])
    lg = G["lg"]
    pT, pY, pR = [ps(f"oT{i}") for i in range(4)], [ps("oY0"), ps("oY1")], ps("oR")
    names = ("w", "m", "mt", "mte", "y", "x1", "ss", "rt", "rr", "h", "ht", "hte", "r", "lg", "v", "z", "he")
    s_w, s_m, s_mt, s_mte, s_y, s_x1, s_ss, s_rt, s_rr, s_h, s_ht, s_hte, s_r, s_lg, s_v, s_z, s_he = (sem("ou_" + n) for n in names)
    s_in, s_st = [sem("ou_i0"), sem("ou_i1")], [sem("ou_s0"), sem("ou_s1")]
    xp, xs = T["x_prompt"][0], T["x_sample"].rearrange("b s d -> (b s) d")
    with nc.Block() as block:
        @block.sync
        def _(sp):
            for j, n in ((2, "ga"), (3, "sf"), (4, "cf")):
                sp.dma_start(mod[n][0][:, :], T["mod"][NS:NC9, j * D:(j + 1) * D].to_broadcast([P, D])).then_inc(s_m, 16)
                sp.dma_start(mod[n][1][:, :], T["mod"][0:NS, j * D:(j + 1) * D]).then_inc(s_m, 16)
            sp.dma_start(gf[:, :], T["g_ffn_norm"].to_broadcast([P, D])).then_inc(s_m, 16)
            sp.dma_start(Wr[:, :, :], T["w_router"][0].rearrange("(k p) n -> p k n", p=P)).then_inc(s_m, 16)
            for t, R in tiles():
                if t >= 2:
                    sp.wait_ge(s_x1, 2 * (t - 1))
                    sp.wait_ge(s_mt, 2 * (t - 1))
                sp.dma_start(mi[t % 2][0:R, :], T["omix"][t * P:t * P + R, :]).then_inc(s_in[t % 2], 16)
                sp.dma_start(xi[t % 2][0:R, :], token_rows(xp, xs, t)).then_inc(s_in[t % 2], 16)
                if t == 0:
                    sp.dma_start(Wo[:, :, :], T["w_out"][0].rearrange("(k p) n -> p k n", p=P)).then_inc(s_w, 16)

        @block.gpsimd
        def _(pool):
            for t, R in tiles():
                pool.wait_ge(s_h, t + 1)
                if t == NT:
                    R2 = P
                else:
                    R2 = R
                pool.dma_start(T["x1"][t * P:t * P + R, :], x1[t % 2][0:R, :]).then_inc(s_st[t % 2], 16)
                pool.dma_start(T["h2"][t * P:t * P + R2, :], h2[t % 2][0:R2, :]).then_inc(s_st[t % 2], 16)
            pool.dma_start(T["h2"][(NT + 1) * P:(NT + 2) * P, :], h2[NT % 2][:, :]).then_inc(s_st[0], 16)
            pool.wait_ge(s_st[0], 32 * 5 + 16)
            pool.wait_ge(s_st[1], 32 * 4)

        @block.tensor
        def _(pe):
            def turn_mix(t, R):
                pe.wait_ge(s_in[t % 2], 32 * (t // 2 + 1))
                if t:
                    pe.wait_ge(s_mte, 2 * t)
                for k in range(KD):
                    m = pe.transpose(pT[k // 4][:, (k % 4) * P:(k % 4) * P + R], mi[t % 2][0:R, k * P:(k + 1) * P], c("ident")[0:R, 0:R])
                    if k % 4 == 3:
                        m.then_inc(s_mt, 1)

            def out(t, R):
                pe.wait_ge(s_mte, 2 * (t + 1))
                if t == 0:
                    pe.wait_ge(s_w, 16)
                else:
                    pe.wait_ge(s_x1, 2 * t)
                for n in range(2):
                    for k in range(KD):
                        m = pe.matmul(pY[n][0:R, :], mT[t % 2][:, k, 0:R], Wo[:, k, n * 512:(n + 1) * 512], start=(k == 0), stop=(k == KD - 1))
                    m.then_inc(s_y, 1)

            def route(t, R):
                pe.wait_ge(s_h, t + 1)
                if t:
                    pe.wait_ge(s_hte, 2 * t)
                for k in range(KD):
                    m = pe.transpose(pT[2 + k // 4][:, (k % 4) * P:(k % 4) * P + R], h2[t % 2][0:R, k * P:(k + 1) * P], c("ident")[0:R, 0:R])
                    if k % 4 == 3:
                        m.then_inc(s_ht, 1)
                pe.wait_ge(s_hte, 2 * (t + 1))
                if t:
                    pe.wait_ge(s_lg, t)
                for k in range(KD):
                    m = pe.matmul(pR[0:R, 0:NE], hT[:, k, 0:R], Wr[:, k, :], start=(k == 0), stop=(k == KD - 1))
                m.then_inc(s_r, 1)

            turn_mix(*tiles()[0])
            for t, R in tiles():
                if t < NT:
                    turn_mix(*tiles()[t + 1])
                out(t, R)
                if t:
                    route(*tiles()[t - 1])
            route(*tiles()[NT])

        @block.scalar
        def _(act):
            def mt(t, R):
                for n in range(2):
                    act.wait_ge(s_mt, 2 * t + n + 1)
                    if t >= 2:
                        act.wait_ge(s_y, 2 * (t - 1))
                    act.activation(mT[t % 2][:, 4 * n:4 * n + 4, 0:R], pT[n][:, :].rearrange("p (k r) -> p k r", k=4)[:, :, 0:R], ACT.Copy).then_inc(s_mte, 1)

            def ht(t, R):
                for n in range(2):
                    act.wait_ge(s_ht, 2 * t + n + 1)
                    if t:
                        act.wait_ge(s_r, t)
                    act.activation(hT[:, 4 * n:4 * n + 4, 0:R], pT[2 + n][:, :].rearrange("p (k r) -> p k r", k=4)[:, :, 0:R], ACT.Copy).then_inc(s_hte, 1)

            act.wait_ge(s_z, 1)
            mt(*tiles()[0])
            for t, R in tiles():
                if t < NT:
                    mt(*tiles()[t + 1])
                if t:
                    ht(*tiles()[t - 1])
                act.wait_ge(s_x1, 2 * (t + 1))
                if t:
                    act.wait_ge(s_ss, t)
                act.activation(junk[0:R, :], x1[t % 2][0:R, :], ACT.Square, accum_out=st[0:R, 0, t:t + 1]).then_inc(s_ss, 1)
                act.wait_ge(s_ss, t + 1)
                act.activation(st[0:R, 1, t:t + 1], st[0:R, 0, t:t + 1], ACT.Sqrt, scale=1.0 / D, bias=epst[0:R, 0:1]).then_inc(s_rt, 1)
            ht(*tiles()[NT])

        @block.vector
        def _(dve):
            link = serial(dve, s_v)
            link(dve.memset(epst[:, :], EPS))
            dve.sem_inc(s_z, 1)
            link(dve.memset(lg[:, :, :], 0.0))
            dve.wait_ge(s_m, 128)
            A = mod["cf"]
            for a, R in ((0, P), (1, NS)):
                link(dve.scalar_tensor_tensor(out=A[a][0:R, :], in0=A[a][0:R, :], scalar=1.0, in1=gf[0:R, :], op0=ALU.add, op1=ALU.mult))
            for t, R in tiles():
                a = 0 if t < NT else 1
                if t >= 2:
                    dve.wait_ge(s_st[t % 2], 32 * (t // 2))
                    dve.wait_ge(s_ht, 2 * (t - 1))
                if t == NT:
                    link(dve.memset(h2[t % 2][:, :], 0.0))
                dve.wait_ge(s_in[t % 2], 32 * (t // 2 + 1))
                for n in range(2):
                    sl = slice(n * 512, (n + 1) * 512)
                    dve.wait_ge(s_y, 2 * t + n + 1)
                    link(dve.tensor_tensor(x1[t % 2][0:R, sl], pY[n][0:R, :], mod["ga"][a][0:R, sl], ALU.mult))
                    dve.tensor_tensor(x1[t % 2][0:R, sl], x1[t % 2][0:R, sl], xi[t % 2][0:R, sl], ALU.add).then_inc(s_x1, 1)
                if t:
                    dve.wait_ge(s_r, t)
                    dve.tensor_copy(lg[0:P, t - 1, :], pR[0:P, 0:NE]).then_inc(s_lg, 1)
                dve.wait_ge(s_rt, t + 1)
                link(dve.reciprocal(st[0:R, 2, t:t + 1], st[0:R, 1, t:t + 1]))
                link(dve.scalar_tensor_tensor(out=h2[t % 2][0:R, :], in0=x1[t % 2][0:R, :], scalar=st[0:R, 2, t:t + 1], in1=A[a][0:R, :],
                                              op0=ALU.mult, op1=ALU.mult))
                dve.tensor_tensor(h2[t % 2][0:R, :], h2[t % 2][0:R, :], mod["sf"][a][0:R, :], ALU.add).then_inc(s_h, 1)
            dve.wait_ge(s_r, NT + 1)
            dve.tensor_copy(lg[0:NS, NT, :], pR[0:NS, 0:NE]).then_inc(s_lg, 1)


def stage_dispatch(nc, T, G, sem, sb, ps):
    c, lg = G["c"], G["lg"]
    NTT = NT + 1
    sh = [P, NTT, NE]
    SC, BI, S1, S2, SEL, GT, SV = (sb("g" + n, sh) for n in ("SC", "BI", "S1", "S2", "SEL", "GT", "SV"))
    br, ones, tot, car, pre = sb("gbr", [P, NE]), sb("gone", [P, NE]), sb("gtot", sh), sb("gcar", sh), sb("gpre", sh)
    m1, m2, cn, gr = (sb("g" + n, [P, NTT, NG]) for n in ("m1", "m2", "cn", "gr"))
    pw, pe2 = sb("gpw", [P, NTT, NG, NG]), sb("gpe", [P, NTT, NG, NG])
    top, need, sums = sb("gtop", [P, NTT, 8]), sb("gneed", [P, NTT]), sb("gsum", [P, NTT])
    nb, nbi, be = sb("gnb", [P, NE]), sb("gnbi", [P, NE], I32), sb("gbe", [P, NE])
    eb, ebT = sb("geb", [P, 2]), sb("gebT", [2, P])
    tok = sb("gtok", [P, NTT], I32)
    tokf = sb("gtokf", [P, NTT])
    zl = sb("gzl", [NBLK, P], I32)
    li, lf = sb("gli", [NBLK, P], I32), sb("glf", [NBLK, P])
    slotf = sb("gslotf", [P, NTT, 8])
    pA, pB, pC, pD, pE, pL = (ps(f"g{n}") for n in "ABCDEL")
    names = ("in", "v", "sg", "sel", "cnt", "z", "zd", "eb", "ebt", "sl", "sc", "li", "lf", "lt", "m")
    s_in, s_v, s_sg, s_sel, s_cnt, s_z, s_zd, s_eb, s_ebt, s_sl, s_sc, s_li, s_lf, s_lt, s_m = (sem("gd_" + n) for n in names)
    W = NTT * NE
    f = lambda a: a[:, :, :].rearrange("p t e -> p (t e)")
    with nc.Block() as block:
        @block.sync
        def _(sp):
            sp.dma_start(br[:, :], T["b_router"].to_broadcast([P, NE])).then_inc(s_in, 16)
            sp.wait_ge(s_z, 1)
            sp.dma_start(T["slot_tok"].rearrange("(b p) o -> b (p o)", p=P), zl[:, :]).then_inc(s_zd, 16)
            sp.wait_ge(s_sc, 16 * NTT * TK)
            sp.dma_start(li[:, :], T["slot_tok"].rearrange("(b p) o -> b (p o)", p=P)).then_inc(s_li, 16)

        @block.scalar
        def _(act):
            act.activation(SC[:, :, :], lg[:, :, :], ACT.Sigmoid).then_inc(s_sg, 1)

        @block.gpsimd
        def _(pool):
            pool.wait_ge(s_zd, 16)
            pool.wait_ge(s_sl, 1)
            for t in range(NTT):
                R = P if t < NT else NS
                for k in range(TK):
                    pool.indirect_dma_start(out=T["slot_tok"], out_offset=bass.IndirectOffsetOnAxis(ap=G["slot"][0:R, t, k:k + 1], axis=0),
                                            in_=tok[0:R, t:t + 1], in_offset=None).then_inc(s_sc, 16)

        @block.tensor
        def _(pe):
            pe.wait_ge(s_sel, 1)
            for w, (p0, p1) in (("ones", (pA, pB)), ("before", (pC, pD))):
                pe.matmul(p0[:, :], c(w), f(SEL)[:, 0:512], start=True, stop=True)
                m = pe.matmul(p1[:, 0:W - 512], c(w), f(SEL)[:, 512:W], start=True, stop=True)
            m.then_inc(s_cnt, 1)
            pe.wait_ge(s_eb, 1)
            pe.transpose(pE[0:2, 0:P], eb[:, :], c("ident")).then_inc(s_ebt, 1)
            pe.wait_ge(s_lf, 1)
            pe.transpose(pL[:, 0:NBLK], lf[:, :], c("ident")[0:NBLK, 0:NBLK]).then_inc(s_lt, 1)

        @block.vector
        def _(dve):
            link = serial(dve, s_v)
            link(dve.memset(zl[:, :], 0))
            dve.sem_inc(s_z, 1)
            link(dve.memset(ones[:, :], 1.0))
            link(dve.tensor_scalar(tokf[:, :], c("iota")[:, 0:NTT], float(P), c("part"), ALU.mult, ALU.add))
            link(dve.tensor_copy(tok[:, :], tokf[:, :]))
            dve.wait_ge(s_in, 16)
            dve.wait_ge(s_sg, 1)
            link(dve.tensor_tensor(BI[:, :, :], SC[:, :, :], br[:, :].unsqueeze(1).to_broadcast(sh), ALU.add))
            g4 = lambda a: a[:, :, :].rearrange("p t (g e) -> p t g e", g=NG)
            bc = lambda a: a[:, :, :].unsqueeze(3).to_broadcast([P, NTT, NG, NE // NG])
            link(dve.tensor_reduce(m1[:, :, :], g4(BI), AX.X, ALU.max))
            link(dve.tensor_tensor(g4(S1), g4(BI), bc(m1), ALU.is_equal))
            link(dve.tensor_reduce(cn[:, :, :], g4(S1), AX.X, ALU.add))
            link(dve.scalar_tensor_tensor(out=S1[:, :, :], in0=S1[:, :, :], scalar=NEG, in1=BI[:, :, :], op0=ALU.mult, op1=ALU.add))
            link(dve.tensor_reduce(m2[:, :, :], g4(S1), AX.X, ALU.max))
            link(dve.tensor_scalar(cn[:, :, :], cn[:, :, :], 2.0, -1.0, ALU.is_ge, ALU.add))
            link(dve.scalar_tensor_tensor(out=cn[:, :, :], in0=cn[:, :, :], scalar=-NEG, in1=m1[:, :, :], op0=ALU.mult, op1=ALU.add))
            link(dve.tensor_tensor(m2[:, :, :], m2[:, :, :], cn[:, :, :], ALU.max))
            link(dve.tensor_tensor(m1[:, :, :], m1[:, :, :], m2[:, :, :], ALU.add))
            mine = m1[:, :, :].unsqueeze(3).to_broadcast([P, NTT, NG, NG])
            other = m1[:, :, :].unsqueeze(2).to_broadcast([P, NTT, NG, NG])
            link(dve.tensor_tensor(pw[:, :, :, :], other, mine, ALU.is_gt))
            link(dve.tensor_tensor(pe2[:, :, :, :], other, mine, ALU.is_equal))
            lower = c("lower8").rearrange("p (a b) -> p a b", a=NG).unsqueeze(1).to_broadcast([P, NTT, NG, NG])
            link(dve.tensor_tensor(pe2[:, :, :, :], pe2[:, :, :, :], lower, ALU.mult))
            link(dve.tensor_tensor(pw[:, :, :, :], pw[:, :, :, :], pe2[:, :, :, :], ALU.add))
            link(dve.tensor_reduce(gr[:, :, :], pw[:, :, :, :], AX.X, ALU.add))
            link(dve.tensor_scalar(gr[:, :, :], gr[:, :, :], float(TKG), -1.0, ALU.is_lt, ALU.add))
            link(dve.tensor_scalar(gr[:, :, :], gr[:, :, :], -NEG, None, ALU.mult))
            link(dve.tensor_tensor(g4(BI), g4(BI), bc(gr), ALU.add))
            for t in range(NTT):
                link(dve.max(top[:, t, :], BI[:, t, :]))
            t6 = top[:, :, TK - 1:TK].to_broadcast(sh)
            link(dve.tensor_tensor(S1[:, :, :], BI[:, :, :], t6, ALU.is_gt))
            link(dve.tensor_tensor(S2[:, :, :], BI[:, :, :], t6, ALU.is_equal))
            link(dve.tensor_reduce(need[:, :], S1[:, :, :], AX.X, ALU.add))
            link(dve.tensor_scalar(need[:, :], need[:, :], -1.0, float(TK), ALU.mult, ALU.add))
            for t in range(NTT):
                link(dve.tensor_tensor_scan(SV[:, t, :], ones[:, :], S2[:, t, :], 0.0, ALU.mult, ALU.add))
            link(dve.tensor_tensor(SV[:, :, :], SV[:, :, :], need[:, :].unsqueeze(2).to_broadcast(sh), ALU.is_le))
            link(dve.tensor_tensor(S2[:, :, :], S2[:, :, :], SV[:, :, :], ALU.mult))
            link(dve.tensor_tensor(S1[:, :, :], S1[:, :, :], S2[:, :, :], ALU.add))
            link(dve.tensor_tensor(SEL[:, :, :], S1[:, :, :], c("is_token").unsqueeze(2).to_broadcast(sh), ALU.mult))
            dve.sem_inc(s_sel, 1)
            link(dve.tensor_tensor(GT[:, :, :], SC[:, :, :], S1[:, :, :], ALU.mult))
            link(dve.tensor_reduce(sums[:, :], GT[:, :, :], AX.X, ALU.add))
            link(dve.reciprocal(sums[:, :], sums[:, :]))
            link(dve.tensor_tensor(GT[:, :, :], GT[:, :, :], sums[:, :].unsqueeze(2).to_broadcast(sh), ALU.mult))
            link(dve.tensor_scalar(GT[:, :, :], GT[:, :, :], ROUTED_SCALE, None, ALU.mult))
            dve.wait_ge(s_cnt, 1)
            link(dve.tensor_copy(f(tot)[:, 0:512], pA[:, :]))
            link(dve.tensor_copy(f(tot)[:, 512:W], pB[:, 0:W - 512]))
            link(dve.tensor_copy(f(pre)[:, 0:512], pC[:, :]))
            link(dve.tensor_copy(f(pre)[:, 512:W], pD[:, 0:W - 512]))
            link(dve.memset(car[:, 0, :], 0.0))
            for t in range(1, NTT):
                link(dve.tensor_tensor(car[:, t, :], car[:, t - 1, :], tot[:, t - 1, :], ALU.add))
            link(dve.tensor_tensor(nb[:, :], car[:, NTT - 1, :], tot[:, NTT - 1, :], ALU.add))
            link(dve.tensor_scalar(nbi[:, :], nb[:, :], float(P - 1), None, ALU.add))
            link(dve.tensor_scalar(nbi[:, :], nbi[:, :], 7, None, ALU.arith_shift_right))
            link(dve.tensor_copy(nb[:, :], nbi[:, :]))
            link(dve.tensor_tensor_scan(be[:, :], ones[:, :], nb[:, :], 0.0, ALU.mult, ALU.add))
            link(dve.tensor_scalar(S1[:, 0, :], be[:, :], c("part"), 0.0, ALU.is_le, ALU.add, accum_out=eb[:, 0:1]))
            link(dve.tensor_scalar(eb[:, 0:1], eb[:, 0:1], float(NE - 1), None, ALU.min))
            link(dve.tensor_copy(eb[:, 1:2], be[:, NE - 1:NE]))
            dve.sem_inc(s_eb, 1)
            link(dve.tensor_tensor(nb[:, :], be[:, :], nb[:, :], ALU.subtract))
            link(dve.tensor_scalar(nb[:, :], nb[:, :], float(P), 1.0, ALU.mult, ALU.add))
            link(dve.tensor_tensor(SV[:, :, :], pre[:, :, :], car[:, :, :], ALU.add))
            link(dve.tensor_tensor(SV[:, :, :], SV[:, :, :], nb[:, :].unsqueeze(1).to_broadcast(sh), ALU.add))
            link(dve.tensor_tensor(SV[:, :, :], SV[:, :, :], SEL[:, :, :], ALU.mult))
            for t in range(NTT):
                link(dve.max(slotf[:, t, :], SV[:, t, :]))
            for k in range(TK):
                link(dve.tensor_tensor(S2[:, :, :], SV[:, :, :], slotf[:, :, k:k + 1].to_broadcast(sh), ALU.is_equal))
                link(dve.tensor_tensor(S2[:, :, :], S2[:, :, :], GT[:, :, :], ALU.mult))
                link(dve.tensor_reduce(G["gate"][:, :, k], S2[:, :, :], AX.X, ALU.add))
            link(dve.tensor_scalar(slotf[:, :, :], slotf[:, :, :], -1.0, 0.0, ALU.add, ALU.max))
            link(dve.tensor_copy(G["slot"][:, :, :], slotf[:, :, :]))
            dve.sem_inc(s_sl, 1)
            dve.wait_ge(s_ebt, 1)
            link(dve.tensor_copy(G["expert"][:, :], pE[0:2, 0:P]))
            dve.wait_ge(s_li, 16)
            link(dve.tensor_copy(lf[:, :], li[:, :]))
            dve.sem_inc(s_lf, 1)
            dve.wait_ge(s_lt, 1)
            link(dve.tensor_copy(G["list"][:, :], pL[:, 0:NBLK]))
    with nc.Block() as block:
        @block.sync
        def _(sp):
            sp.dma_start(G["nblk"][0:1, :], G["expert"][1:2, 0:1]).then_inc(s_m, 16)
            sp.wait_ge(s_m, 16)


def swiglu_blocks(nc, T, G, sem, sb, ps, pre, n_pairs, shared):
    c = G["c"]
    GU0, Y0, XT0 = 4, 7, 7
    WG = [sb(f"{pre}WG{i}", [P, KD, 2 * DE]) for i in range(1 if shared else 4)]
    WD = [sb(f"{pre}WD{i}", [P, 2, D]) for i in range(1 if shared else 4)]
    X = [sb(f"{pre}X{i}", [P, D]) for i in range(4)]
    XT = [sb(f"{pre}XT{i}", [P, KD, P]) for i in range(2)]
    sg = [sb(f"{pre}sg{i}", [P, DE]) for i in range(2)]
    av = [sb(f"{pre}av{i}", [P, DE]) for i in range(2)]
    AT = [sb(f"{pre}AT{i}", [P, 2, P]) for i in range(2)]
    Y = [sb(f"{pre}Y{i}", [P, D]) for i in range(2)]
    ix = [sb(f"{pre}ix{i}", [P, 1], I32) for i in range(4)]
    pX, pG, pA, pY = [ps(pre + "pX0"), ps(pre + "pX1")], [ps(pre + "pG0"), ps(pre + "pG1")], ps(pre + "pA"), [ps(pre + "pY0"), ps(pre + "pY1")]
    names = ("ix", "xt", "xea", "xed", "gu", "sg", "a1", "a", "at", "ate", "y", "yea", "yed", "k")
    s_ix, s_xt, s_xea, s_xed, s_gu, s_sg, s_a1, s_a, s_at, s_ate, s_y, s_yea, s_yed, s_k = (sem(pre + n) for n in names)
    s_w, s_wd, s_x = ([sem(f"{pre}{n}{i}") for i in range(4)] for n in ("w", "wd", "x"))
    s_st = [sem(f"{pre}st{i}") for i in range(2)]
    s_z, s_zd = sem(pre + "z"), sem(pre + "zd")
    zero = None if shared else sb(pre + "zero", [P, D])
    out = T["ysh"] if shared else T["yblk"]

    def run(eng, pair):
        if shared:
            with eng.Fori(0, n_pairs // 2) as i:
                for q in range(2):
                    pair(i, q)
            if n_pairs % 2:
                pair(n_pairs // 2, 0)
        else:
            used = eng.value_load(G["nblk"][0:1, 0:1], min_val=0, max_val=NBLK)
            with eng.Fori(0, n_pairs // 2) as i:
                for q in range(2):
                    with eng.If(i * 4 + 2 * q < used):
                        pair(i, q)

    with nc.Block() as block:
        @block.sync
        def _(sp):
            if shared:
                sp.dma_start(WG[0][:, :, :], T["w_s_gu"].rearrange("a (k p) n -> p (a k) n", p=P)).then_inc(s_w[0], 16)
                sp.dma_start(WD[0][:, :, :], T["w_s_down"].rearrange("a (k p) n -> p (a k) n", p=P)).then_inc(s_wd[0], 16)

                def rows(i, q):
                    for u in range(2):
                        b = 2 * q + u
                        sp.wait_ge(s_xt, (i * 4 + b) * 2 + 1)
                        sp.dma_start(X[b][:, :], T["h2"].rearrange("(t p) d -> t p d", p=P)[bass.ds(i * 4 + b, 1)]
                                     .rearrange("a p d -> p (a d)")).then_inc(s_x[b], 16)
                run(sp, rows)
                return

            def weights(i, q):
                for u in range(2):
                    b = 2 * q + u
                    e = sp.value_load(G["expert"][0:1, bass.ds(i * 4 + b, 1)], min_val=0, max_val=NE - 1)
                    sp.wait_ge(s_gu, i * 4 + b + 1)
                    sp.dma_start(WG[b][:, :, :], T["w_e_gu"][0, bass.ds(e, 1)].rearrange("a (k p) n -> p (a k) n", p=P)).then_inc(s_w[b], 16)
                    sp.wait_ge(s_y, (i * 4 + b) * 2 + 1)
                    sp.dma_start(WD[b][:, :, :], T["w_e_down"][0, bass.ds(e, 1)].rearrange("a (k p) n -> p (a k) n", p=P)).then_inc(s_wd[b], 16)
            used = sp.value_load(G["nblk"][0:1, 0:1], min_val=0, max_val=NBLK)
            with sp.Fori(0, n_pairs // 2) as i:
                for q in range(2):
                    with sp.If(i * 4 + 2 * q < used):
                        weights(i, q)
            sp.wait_ge(s_z, 1)
            with sp.Fori(0, n_pairs) as i:
                with sp.If((n_pairs - 1 - i) * 2 >= used):
                    sp.dma_start(out.rearrange("(q u p) d -> q p u d", u=2, p=P)[bass.ds(n_pairs - 1 - i, 1)].rearrange("a p u d -> p (a u) d"),
                                 zero[:, :].unsqueeze(1).to_broadcast([P, 2, D])).then_inc(s_zd, 16)
                    sp.wait_ge(s_zd, i * 16 + 16)
                    sp.sem_inc(s_z, 1)

        if not shared:
            @block.gpsimd
            def _(pool):
                def gather(i, q):
                    for u in range(2):
                        b = 2 * q + u
                        pool.wait_ge(s_xt, (i * 4 + b) * 2 + 1)
                        pool.tensor_copy(ix[b][:, :], G["list"][:, bass.ds(i * 4 + b, 1)]).then_inc(s_ix, 1)
                        pool.wait_ge(s_ix, i * 4 + b + 1)
                        pool.sem_inc(s_k, 1)
                        pool.indirect_dma_start(out=X[b][:, :], out_offset=None, in_=T["h2"],
                                                in_offset=bass.IndirectOffsetOnAxis(ap=ix[b][:, 0:1], axis=0)).then_inc(s_x[b], 16)
                run(pool, gather)

        @block.tensor
        def _(pe):
            for s, start in ((s_xt, XT0), (s_gu, GU0), (s_at, 1), (s_y, Y0)):
                pe.sem_inc(s, start)

            def pair(i, q):
                n0 = i * 4 + 2 * q
                for u in range(2):
                    pe.wait_ge(s_x[2 * q + u], i * 16 + 16)
                    for n in range(2):
                        pe.wait_ge(s_xea if n == 0 else s_xed, n0 + u + 1)
                        for k in range(4):
                            m = pe.transpose(pX[n][:, k * P:(k + 1) * P], X[2 * q + u][:, (4 * n + k) * P:(4 * n + k + 1) * P], c("ident"))
                        m.then_inc(s_xt, 1)
                for u in range(2):
                    w = 0 if shared else 2 * q + u
                    pe.wait_ge(s_w[w], 16 if shared else i * 16 + 16)
                    pe.wait_ge(s_xea, n0 + u + 1 + 1)
                    pe.wait_ge(s_xed, n0 + u + 1 + 1)
                    pe.wait_ge(s_a, n0 + 1)
                    for k in range(KD):
                        m = pe.matmul(pG[u][:, :], XT[u][:, k, :], WG[w][:, k, :], start=(k == 0), stop=(k == KD - 1))
                    m.then_inc(s_gu, 1)
                for u in range(2):
                    w = 0 if shared else 2 * q + u
                    pe.wait_ge(s_a, n0 + u + 1 + 1)
                    pe.wait_ge(s_ate, n0 + u + 1)
                    for k in range(2):
                        m = pe.transpose(pA[:, k * P:(k + 1) * P], av[u][:, k * P:(k + 1) * P], c("ident"))
                    m.then_inc(s_at, 1)
                    pe.wait_ge(s_ate, n0 + u + 1 + 1)
                    pe.wait_ge(s_wd[w], 16 if shared else i * 16 + 16)
                    for n in range(2):
                        pe.wait_ge(s_yea if n == 0 else s_yed, n0 + u + 1)
                        for k in range(2):
                            m = pe.matmul(pY[n][:, :], AT[u][:, k, :], WD[w][:, k, n * 512:(n + 1) * 512], start=(k == 0), stop=(k == 1))
                        m.then_inc(s_y, 1)
            run(pe, pair)

        @block.scalar
        def _(act):
            for s in (s_xea, s_yea):
                act.sem_inc(s, 1)
            for u in range(2):
                act.dma_start(T["pad"][u:u + 1, :], c("iota")[0:1, :]).then_inc(s_st[u], 16)

            def pair(i, q):
                n0 = i * 4 + 2 * q
                for u in range(2):
                    act.wait_ge(s_xt, (n0 + u) * 2 + 1 + XT0)
                    act.wait_ge(s_gu, n0 + u - 2 + 1 + GU0)
                    act.activation(XT[u][:, 0:4, :], pX[0][:, :].rearrange("p (k r) -> p k r", k=4), ACT.Copy).then_inc(s_xea, 1)
                for u in range(2):
                    act.wait_ge(s_gu, n0 + u + 1 + GU0)
                    act.wait_ge(s_a1, n0 + 1)
                    act.activation(sg[u][:, :], pG[u][:, 0:DE], ACT.Sigmoid).then_inc(s_sg, 1)
                for u in range(2):
                    act.wait_ge(s_y, (n0 + u) * 2 + 1 + Y0)
                    act.wait_ge(s_st[u], (i * 2 + q) * 16 + 16)
                    act.activation(Y[u][:, 0:512], pY[0][:, :], ACT.Copy).then_inc(s_yea, 1)
                    act.wait_ge(s_yea, n0 + u + 1 + 1)
                    act.wait_ge(s_yed, n0 + u + 1 + 1)
                    act.dma_start(out.rearrange("(t p) d -> t p d", p=P)[bass.ds(n0 + u, 1)].rearrange("a p d -> p (a d)"),
                                  Y[u][:, :]).then_inc(s_st[u], 16)
            run(act, pair)

        @block.vector
        def _(dve):
            for s in (s_xed, s_a1, s_a, s_ate, s_yed):
                dve.sem_inc(s, 1)
            if not shared:
                dve.memset(zero[:, :], 0.0).then_inc(s_z, 1)

            def pair(i, q):
                n0 = i * 4 + 2 * q
                for u in range(2):
                    dve.wait_ge(s_xt, (n0 + u) * 2 + 2 + XT0)
                    dve.wait_ge(s_gu, n0 + u - 2 + 1 + GU0)
                    dve.tensor_copy(XT[u][:, 4:8, :], pX[1][:, :].rearrange("p (k r) -> p k r", k=4)).then_inc(s_xed, 1)
                for u in range(2):
                    dve.wait_ge(s_sg, n0 + u + 1)
                    dve.tensor_tensor(sg[u][:, :], sg[u][:, :], pG[u][:, 0:DE], ALU.mult).then_inc(s_a1, 1)
                    dve.wait_ge(s_a1, n0 + u + 1 + 1)
                    dve.wait_ge(s_at, n0 + 1)
                    dve.tensor_tensor(av[u][:, :], sg[u][:, :], pG[u][:, DE:2 * DE], ALU.mult).then_inc(s_a, 1)
                for u in range(2):
                    dve.wait_ge(s_at, n0 + u + 1 + 1)
                    dve.wait_ge(s_y, n0 * 2 + Y0)
                    dve.tensor_copy(AT[u][:, :, :], pA[:, 0:2 * P].rearrange("p (k r) -> p k r", k=2)).then_inc(s_ate, 1)
                    dve.wait_ge(s_y, (n0 + u) * 2 + 2 + Y0)
                    dve.wait_ge(s_st[u], (i * 2 + q) * 16 + 16)
                    dve.tensor_copy(Y[u][:, 512:D], pY[1][:, :]).then_inc(s_yed, 1)
            run(dve, pair)
    with nc.Block() as block:
        @block.sync
        def _(sp):
            if shared:
                for u in range(2):
                    sp.wait_ge(s_st[u], 16 * n_pairs + 16)
            else:
                used = sp.value_load(G["nblk"][0:1, 0:1], min_val=0, max_val=NBLK)
                with sp.Fori(0, n_pairs) as i:
                    with sp.If(i * 2 < used):
                        for u in range(2):
                            sp.wait_ge(s_st[u], i * 16 + 32)
                        sp.sem_inc(s_z, 1)


def stage_shared(nc, T, G, sem, sb, ps):
    swiglu_blocks(nc, T, G, sem, sb, ps, "sh_", (NT + 2) // 2, True)


def stage_routed(nc, T, G, sem, sb, ps):
    swiglu_blocks(nc, T, G, sem, sb, ps, "ex_", NBLK // 2, False)


def stage_combine(nc, T, G, sem, sb, ps):
    acc = [sb(f"cacc{i}", [P, D]) for i in range(2)]
    x1 = [sb(f"cx1{i}", [P, D]) for i in range(2)]
    E = [sb(f"cE{i}", [P, TK, D]) for i in range(2)]
    gf, gfs = sb("cgf", [P, D]), sb("cgfs", [NS, D])
    s_m, s_v, s_r = sem("cb_m"), sem("cb_v"), sem("cb_r")
    s_in, s_e, s_o = ([sem(f"cb_{n}{i}") for i in range(2)] for n in ("in", "e", "o"))
    y_p, y_s = T["o0"][0], T["o1"].rearrange("b s d -> (b s) d")
    with nc.Block() as block:
        @block.sync
        def _(sp):
            sp.dma_start(gf[:, :], T["mod"][NS:NC9, 5 * D:6 * D].to_broadcast([P, D])).then_inc(s_m, 16)
            sp.dma_start(gfs[:, :], T["mod"][0:NS, 5 * D:6 * D]).then_inc(s_m, 16)
            for t, R in tiles():
                if t >= 2:
                    sp.wait_ge(s_o[t % 2], 16 * (t // 2))
                sp.dma_start(acc[t % 2][0:R, :], T["ysh"][t * P:t * P + R, :]).then_inc(s_in[t % 2], 16)
                sp.dma_start(x1[t % 2][0:R, :], T["x1"][t * P:t * P + R, :]).then_inc(s_in[t % 2], 16)

        @block.gpsimd
        def _(pool):
            for t, R in tiles():
                if t >= 2:
                    pool.wait_ge(s_r, t - 1)
                for k in range(TK):
                    pool.indirect_dma_start(out=E[t % 2][0:R, k, :], out_offset=None, in_=T["yblk"],
                                            in_offset=bass.IndirectOffsetOnAxis(ap=G["slot"][0:R, t, k:k + 1], axis=0)).then_inc(s_e[t % 2], 16)

        @block.scalar
        def _(act):
            for t, R in tiles():
                act.wait_ge(s_r, t + 1)
                act.dma_start(token_rows(y_p, y_s, t), acc[t % 2][0:R, :]).then_inc(s_o[t % 2], 16)
            act.wait_ge(s_o[0], 16 * 5)
            act.wait_ge(s_o[1], 16 * 4)

        @block.vector
        def _(dve):
            link = serial(dve, s_v)
            dve.wait_ge(s_m, 32)
            for t, R in tiles():
                a = acc[t % 2][0:R, :]
                dve.wait_ge(s_in[t % 2], 32 * (t // 2 + 1))
                dve.wait_ge(s_e[t % 2], 16 * TK * (t // 2 + 1))
                for k in range(TK):
                    link(dve.scalar_tensor_tensor(out=a, in0=E[t % 2][0:R, k, :], scalar=G["gate"][0:R, t, k:k + 1], in1=a,
                                                  op0=ALU.mult, op1=ALU.add))
                link(dve.tensor_tensor(a, a, gf[:, :] if t < NT else gfs[:, :], ALU.mult))
                dve.tensor_tensor(a, a, x1[t % 2][0:R, :], ALU.add).then_inc(s_r, 1)


_INS = ['x_prompt', 'x_sample', 'cache_mla_latent', 'cache_mla_krope', 'cache_dsa_k', 'cache_dsa_v', 'cache_idx_k',
        'page_table', 'c_prompt', 'c_sample', 'rel_bias', 'w_ada', 'b_ada', 'g_attn_norm', 'w_in', 'g_q_lora', 'w_q_up',
        'g_kv_lora', 'w_kv_up', 'g_mla_qn', 'g_mla_qr', 'g_mla_kn', 'g_mla_kr', 'g_dsa_q', 'g_dsa_k', 'w_out', 'g_ffn_norm',
        'w_router', 'b_router', 'w_e_gu', 'w_e_down', 'w_s_gu', 'w_s_down']
_OUTS = [(1, SEQ, D), (NS, 1, D), (1, 1, SEQ, KVL), (1, 1, SEQ, ROPE), (1, 1, SEQ, H, 64), (1, 1, SEQ, H, 64),
         (1, 1, SEQ, IDX), (1, NS, 1, KVL), (1, NS, 1, ROPE), (1, NS, 1, H, 64), (1, NS, 1, H, 64), (1, NS, 1, IDX)]
_SCRATCH = {"mod": (NC9, 6 * D), "p": (NTOK, D_IN), "wi": (NTOK, H), "vm": (NTOK, 512), "vd": (NTOK, 512), "qm": (NTOK, H * QK),
            "qd": (NTOK, 512), "qmT": (H, QK, NTOK), "kmT": (H, QK, NTOK), "tdT": (13, P, NTOK), "mixT": (D, NTOK), "x1": (NTOK, D),
            "h2": ((NT + 2) * P, D), "yblk": (SLOTS, D), "ysh": ((NT + 2) * P, D), "score": (SEQ, SEQ), "omix": (NTOK, D), "pad": (2, P),
            "dpos": (NS // 2, 32, 16), "drow": (NS // 2, 32, 16)}


def kernel(**inputs):
    import concourse.bacc as _bacc
    from concourse.bass_utils import run_bass_kernel_spmd as _run

    nc = _bacc.Bacc("TRN2", target_bir_lowering=False, num_devices=1)
    arrays, T = {}, {}

    def give(name, a):
        a = np.ascontiguousarray(a)
        arrays[f"in_{name}"] = a
        T[name] = nc.dram_tensor(f"in_{name}", a.shape, mybir.dt.from_np(a.dtype), kind="ExternalInput").ap()

    for name in _INS:
        give(name, inputs[name])
    give("const", CONST)
    give("rope", rope_table())
    for name, shape in _SCRATCH.items():
        T[name] = nc.dram_tensor(f"s_{name}", shape, F32).ap()
    T["slot_tok"] = nc.dram_tensor("s_slot_tok", (SLOTS, 1), I32).ap()
    for i, shape in enumerate(_OUTS):
        T[f"o{i}"] = nc.dram_tensor(f"out_{i}", shape, F32, kind="ExternalOutput").ap()
    build(nc, T)
    r = _run(nc, [arrays], core_ids=[0])
    return tuple(r.results[0][f"out_{i}"] for i in range(len(_OUTS)))
```

```python
import math
from contextlib import ExitStack

import numpy as np
import concourse.bass as bass
from concourse import mybir

F32 = mybir.dt.float32
I32 = mybir.dt.int32
U32 = mybir.dt.uint32
BF16 = mybir.dt.bfloat16
ALU = mybir.AluOpType
ACT = mybir.ActivationFunctionType
AX = mybir.AxisListType
RMAX = bass.bass_isa.ReduceOp.max

P = 128
D = 1024
KD = D // P
SEQ, NS, PAST, PAGE = 1024, 8, 8192, 128
NT = SEQ // P
NTOK = SEQ + NS
NPG = PAST // PAGE
EPS = 1e-6
H, NOPE, ROPE, VD = 8, 64, 32, 64
QK = NOPE + ROPE
QL, KVL, IDX = 256, 128, 64
MLA_SCALE = QK ** -0.5
DSA_SCALE = 64 ** -0.5
TOPK = 256
NB_REL = 32
NE, TK, NG, TKG, DE = 64, 6, 8, 4, 256
ROUTED_SCALE = 2.5
C_Q, C_KV, C_KR = 0, 256, 384
C_QD, C_KD, C_VD, C_QI, C_KI, C_WI = 416, 928, 1440, 1952, 2464, 2528
D_IN = 2536
NEG = -3.0e38
NC9 = NS + 1
NBLK = NE + (NTOK * TK - NE) // P
NBLK += NBLK % 2
SLOTS = NBLK * P
BIGM = 1.0e9


def t5_bucket(d):
    exact = NB_REL // 2
    if d < exact:
        return max(d, 0)
    return min(exact + int(math.log(d / exact) / math.log(128 / exact) * (NB_REL - exact) + 1e-9), NB_REL - 1)


def shape_constants():
    c = {}
    i, j = np.arange(P)[:, None], np.arange(P)[None, :]
    c["ident"] = (i == j)
    c["causal"] = np.where(j <= i, 0.0, NEG)
    c["before"] = (i < j)
    c["ones"] = np.ones((P, P))
    c["same_half"] = (i // 64 == j // 64)
    c["before_half"] = (i < j) & (i // 64 == j // 64)
    c["iota"] = np.arange(P)[None, :] + np.zeros((P, 1))
    c["part"] = i
    c["page_of"] = i % 64
    c["half32"] = 16.0 * (i // 64)
    c["half_neg"] = np.where(np.stack([i[:, 0] < 64, i[:, 0] >= 64], 1), 0.0, NEG)
    c["half_one"] = np.stack([i[:, 0] < 64, i[:, 0] >= 64], 1)
    c["fresh_neg"] = np.where(i % 64 == 63, 0.0, NEG)
    bucket = np.array([[t5_bucket(x - g - 127) for x in range(384)] for g in range(4)])
    c["rel_onehot"] = (bucket[:, None, :] == np.arange(NB_REL)[None, :, None]).reshape(P, 384)
    thr = [min(x for x in range(0, 200) if t5_bucket(x) >= k) for k in range(1, NB_REL)]
    c["rel_from"] = np.array(thr)[None, :] + np.zeros((P, 1))
    c["row8"] = np.where(i == NS, 1.0, 0.0) + np.zeros((1, P))
    hb = np.zeros((P, H, 64))
    for p in range(16):
        hb[p, p % 8] = 1.0
    c["own_head"] = hb.reshape(P, 512)
    es = np.zeros((P, NS, NS))
    for p in range(16):
        for s in range(NS):
            es[p, s, s] = p < 8
    c["to_row"] = es.reshape(P, NS * NS)
    ep = np.zeros((P, NS // 2, NS))
    for p in range(16):
        for s in range(NS // 2):
            ep[p, s, 2 * s + p // 8] = 1.0
    c["to_pair"] = ep.reshape(P, NS // 2 * NS)
    c["lower8"] = np.tile((np.arange(8)[None, :] < np.arange(8)[:, None]).reshape(1, 64), (P, 1))
    c["is_token"] = np.stack([np.ones(P)] * NT + [np.arange(P) < NS], 1)
    c = {k: np.asarray(v, np.float32) for k, v in c.items()}
    b = np.empty((P, 31), np.int32)
    b[:] = np.int32(1) << np.arange(30, -1, -1, dtype=np.int32)
    c["bits"] = b.view(np.float32)
    at, cols, n = {}, [], 0
    for k, v in c.items():
        at[k] = (n, v.shape[1])
        cols.append(v)
        n += v.shape[1]
    return at, np.ascontiguousarray(np.concatenate(cols, 1))


def rope_table():
    half = ROPE // 2
    inv = (np.float32(10000.0) ** (-np.arange(half, dtype=np.float32) / np.float32(half))).astype(np.float32)
    pos = np.concatenate([np.arange(SEQ), np.full(NS, PAST)]).astype(np.float32)
    a = (pos[:, None] * inv[None, :]).astype(np.float32)
    return np.concatenate([np.cos(a), np.sin(a)], 1).astype(np.float32)


CONST_AT, CONST = shape_constants()


def build(nc, T):
    root = ExitStack()
    with root:
        sem_cache = {}

        def sem(name):
            if name not in sem_cache:
                sem_cache[name] = nc.alloc_semaphore(name)
            return sem_cache[name]

        stage_name = [""]

        def alloc(ctx):
            def sb(name, shape, dt=F32):
                return ctx.enter_context(nc.sbuf_tensor(stage_name[0] + name, shape, dt))

            def ps(name, dt=F32):
                return ctx.enter_context(nc.psum_tensor(stage_name[0] + name, [P, 512], dt))
            return sb, ps

        sb, _ = alloc(root)
        K = sb("K", [P, CONST.shape[1]])
        G = {"K": K, "c": lambda k: K[:, CONST_AT[k][0]:CONST_AT[k][0] + CONST_AT[k][1]]}
        for n in ("Aa", "Ba", "Af", "Bf"):
            G[n] = sb(n, [P, KD, NC9])
        G["lg"] = sb("lg", [P, NT + 1, NE])
        G["gate"] = sb("gate", [P, NT + 1, TK])
        G["slot"] = sb("slot", [P, NT + 1, 8], I32)
        G["expert"] = sb("expert", [3, P], I32)
        G["nblk"] = sb("nblk", [1, 2], I32)
        G["list"] = sb("list", [P, NBLK], I32)
        G["pages"] = sb("pages", [P, NS // 2], I32)
        G["pagef"] = sb("pagef", [P, NS // 2])
        G["SD"] = sb("SD", [P, NS // 2, PAGE + 1])
        G["thr"] = sb("sthr", [P, NS // 2])
        for st in (stage_ada, stage_in, stage_index, stage_prompt, stage_sample, stage_out, stage_dispatch, stage_routed,
                   stage_combine):
            stage_name[0] = st.__name__[6:] + "_"
            with ExitStack() as ctx:
                st(nc, T, G, sem, *alloc(ctx))
            nc.clear_and_free_semaphores(list(sem_cache.values()))
            nc.all_engine_barrier()
            sem_cache.clear()


def serial(eng, s):
    n = [0]

    def link(ins):
        n[0] += 1
        ins.then_inc(s, 1)
        eng.wait_ge(s, n[0])
    return link


def stage_ada(nc, T, G, sem, sb, ps):
    K, c = G["K"], G["c"]
    NCH = 6 * D // 512
    cs = sb("cs", [NC9, D])
    sc = sb("sc", [NC9, D])
    cT = sb("cT", [P, KD, NC9])
    W = [sb(f"Wada{i}", [P, KD, 512]) for i in range(3)]
    mod = sb("mod", [NC9, 6 * D])
    badd = sb("badd", [NC9, 6 * D])
    gr = sb("gr", [2 * KD, P])
    gT = sb("gT", [P, 2 * KD])
    one = sb("one", [P, KD * NC9])
    pt, pg, pm = ps("pt"), ps("pg"), [ps("pm0"), ps("pm1")]
    s_k, s_c, s_w = sem("ada_const"), sem("ada_c"), [sem(f"ada_w{i}") for i in range(3)]
    s_sc, s_cT, s_cTs, s_mm, s_mod, s_out = (sem("ada_" + n) for n in ("silu", "cT", "cTs", "mm", "mod", "out"))
    s_tr, s_gt, s_v = sem("ada_tr"), sem("ada_gt"), sem("ada_v")
    with nc.Block() as block:
        @block.sync
        def _(sp):
            sp.dma_start(K[:, :], T["const"]).then_inc(s_k, 16)
            sp.dma_start(cs[0:NS, :], T["c_sample"]).then_inc(s_c, 16)
            sp.dma_start(cs[NS:NC9, :], T["c_prompt"]).then_inc(s_c, 16)
            sp.dma_start(gr[0:KD, :], T["g_attn_norm"][0].rearrange("(k p) -> k p", p=P)).then_inc(s_c, 16)
            sp.dma_start(gr[KD:2 * KD, :], T["g_ffn_norm"][0].rearrange("(k p) -> k p", p=P)).then_inc(s_c, 16)
            sp.dma_start(badd[:, :], T["b_ada"].to_broadcast([NC9, 6 * D])).then_inc(s_c, 16)
            for g in range(NCH):
                if g >= 3:
                    sp.wait_ge(s_mm, g - 2)
                sp.dma_start(W[g % 3][:, :, :], T["w_ada"][0, :, 512 * g:512 * g + 512]
                             .rearrange("(k p) n -> p k n", p=P)).then_inc(s_w[g % 3], 16)
            sp.wait_ge(s_mod, NCH)
            sp.dma_start(T["mod"], mod[:, :]).then_inc(s_out, 16)
            sp.wait_ge(s_out, 16)

        @block.scalar
        def _(act):
            act.wait_ge(s_c, 80)
            act.activation(sc[:, :], cs[:, :], ACT.Sigmoid).then_inc(s_sc, 1)

        @block.tensor
        def _(pe):
            pe.wait_ge(s_k, 16)
            pe.wait_ge(s_sc, 2)
            for k in range(KD):
                m = pe.transpose(pt[:, k * NC9:(k + 1) * NC9], sc[:, k * P:(k + 1) * P], c("ident")[0:NC9, 0:NC9])
            m.then_inc(s_cT, 1)
            pe.transpose(pg[:, 0:2 * KD], gr[:, :], c("ident")[0:2 * KD, 0:2 * KD]).then_inc(s_gt, 1)
            pe.wait_ge(s_cTs, 1)
            for g in range(NCH):
                pe.wait_ge(s_w[g % 3], 16 * (g // 3 + 1))
                if g >= 2:
                    pe.wait_ge(s_mod, g - 1)
                for k in range(KD):
                    m = pe.matmul(pm[g % 2][0:NC9, :], cT[:, k, :], W[g % 3][:, k, :], start=(k == 0), stop=(k == KD - 1))
                m.then_inc(s_mm, 1)
            pe.wait_ge(s_mod, NCH)
            pe.wait_ge(s_gt, 2)
            for j, part in enumerate((0, 1, 3, 4)):
                for k in range(KD):
                    a = part * D + k * P
                    m = pe.transpose(pg[:, (j * KD + k) * NC9:(j * KD + k + 1) * NC9], mod[:, a:a + P],
                                     c("ident")[0:NC9, 0:NC9])
            m.then_inc(s_tr, 1)

        @block.vector
        def _(dve):
            link = serial(dve, s_v)
            dve.wait_ge(s_sc, 1)
            dve.tensor_tensor(sc[:, :], sc[:, :], cs[:, :], ALU.mult).then_inc(s_sc, 1)
            link(dve.memset(one[:, :], 1.0))
            dve.wait_ge(s_cT, 1)
            dve.tensor_copy(cT[:, :, :].rearrange("p k n -> p (k n)"), pt[:, 0:KD * NC9]).then_inc(s_cTs, 1)
            dve.wait_ge(s_gt, 1)
            dve.tensor_copy(gT[:, :], pg[:, 0:2 * KD]).then_inc(s_gt, 1)
            for g in range(NCH):
                dve.wait_ge(s_mm, g + 1)
                dve.tensor_tensor(mod[:, 512 * g:512 * g + 512], pm[g % 2][0:NC9, :],
                                  badd[:, 512 * g:512 * g + 512], ALU.add).then_inc(s_mod, 1)
            dve.wait_ge(s_tr, 1)
            for j, (a, b) in enumerate((("Aa", "Ba"), ("Af", "Bf"))):
                n = KD * NC9
                link(dve.tensor_copy(G[b][:, :, :].rearrange("p k n -> p (k n)"), pg[:, 2 * j * n:(2 * j + 1) * n]))
                link(dve.tensor_tensor(G[a][:, :, :].rearrange("p k n -> p (k n)"),
                                       pg[:, (2 * j + 1) * n:(2 * j + 2) * n], one[:, :], ALU.add))
                link(dve.tensor_tensor(G[a][:, :, :], G[a][:, :, :],
                                       gT[:, j * KD:(j + 1) * KD].unsqueeze(2).to_broadcast([P, KD, NC9]), ALU.mult))


def tiles():
    return [(t, P if t < NT else NS) for t in range(NT + 1)]


def token_rows(prompt, sample, t):
    return prompt[t * P:(t + 1) * P, :] if t < NT else sample


def stage_in(nc, T, G, sem, sb, ps):
    c = G["c"]
    NTT = NT + 1
    R_ = [R for _, R in tiles()]
    Win = sb("Win", [P, KD, D_IN])
    x = sb("x", [P, D])
    xn = [sb(f"xn{i}", [P, D]) for i in range(2)]
    hT = [sb(f"hT{i}", [P, KD, P]) for i in range(2)]
    pr = [sb(f"pr{i}", [P, D_IN]) for i in range(3)]
    st, epst = sb("st", [P, 4, NTT]), sb("epst", [P, 1])
    Wq = sb("Wq", [P, 2, H * QK])
    Wkv = sb("Wkv", [P, H, NOPE + VD])
    gains = {n: sb("m_" + n, [P, w]) for n, w in (("g_q_lora", QL), ("g_kv_lora", KVL), ("g_mla_qn", NOPE), ("g_mla_qr", ROPE),
                                                  ("g_mla_kn", NOPE), ("g_mla_kr", ROPE), ("g_dsa_q", 64), ("g_dsa_k", 64))}
    cs = [sb(f"cs{i}", [P, ROPE]) for i in range(2)]
    ql, qlT, ckvT = sb("ql", [P, QL]), sb("qlT", [P, 2, P]), sb("ckvT", [P, P])
    ckv, krr, qkd, qm, km, vm, kir = ([sb(f"{n}{i}", sh) for i in range(2)] for n, sh in (
        ("ckv", [P, KVL]), ("krr", [P, ROPE]), ("qkd", [P, 1024]), ("qm", [P, H, QK]), ("km", [P, H, QK]), ("vm", [P, 512]),
        ("kir", [P, 2 * IDX])))
    tq = sb("tq", [P, 16, P])
    td = sb("td", [P, 13, P])
    sq = sb("sq", [P, 1024])
    r16 = sb("r16", [P, 3, 16])
    rt = sb("rt", [P, H, ROPE])
    pt = [ps("pt0"), ps("pt1")]
    pp = [ps("pp0"), ps("pp1")]
    pq, pk, pv = [ps("mq0"), ps("mq1")], ps("mk"), ps("mv")
    pA = pv
    cols = [(0, 512), (512, 1024), (1024, 1536), (1536, 2048), (2048, D_IN)]
    s_ss, s_rs, s_xn, s_t, s_h, s_p, s_e, s_eps, s_b, s_w2, s_v = (
        sem("in_" + n) for n in ("ss", "rstd", "xn", "t", "h", "p", "evac", "eps", "b", "weights", "v"))
    s_x, s_wc, s_cs = sem("in_x"), [sem(f"in_w{g}") for g in range(5)], [sem("in_cs0"), sem("in_cs1")]
    s_o, s_qT, s_ckT, s_q, s_root, s_rooted, s_rows, s_tT, s_te, s_rd, s_vc = (
        sem("mx_" + n) for n in ("o", "qT", "ckT", "q", "root", "rooted", "rows", "tT", "te", "stored", "vm"))
    NROOT = 7
    xp, xs = T["x_prompt"][0], T["x_sample"].rearrange("b s d -> (b s) d")
    with nc.Block() as block:
        @block.sync
        def _(sp):
            def load(t):
                if t >= NTT:
                    return
                if t:
                    sp.wait_ge(s_xn, t)
                sp.dma_start(x[0:R_[t], :], token_rows(xp, xs, t)).then_inc(s_x, 16)

            load(0)
            for g, (a, b) in enumerate(cols):
                sp.dma_start(Win[:, :, a:b], T["w_in"][0, :, a:b].rearrange("(k p) n -> p k n", p=P)).then_inc(s_wc[g], 16)
                if g == 0:
                    load(1)
            sp.dma_start(Wq[:, :, :], T["w_q_up"][0].rearrange("(k p) n -> p k n", p=P)).then_inc(s_w2, 16)
            sp.dma_start(Wkv[:, :, :], T["w_kv_up"][0].rearrange("p (h n) -> p h n", h=H)).then_inc(s_w2, 16)
            for n, g in gains.items():
                sp.dma_start(g[:, :], T[n].to_broadcast([P, g.shape[1]])).then_inc(s_w2, 16)
            for step in range(NTT + 2):
                load(step + 2)
                t = step
                if t < NTT:
                    if t >= 2:
                        sp.wait_ge(s_rows, t - 1)
                    sp.dma_start(cs[t % 2][0:R_[t], :], T["rope"][t * P:t * P + R_[t], :]).then_inc(s_cs[t % 2], 16)
                t = step - 2
                if t < 0:
                    continue
                R = R_[t]
                sp.wait_ge(s_rows, t + 1)
                sp.wait_ge(s_vc, t + 1)
                rs = slice(t * P, t * P + R)
                if t < NT:
                    outs = [T["o2"][0, 0, rs, :], T["o3"][0, 0, rs, :], T["o4"][0, 0, rs].rearrange("r h d -> r (h d)"),
                            T["o5"][0, 0, rs].rearrange("r h d -> r (h d)"), T["o6"][0, 0, rs, :]]
                else:
                    outs = [T["o7"].rearrange("l b s d -> (l b s) d"), T["o8"].rearrange("l b s d -> (l b s) d"),
                            T["o9"].rearrange("l b s h d -> (l b s) (h d)"), T["o10"].rearrange("l b s h d -> (l b s) (h d)"),
                            T["o11"].rearrange("l b s d -> (l b s) d")]
                p_, k = pr[t % 3], t % 2
                for o, src in zip(outs, (ckv[k][0:R, :], krr[k][0:R, :], qkd[k][0:R, 512:1024], p_[0:R, C_VD:C_VD + 512],
                                         p_[0:R, C_KI:C_KI + IDX])):
                    sp.dma_start(o, src).then_inc(s_o, 16)
                sp.dma_start(T["wi"][rs, :], p_[0:R, C_WI:C_WI + H]).then_inc(s_o, 16)
                sp.dma_start(T["vm"][rs, :], vm[k][0:R, :]).then_inc(s_o, 16)
                sp.dma_start(T["vd"][rs, :], p_[0:R, C_VD:C_VD + 512]).then_inc(s_o, 16)
                more = 11
                if t == NT:
                    sp.dma_start(T["qm"][rs, :], qm[k][0:R, :, :].rearrange("p h d -> p (h d)")).then_inc(s_o, 16)
                    sp.dma_start(T["qd"][rs, :], qkd[k][0:R, 0:512]).then_inc(s_o, 16)
                    sp.dma_start(T["p"][rs, :], p_[0:R, :]).then_inc(s_o, 16)
                    more = 14
                sp.wait_ge(s_te, 8 * t + 8)
                ts = slice(t * P, t * P + R)
                sp.dma_start(T["qmT"][:, :, ts].rearrange("h d s -> d h s"), tq[0:QK, 0:8, 0:R]).then_inc(s_o, 16)
                sp.dma_start(T["kmT"][:, :, ts].rearrange("h d s -> d h s"), tq[0:QK, 8:16, 0:R]).then_inc(s_o, 16)
                sp.dma_start(T["tdT"][:, :, ts].rearrange("h d s -> d h s"), td[:, :, 0:R]).then_inc(s_o, 16)
                sp.wait_ge(s_o, 16 * (11 * t + more))
                sp.sem_inc(s_rd, 1)

        @block.scalar
        def _(act):
            def norm_x(t):
                if t >= NTT:
                    return
                R = R_[t]
                act.wait_ge(s_x, 16 * (t + 1))
                if t >= 2:
                    act.wait_ge(s_t, t - 1)
                act.activation(xn[t % 2][0:R, :], x[0:R, :], ACT.Square, accum_out=st[0:R, 0, t:t + 1]).then_inc(s_ss, 1)
                act.wait_ge(s_ss, t + 1)
                act.activation(st[0:R, 1, t:t + 1], st[0:R, 0, t:t + 1], ACT.Sqrt, scale=1.0 / D, bias=epst[0:R, 0:1]).then_inc(s_rs, 1)
                act.wait_ge(s_rs, 2 * t + 2)
                act.activation(xn[t % 2][0:R, :], x[0:R, :], ACT.Copy, scale=st[0:R, 2, t:t + 1]).then_inc(s_xn, 1)

            def roots(t, which):
                for j in which:
                    w, cnt = ((QL, 1), (KVL, 1), (ROPE, 1), (64, 16), (64, 8), (32, 8), (64, 8))[j]
                    act.wait_ge(s_root, NROOT * t + j + 1)
                    act.activation(r16[0:R_[t], 1, 0:cnt], r16[0:R_[t], 0, 0:cnt], ACT.Sqrt, scale=1.0 / w,
                                   bias=epst[0:R_[t], 0:1]).then_inc(s_rooted, 1)

            def take(t, g):
                if t >= NTT:
                    return
                if t >= 3 and g == 0:
                    act.wait_ge(s_rd, t - 2)
                a, b = cols[g]
                act.wait_ge(s_p, 5 * t + g + 1)
                act.activation(pr[t % 3][0:R_[t], a:b], pp[(5 * t + g) % 2][0:R_[t], 0:b - a], ACT.Copy).then_inc(s_e, 1)

            act.wait_ge(s_eps, 1)
            norm_x(0)
            norm_x(1)
            for step in range(NTT + 2):
                norm_x(step + 2)
                t = step - 1
                if 0 <= t < NTT:
                    roots(t, (0, 1, 2))
                take(step, 0)
                t = step - 2
                if t >= 0:
                    if t:
                        act.wait_ge(s_rd, t)
                    for b in range(8):
                        act.wait_ge(s_tT, 8 * t + b + 1)
                        if b < 4:
                            act.activation(tq[0:QK, 4 * b:4 * b + 4, :], pt[b % 2][0:QK, :].rearrange("p (a q) -> p a q", a=4),
                                           ACT.Copy).then_inc(s_te, 1)
                        else:
                            m = 4 if b < 7 else 1
                            act.activation(td[:, 4 * (b - 4):4 * (b - 4) + m, :], pt[b % 2][:, 0:m * P].rearrange("p (a q) -> p a q", a=m),
                                           ACT.Copy).then_inc(s_te, 1)
                t = step - 1
                if 0 <= t < NTT:
                    roots(t, (3,))
                take(step, 1)
                if 0 <= t < NTT:
                    act.wait_ge(s_q, t + 1)
                    if t >= 2:
                        act.wait_ge(s_rd, t - 1)
                    act.activation(vm[t % 2][0:R_[t], :], pv[0:R_[t], :], ACT.Copy).then_inc(s_vc, 1)
                    roots(t, (4, 5))
                take(step, 2)
                if 0 <= t < NTT:
                    roots(t, (6,))
                take(step, 3)
                take(step, 4)

        @block.tensor
        def _(pe):
            def turn_h(t):
                if t >= NTT:
                    return
                R = R_[t]
                pe.wait_ge(s_xn, t + 1)
                if t >= 1:
                    pe.wait_ge(s_h, 8 * t)
                if t >= 4:
                    pe.wait_ge(s_te, 8 * (t - 3))
                for k in range(KD):
                    m = pe.transpose(pt[k // 4][:, (k % 4) * P:(k % 4) * P + R], xn[t % 2][0:R, k * P:(k + 1) * P],
                                     c("ident")[0:R, 0:R])
                m.then_inc(s_t, 1)

            def project(t, g):
                if t >= NTT:
                    return
                R, n = R_[t], 5 * t + g
                a, b = cols[g]
                if g == 0:
                    pe.wait_ge(s_h, 8 * (t + 1))
                if t == 0:
                    pe.wait_ge(s_wc[g], 16)
                if n >= 2:
                    pe.wait_ge(s_e, n - 1)
                for k in range(KD):
                    m = pe.matmul(pp[n % 2][0:R, 0:b - a], hT[t % 2][:, k, 0:R], Win[:, k, a:b], start=(k == 0), stop=(k == KD - 1))
                m.then_inc(s_p, 1)

            def turn_operands(t):
                if t < 0:
                    return
                R, k, p_ = R_[t], t % 2, pr[t % 3]
                pe.wait_ge(s_rows, t + 1)
                pe.wait_ge(s_h, 8 * min(t + 4, NTT))
                bank = [[qm[k][0:R, a, :] for a in range(4)], [qm[k][0:R, 4 + a, :] for a in range(4)],
                        [km[k][0:R, a, :] for a in range(4)], [km[k][0:R, 4 + a, :] for a in range(4)],
                        [qkd[k][0:R, a * P:(a + 1) * P] for a in range(4)], [qkd[k][0:R, (4 + a) * P:(5 + a) * P] for a in range(4)],
                        [p_[0:R, C_QI + a * P:C_QI + (a + 1) * P] for a in range(4)], [kir[k][0:R, :]]]
                for b, srcs in enumerate(bank):
                    if 8 * t + b >= 2:
                        pe.wait_ge(s_te, 8 * t + b - 1)
                    for a, src in enumerate(srcs):
                        m = pe.transpose(pt[b % 2][0:src.shape[1], a * P:a * P + R], src, c("ident")[0:R, 0:R])
                    m.then_inc(s_tT, 1)

            def low_rank_turn(t):
                if not 0 <= t < NTT:
                    return
                R = R_[t]
                I = c("ident")[0:R, 0:R]
                if t >= 1:
                    pe.wait_ge(s_vc, t)
                pe.wait_ge(s_qT, 4 * t + 2)
                for k in range(2):
                    pe.transpose(pA[:, k * P:k * P + R], ql[0:R, k * P:(k + 1) * P], I)
                pe.transpose(pA[:, 256:256 + R], ckv[t % 2][0:R, :], I).then_inc(s_ckT, 1)

            def low_rank(t):
                if not 0 <= t < NTT:
                    return
                R = R_[t]
                if t == 0:
                    pe.wait_ge(s_w2, 160)
                if t >= 1:
                    pe.wait_ge(s_rows, t)
                pe.wait_ge(s_qT, 4 * t + 4)
                for n in range(2):
                    for k in range(2):
                        pe.matmul(pq[n][0:R, 0:384], qlT[:, k, 0:R], Wq[:, k, 384 * n:384 * n + 384], start=(k == 0), stop=(k == 1))
                pe.matmul(pk[0:R, :], ckvT[:, 0:R], Wkv[:, :, 0:NOPE], start=True, stop=True)
                pe.matmul(pv[0:R, :], ckvT[:, 0:R], Wkv[:, :, NOPE:], start=True, stop=True).then_inc(s_q, 1)

            turn_h(0)
            for step in range(NTT + 2):
                turn_h(step + 1)
                project(step, 0)
                low_rank_turn(step - 1)
                turn_operands(step - 2)
                project(step, 1)
                low_rank(step - 1)
                project(step, 2)
                project(step, 3)
                project(step, 4)

        @block.vector
        def _(dve):
            done = [0]

            def go(ins):
                done[0] += 1
                ins.then_inc(s_v, 1)

            def link(ins):
                go(ins)
                dve.wait_ge(s_v, done[0])

            n = [0]

            def norm(parts, src, cnt, w, R):
                s3 = sq[0:R, 0:cnt * w].rearrange("p (c w) -> p c w", c=cnt)
                link(dve.tensor_tensor(s3, src, src, ALU.mult))
                dve.tensor_reduce(r16[0:R, 0, 0:cnt], s3, AX.X, ALU.add).then_inc(s_root, 1)
                n[0] += 1
                dve.wait_ge(s_rooted, n[0])
                link(dve.reciprocal(r16[0:R, 2, 0:cnt], r16[0:R, 1, 0:cnt]))
                link(dve.tensor_tensor(s3, src, r16[0:R, 2, 0:cnt].unsqueeze(2).to_broadcast([R, cnt, w]), ALU.mult))
                for dst, sl, gain in parts:
                    k = sl.stop - sl.start
                    go(dve.tensor_tensor(dst, s3[:, sl, :], gains[gain][0:R, :].unsqueeze(1).to_broadcast([R, k, w]), ALU.mult))
                dve.wait_ge(s_v, done[0])

            def rotate(dst, src, cnt, R, table):
                co = table[0:R, 0:16].unsqueeze(1).to_broadcast([R, cnt, 16])
                si = table[0:R, 16:32].unsqueeze(1).to_broadcast([R, cnt, 16])
                part = [sq[0:R, 256 * i:256 * i + cnt * 16].rearrange("p (c w) -> p c w", c=cnt) for i in range(4)]
                go(dve.tensor_tensor(part[0], src[:, :, 0:16], co, ALU.mult))
                go(dve.tensor_tensor(part[1], src[:, :, 16:32], si, ALU.mult))
                go(dve.tensor_tensor(part[2], src[:, :, 16:32], co, ALU.mult))
                link(dve.tensor_tensor(part[3], src[:, :, 0:16], si, ALU.mult))
                go(dve.tensor_tensor(dst[:, :, 0:16], part[0], part[1], ALU.subtract))
                link(dve.tensor_tensor(dst[:, :, 16:32], part[2], part[3], ALU.add))

            def root_x(t):
                if t < NTT:
                    dve.wait_ge(s_rs, 2 * t + 1)
                    dve.reciprocal(st[0:R_[t], 2, t:t + 1], st[0:R_[t], 1, t:t + 1]).then_inc(s_rs, 1)

            def scale_h(t):
                if t >= NTT:
                    return
                dve.wait_ge(s_t, t + 1)
                if t >= 2:
                    dve.wait_ge(s_p, 5 * (t - 1))
                for k in range(KD):
                    src = pt[k // 4][:, (k % 4) * P:(k % 4) * P + R_[t]]
                    if t < NT:
                        dve.tensor_scalar(hT[t % 2][:, k, :], src, G["Aa"][:, k, NS:NC9], G["Ba"][:, k, NS:NC9],
                                          ALU.mult, ALU.add).then_inc(s_h, 1)
                    else:
                        dve.tensor_tensor(hT[t % 2][:, k, 0:NS], src, G["Aa"][:, k, 0:NS], ALU.mult).then_inc(s_b, 1)
                        dve.wait_ge(s_b, k + 1)
                        dve.tensor_tensor(hT[t % 2][:, k, 0:NS], hT[t % 2][:, k, 0:NS], G["Ba"][:, k, 0:NS],
                                          ALU.add).then_inc(s_h, 1)

            def mix(t):
                R, k, p_ = R_[t], t % 2, pr[t % 3]
                if t == 0:
                    dve.wait_ge(s_w2, 160)
                if t >= 2:
                    dve.wait_ge(s_rd, t - 1)
                u = lambda ap: ap.unsqueeze(1)
                v3 = lambda ap: ap.rearrange("p (h d) -> p h d", d=64)
                one = slice(0, 1)
                dve.wait_ge(s_e, 5 * t + 1)
                norm([(u(ql[0:R, :]), one, "g_q_lora")], u(p_[0:R, C_Q:C_Q + QL]), 1, QL, R)
                dve.sem_inc(s_qT, 1)
                norm([(u(ckv[k][0:R, :]), one, "g_kv_lora")], u(p_[0:R, C_KV:C_KV + KVL]), 1, KVL, R)
                dve.sem_inc(s_qT, 1)
                norm([(u(rt[0:R, 0, :]), one, "g_mla_kr")], u(p_[0:R, C_KR:C_KR + ROPE]), 1, ROPE, R)
                dve.wait_ge(s_cs[k], 16 * (t // 2 + 1))
                rotate(u(krr[k][0:R, :]), u(rt[0:R, 0, :]), 1, R, cs[k])
                dve.wait_ge(s_ckT, t + 1)
                go(dve.tensor_copy(qlT[:, :, 0:R], pA[:, 0:256].rearrange("p (k r) -> p k r", k=2)[:, :, 0:R]))
                link(dve.tensor_copy(ckvT[:, 0:R], pA[:, 256:256 + R]))
                dve.sem_inc(s_qT, 2)
                dve.wait_ge(s_e, 5 * t + 5)
                norm([(v3(qkd[k][0:R, 0:512]), slice(0, 8), "g_dsa_q"), (v3(qkd[k][0:R, 512:1024]), slice(8, 16), "g_dsa_k")],
                     v3(p_[0:R, C_QD:C_QD + 1024]), 16, 64, R)
                for a in range(2):
                    go(dve.tensor_copy(kir[k][0:R, a * IDX:(a + 1) * IDX], p_[0:R, C_KI:C_KI + IDX]))
                dve.wait_ge(s_q, t + 1)
                for a in range(2):
                    go(dve.tensor_copy(qm[k][0:R, 4 * a:4 * a + 4, :], pq[a][0:R, 0:384].rearrange("p (h d) -> p h d", h=4)))
                link(dve.tensor_copy(km[k][0:R, :, 0:NOPE], v3(pk[0:R, :])))
                norm([(qm[k][0:R, :, 0:NOPE], slice(0, 8), "g_mla_qn")], qm[k][0:R, :, 0:NOPE], 8, 64, R)
                norm([(rt[0:R, :, :], slice(0, 8), "g_mla_qr")], qm[k][0:R, :, NOPE:QK], 8, 32, R)
                rotate(qm[k][0:R, :, NOPE:QK], rt[0:R, :, :], 8, R, cs[k])
                norm([(km[k][0:R, :, 0:NOPE], slice(0, 8), "g_mla_kn")], km[k][0:R, :, 0:NOPE], 8, 64, R)
                link(dve.tensor_copy(km[k][0:R, :, NOPE:QK], u(krr[k][0:R, :]).to_broadcast([R, H, ROPE])))
                dve.sem_inc(s_rows, 1)

            dve.memset(epst[:, :], EPS).then_inc(s_eps, 1)
            root_x(0)
            root_x(1)
            scale_h(0)
            for step in range(NTT + 1):
                root_x(step + 2)
                scale_h(step + 1)
                if step:
                    mix(step - 1)


def stage_prompt(nc, T, G, sem, sb, ps):
    c = G["c"]
    FIRST = TOPK // P
    widths = [(i + 1) * P for i in range(NT)]
    at = [sum(widths[FIRST:i]) for i in range(NT)]
    kiT = sb("kiT", [P, SEQ])
    U = sb("U", [P, sum(widths[FIRST:])])
    bias = sb("bias", [P, H, 2 * P])
    kmT = sb("kmTs", [P, H, SEQ])
    kdT = sb("kdTs", [P, 4, SEQ])
    V = [sb("vmS", [P, NT, 512]), sb("vdS", [P, NT, 512])]
    sel_phase = ExitStack()
    with sel_phase as ctx:
        def sb1(name, shape, dt=F32):
            return ctx.enter_context(nc.sbuf_tensor(name, shape, dt))

        def ps1(name):
            return ctx.enter_context(nc.psum_tensor(name, [P, 512], F32))
        index_and_select(nc, T, G, sem, sb1, ps1, kiT, U, bias, FIRST, widths, at, kmT, kdT, V)
    with ExitStack() as ctx:
        def sb2(name, shape, dt=F32):
            return ctx.enter_context(nc.sbuf_tensor(name, shape, dt))

        def ps2(name):
            return ctx.enter_context(nc.psum_tensor(name, [P, 512], F32))
        attend(nc, T, G, sem, sb2, ps2, U, bias, FIRST, widths, at, kmT, kdT, V)


def index_and_select(nc, T, G, sem, sb, ps, kiT, U, bias, FIRST, widths, at, kmT, kdT, V):
    c = G["c"]
    NSEL = NT - FIRST
    qi = [sb(f"qi{i}", [P, 4, P]) for i in range(2)]
    wi = sb("wiall", [P, NSEL, H])
    rl = [sb(f"rl{i}", [P, SEQ]) for i in range(2)]
    junk = sb("sjunk", [P, U.shape[1]], BF16)
    eq, rank = sb("eq", [P, SEQ]), sb("rank", [P, SEQ])
    ones = sb("onesrow", [P, SEQ])
    SD, NP2, NSL = G["SD"], NS // 2, PAGE + 1
    NC = NSEL + NP2
    cand, best, keep = (sb(n, [P, NC], I32) for n in ("cand", "best", "keep"))
    cnt, goal, pos, sgn, ncol, thr = (sb(n, [P, NC]) for n in ("cnt", "goal", "pos", "sgn", "ncol", "thr"))
    sjunk = sb("sdjunk", [P, NP2, NSL], BF16)
    rb, rb31 = sb("rb", [P, 4, H]), sb("rb31", [P, 4, H])
    pS = [[ps(f"iS{a}{b}") for b in range(2)] for a in range(2)]
    pB = [ps(f"iB{a}") for a in range(4)]
    pC = pS[0][0]
    s_k, s_wi, s_q, s_s, s_r, s_a, s_v, s_b, s_bd = (sem("ix_" + n) for n in ("k", "wi", "q", "s", "relu", "acc", "v", "bias", "biasd"))
    s_kv, s_rz, s_bit, s_c, s_p, s_bp = sem("ix_kv"), sem("ix_rz"), sem("ix_bit"), sem("ix_c"), sem("ix_p"), sem("ix_bp")
    per = NC + 5
    with nc.Block() as block:
        @block.sync
        def _(sp):
            sp.dma_start(kiT[:, :], T["tdT"][12, :, 0:SEQ]).then_inc(s_k, 16)
            sp.dma_start(wi[:, :, :], T["wi"][FIRST * P:SEQ, :].rearrange("(t p) h -> p t h", p=P)).then_inc(s_wi, 16)
            sp.wait_ge(s_rz, 2)
            for g in range(4):
                r = slice(NB_REL * g, NB_REL * (g + 1))
                sp.dma_start(rb[r, g, :], T["rel_bias"]).then_inc(s_wi, 16)
                sp.dma_start(rb31[r, g, :], T["rel_bias"][NB_REL - 1:NB_REL, :].to_broadcast([NB_REL, H])).then_inc(s_wi, 16)
            for j in range(NSEL):
                i = FIRST + j
                if j >= 2:
                    sp.wait_ge(s_s, 8 * (j - 1))
                sp.wait_ge(s_q, 16 * j)
                sp.dma_start(qi[j % 2][:, :, :], T["tdT"][8:12, :, i * P:(i + 1) * P].rearrange("h d s -> d h s")).then_inc(s_q, 16)
            sp.dma_start(kmT[0:QK, :, :], T["kmT"][:, :, 0:SEQ].rearrange("h d s -> d h s")).then_inc(s_kv, 16)
            sp.dma_start(kdT[:, :, :], T["tdT"][4:8, :, 0:SEQ].rearrange("h d s -> d h s")).then_inc(s_kv, 16)
            for g, name in enumerate(("vm", "vd")):
                sp.dma_start(V[g][:, :, :], T[name][0:SEQ, :].rearrange("(t p) d -> p t d", p=P)).then_inc(s_kv, 16)
            sp.wait_ge(s_kv, 64)

        @block.tensor
        def _(pe):
            pe.wait_ge(s_k, 16)
            pe.wait_ge(s_bd, 1)
            n = 0
            EACH = -(-2 * P // 4 // (NSEL * H))
            for j in range(NSEL):
                pe.wait_ge(s_q, 16 * (j + 1))
                for h in range(H):
                    for m in range(n * EACH, min((n + 1) * EACH, 2 * P // 4)):
                        k = 4 * m
                        mm = pe.matmul(pB[k // 64][:, (k % 64) * H:(k % 64 + 4) * H], c("rel_onehot")[:, 255 - k:255 - k + P],
                                       rb[:, :, :].rearrange("p a h -> p (a h)"), start=True, stop=True)
                        if k == 2 * P - 4:
                            mm.then_inc(s_b, 1)
                    b = 64 * (h % 2)
                    if n >= 2:
                        pe.wait_ge(s_r, n - 1)
                    w = widths[FIRST + j]
                    for z in range(0, w, 512):
                        m = pe.matmul(pS[n % 2][z // 512][:, 0:min(512, w - z)], qi[j % 2][b:b + 64, h // 2, :],
                                      kiT[b:b + 64, z:min(z + 512, w)], start=True, stop=True)
                    m.then_inc(s_s, 1)
                    n += 1
            pe.wait_ge(s_c, 1)
            pe.matmul(pC[:, 0:NP2], c("same_half"), cnt[:, NSEL:NC], start=True, stop=True).then_inc(s_p, 1)
            with pe.Fori(0, 31) as k:
                pe.wait_ge(s_bit, k * per + 2 + NP2)
                pe.matmul(pC[:, 0:NP2], c("same_half"), cnt[:, NSEL:NC], start=True, stop=True).then_inc(s_bp, 1)

        @block.scalar
        def _(act):
            n = 0
            for j in range(NSEL):
                for h in range(H):
                    w = widths[FIRST + j]
                    act.wait_ge(s_s, n + 1)
                    if n >= 2:
                        act.wait_ge(s_a, n - 1)
                    for z in range(0, w, 512):
                        a = act.activation(rl[n % 2][:, z:min(z + 512, w)], pS[n % 2][z // 512][:, 0:min(512, w - z)],
                                           ACT.Relu, scale=IDX ** -0.5)
                    a.then_inc(s_r, 1)
                    n += 1

        @block.vector
        def _(dve):
            link = serial(dve, s_v)
            dve.memset(rb[:, :, :], 0.0).then_inc(s_rz, 1)
            dve.memset(rb31[:, :, :], 0.0).then_inc(s_rz, 1)
            dve.wait_ge(s_wi, 144)
            link(dve.tensor_scalar(wi[:, :, :], wi[:, :, :], H ** -0.5, None, ALU.mult))
            link(dve.tensor_tensor(rb[:, :, :], rb[:, :, :], rb31[:, :, :], ALU.subtract))
            dve.tensor_scalar(rb[:, :, :], rb[:, :, :], 1.0 / DSA_SCALE, None, ALU.mult).then_inc(s_bd, 1)
            n = 0
            for j in range(NSEL):
                w = widths[FIRST + j]
                u = U[:, at[FIRST + j]:at[FIRST + j] + w]
                for h in range(H):
                    dve.wait_ge(s_r, n + 1)
                    if n:
                        dve.wait_ge(s_a, n)
                    if h == 0:
                        dve.tensor_scalar(u, rl[n % 2][:, 0:w], wi[:, j, h:h + 1], None, ALU.mult).then_inc(s_a, 1)
                    else:
                        dve.scalar_tensor_tensor(out=u, in0=rl[n % 2][:, 0:w], scalar=wi[:, j, h:h + 1], in1=u,
                                                 op0=ALU.mult, op1=ALU.add).then_inc(s_a, 1)
                    n += 1
            dve.wait_ge(s_a, n)
            tiles_ = [(j, widths[FIRST + j], at[FIRST + j]) for j in range(NSEL)]
            for j, w, a in tiles_:
                link(dve.tensor_tensor(U[:, a + w - P:a + w], U[:, a + w - P:a + w], c("causal"), ALU.add))
                link(dve.memset(ncol[:, j:j + 1], float(w - TOPK + 1)))
            link(dve.memset(ncol[:, NSEL:NC], float(64 * NSL - TOPK + 1)))
            link(dve.memset(best[:, :], 0))
            link(dve.memset(ones[:, :], 1.0))
            for pr in range(NP2):
                link(dve.tensor_scalar(sjunk[:, pr, :], SD[:, pr, :], 0.0, 0.0, ALU.is_ge, ALU.add, accum_out=cnt[:, NSEL + pr:NSEL + pr + 1]))
            dve.sem_inc(s_c, 1)
            for j, w, a in tiles_:
                link(dve.tensor_scalar(junk[:, a:a + w], U[:, a:a + w], 0.0, 0.0, ALU.is_ge, ALU.add, accum_out=cnt[:, j:j + 1]))
            dve.wait_ge(s_p, 1)
            link(dve.tensor_copy(cnt[:, NSEL:NC], pC[:, 0:NP2]))
            link(dve.tensor_scalar(pos[:, :], cnt[:, :], float(TOPK), None, ALU.is_ge))
            link(dve.tensor_scalar(sgn[:, :], pos[:, :], 2.0, -1.0, ALU.mult, ALU.add))
            link(dve.tensor_scalar(goal[:, :], ncol[:, :], -1.0, float(TOPK), ALU.mult, ALU.add))
            link(dve.tensor_tensor(goal[:, :], goal[:, :], pos[:, :], ALU.mult))
            link(dve.tensor_tensor(goal[:, :], goal[:, :], ncol[:, :], ALU.add))
            for j, w, a in tiles_:
                link(dve.tensor_scalar(U[:, a:a + w], U[:, a:a + w], sgn[:, j:j + 1], None, ALU.mult))
            for pr in range(NP2):
                link(dve.tensor_scalar(SD[:, pr, :], SD[:, pr, :], sgn[:, NSEL + pr:NSEL + pr + 1], None, ALU.mult))
            link(dve.tensor_scalar(goal[:, :], goal[:, :], -1.0, None, ALU.add))
            bits = c("bits").bitcast(I32)
            dve.sem_inc(s_bit, 1)
            with dve.Fori(0, 31) as k:
                dve.wait_ge(s_bit, k * per + 1)
                dve.tensor_tensor(cand[:, :], best[:, :], bits[:, bass.ds(k, 1)].to_broadcast([P, NC]),
                                  ALU.bitwise_or).then_inc(s_bit, 1)
                dve.wait_ge(s_bit, k * per + 2)
                for pr in range(NP2):
                    dve.tensor_scalar(sjunk[:, pr, :], SD[:, pr, :], cand[:, NSEL + pr:NSEL + pr + 1].bitcast(F32), 0.0, ALU.is_ge, ALU.add,
                                      accum_out=cnt[:, NSEL + pr:NSEL + pr + 1]).then_inc(s_bit, 1)
                for j, w, a in tiles_:
                    dve.tensor_scalar(junk[:, a:a + w], U[:, a:a + w], cand[:, j:j + 1].bitcast(F32), 0.0, ALU.is_ge, ALU.add,
                                      accum_out=cnt[:, j:j + 1]).then_inc(s_bit, 1)
                dve.wait_ge(s_bp, k + 1)
                dve.tensor_tensor(keep[:, NSEL:NC], goal[:, NSEL:NC], pC[:, 0:NP2], ALU.subtract).then_inc(s_bit, 1)
                dve.wait_ge(s_bit, k * per + 2 + NC)
                dve.tensor_tensor(keep[:, 0:NSEL], goal[:, 0:NSEL], cnt[:, 0:NSEL], ALU.subtract).then_inc(s_bit, 1)
                dve.wait_ge(s_bit, k * per + 4 + NC)
                dve.tensor_scalar(keep[:, :], keep[:, :], 31, bits[:, bass.ds(k, 1)], ALU.arith_shift_right,
                                  ALU.bitwise_and).then_inc(s_bit, 1)
                dve.wait_ge(s_bit, k * per + 5 + NC)
                dve.tensor_tensor(best[:, :], best[:, :], keep[:, :], ALU.bitwise_or).then_inc(s_bit, 1)
            dve.wait_ge(s_bit, 31 * per + 1)
            link(dve.tensor_tensor(thr[:, :], best[:, :].bitcast(F32), sgn[:, :], ALU.mult))
            link(dve.tensor_copy(G["thr"][:, :], thr[:, NSEL:NC]))
            for pr in range(NP2):
                link(dve.tensor_scalar(SD[:, pr, :], SD[:, pr, :], sgn[:, NSEL + pr:NSEL + pr + 1], None, ALU.mult))
            for j, w, a in tiles_:
                u = U[:, a:a + w]
                link(dve.tensor_scalar(u, u, sgn[:, j:j + 1], None, ALU.mult))
                link(dve.tensor_scalar(junk[:, a:a + w], u, thr[:, j:j + 1], 0.0, ALU.is_gt, ALU.add, accum_out=cnt[:, j:j + 1]))
                link(dve.tensor_scalar(cnt[:, j:j + 1], cnt[:, j:j + 1], -1.0, float(TOPK), ALU.mult, ALU.add))
                link(dve.tensor_scalar(eq[:, 0:w], u, thr[:, j:j + 1], None, ALU.is_equal))
                link(dve.tensor_tensor_scan(rank[:, 0:w], ones[:, 0:w], eq[:, 0:w], 0.0, ALU.mult, ALU.add))
                link(dve.scalar_tensor_tensor(out=eq[:, 0:w], in0=rank[:, 0:w], scalar=cnt[:, j:j + 1], in1=eq[:, 0:w],
                                              op0=ALU.is_le, op1=ALU.mult))
                link(dve.scalar_tensor_tensor(out=u, in0=u, scalar=thr[:, j:j + 1], in1=eq[:, 0:w], op0=ALU.is_gt, op1=ALU.add))
                link(dve.tensor_scalar(u, u, -NEG, NEG, ALU.mult, ALU.add))
            dve.wait_ge(s_b, 1)
            for g in range(4):
                link(dve.tensor_copy(bias[:, :, 64 * g:64 * g + 64], pB[g][:, :].rearrange("p (k h) -> p h k", h=H)))


def attend(nc, T, G, sem, sb, ps, U, bias, FIRST, widths, at, kmT, kdT, V):
    c = G["c"]
    qm = [sb(f"qmt{i}", [P, H, P]) for i in range(2)]
    qd = [sb(f"qdt{i}", [P, 4, P]) for i in range(2)]
    open_row = sb("open_row", [P, SEQ])
    mb = [sb(f"mb{i}", [P, H, 2 * P]) for i in range(2)]
    S = [sb(f"S{i}", [P, SEQ]) for i in range(2)]
    Pr = [sb(f"Pr{i}", [P, SEQ]) for i in range(2)]
    PT = [sb(f"PT{i}", [P, NT, P]) for i in range(2)]
    O = [sb(f"O{i}", [P, D]) for i in range(2)]
    mx = sb("mx", [P, 4, 2])
    rs = sb("rs", [P, 2])
    mxp = sb("mxp", [P, 2, 4])
    pS = [[ps(f"aS{a}{b}") for b in range(2)] for a in range(2)]
    pT = [ps("aT0"), ps("aT1")]
    pO = [ps("aO0"), ps("aO1")]
    names = ("S", "nm", "P", "T", "evd", "eva", "O", "on", "row", "mb", "st", "mx")
    s_S, s_nm, s_P, s_T, s_evd, s_eva, s_O, s_on, s_row, s_mb, s_st, s_mx = (sem("at_" + n) for n in names)
    s_q, s_out = [sem("at_q0"), sem("at_q1")], [sem("at_o0"), sem("at_o1")]
    items = [(i, g, h) for i in range(NT) for g in range(2) for h in range(H)]
    groups, gfirst = [], []
    for n, (i, g, h) in enumerate(items):
        gfirst.append(len(groups))
        groups += [(n, b, min(4, i + 1 - b)) for b in range(0, i + 1, 4)]
    gfirst.append(len(groups))

    def by_dve(upto):
        return (upto + 1) // 2

    with nc.Block() as block:
        @block.sync
        def _(sp):
            def store(i):
                sp.wait_ge(s_on, 16 * (i + 1))
                sp.dma_start(T["omix"][i * P:(i + 1) * P, :], O[i % 2][:, :]).then_inc(s_out[i % 2], 16)

            for i in range(NT):
                if i >= 2:
                    sp.wait_ge(s_S, 16 * (i - 1))
                sl = slice(i * P, (i + 1) * P)
                sp.dma_start(qm[i % 2][0:QK, :, :], T["qmT"][:, :, sl].rearrange("h d s -> d h s")).then_inc(s_q[i % 2], 16)
                sp.dma_start(qd[i % 2][:, :, :], T["tdT"][0:4, :, sl].rearrange("h d s -> d h s")).then_inc(s_q[i % 2], 16)
                if i >= 2:
                    store(i - 2)
            store(NT - 2)
            store(NT - 1)
            for s in s_out:
                sp.wait_ge(s, 16 * NT // 2)

        @block.gpsimd
        def _(pool):
            pool.memset(open_row[:, 0:SEQ - P], 0.0).then_inc(s_row, 1)
            pool.tensor_copy(open_row[:, SEQ - P:SEQ], c("causal")).then_inc(s_row, 1)
            pool.wait_ge(s_row, 2)
            for i in range(NT):
                if i >= 2:
                    pool.wait_ge(s_nm, 16 * (i - 1))
                w = min(2 * P, widths[i])
                m = U[:, at[i] + widths[i] - w:at[i] + widths[i]] if i >= FIRST else open_row[:, SEQ - w:SEQ]
                pool.tensor_tensor(mb[i % 2][:, :, 2 * P - w:2 * P], bias[:, :, 2 * P - w:2 * P],
                                   m.unsqueeze(1).to_broadcast([P, H, w]), ALU.add).then_inc(s_mb, 1)

        @block.tensor
        def _(pe):
            def scores(n):
                i, g, h = items[n]
                if g == 0 and h == 0:
                    pe.wait_ge(s_q[i % 2], 32 * (i // 2 + 1))
                if n >= 2:
                    pe.wait_ge(s_nm, n - 1)
                w = widths[i]
                b = 64 * (h % 2)
                q = qm[i % 2][0:QK, h, :] if g == 0 else qd[i % 2][b:b + 64, h // 2, :]
                for z in range(0, w, 512):
                    e = min(z + 512, w)
                    k = kmT[0:QK, h, z:e] if g == 0 else kdT[b:b + 64, h // 2, z:e]
                    m = pe.matmul(pS[n % 2][z // 512][:, 0:e - z], q, k, start=True, stop=True)
                m.then_inc(s_S, 1)

            def turn(n):
                pe.wait_ge(s_P, n + 1)
                for gi in range(gfirst[n], gfirst[n + 1]):
                    _, b0, cnt = groups[gi]
                    if gi >= 2:
                        pe.wait_ge(s_evd if gi % 2 == 0 else s_eva, gi // 2)
                    for b in range(cnt):
                        m = pe.transpose(pT[gi % 2][:, b * P:(b + 1) * P], Pr[n % 2][:, (b0 + b) * P:(b0 + b + 1) * P], c("ident"))
                    m.then_inc(s_T, 1)

            def pv(n):
                i, g, h = items[n]
                pe.wait_ge(s_evd, by_dve(gfirst[n + 1]))
                if gfirst[n + 1] >= 2:
                    pe.wait_ge(s_eva, gfirst[n + 1] // 2)
                if n >= 2:
                    pe.wait_ge(s_on, n - 1)
                for j in range(i + 1):
                    m = pe.matmul(pO[n % 2][:, 0:64], PT[n % 2][:, j, :], V[g][:, j, h * 64:h * 64 + 64], start=(j == 0), stop=(j == i))
                m.then_inc(s_O, 1)

            scores(0)
            for n in range(len(items)):
                if n + 1 < len(items):
                    scores(n + 1)
                turn(n)
                if n:
                    pv(n - 1)
            pv(len(items) - 1)

        def evac(eng, n, odd):
            for gi in range(gfirst[n], gfirst[n + 1]):
                if gi % 2 == odd:
                    _, b0, cnt = groups[gi]
                    eng.wait_ge(s_T, gi + 1)
                    if n >= 2:
                        eng.wait_ge(s_O, n - 1)
                    dst = PT[n % 2][:, b0:b0 + cnt, :].rearrange("p a q -> p (a q)")
                    if odd:
                        eng.activation(dst, pT[1][:, 0:cnt * P], ACT.Copy).then_inc(s_eva, 1)
                    else:
                        eng.tensor_copy(dst, pT[0][:, 0:cnt * P]).then_inc(s_evd, 1)

        @block.scalar
        def _(act):
            def exps(n):
                w = widths[items[n][0]]
                act.wait_ge(s_nm, n + 1)
                if n >= 2:
                    act.wait_ge(s_T, gfirst[n - 1])
                if n >= 4:
                    act.wait_ge(s_on, n - 3)
                act.activation(Pr[n % 2][:, 0:w], S[n % 2][:, 0:w], ACT.Exp, bias=mx[:, n % 4, 0:1],
                               accum_out=mx[:, n % 4, 1:2]).then_inc(s_P, 1)
            exps(0)
            for n in range(len(items)):
                if n + 1 < len(items):
                    exps(n + 1)
                evac(act, n, 1)

        @block.vector
        def _(dve):
            dve.wait_ge(s_row, 2)
            nmx = [0]

            def scale_and_max(n):
                i, g, h = items[n]
                w, k = widths[i], n % 2
                dve.wait_ge(s_S, n + 1)
                if n >= 2:
                    dve.wait_ge(s_P, n - 1)
                near = min(w, 2 * P) if g else 0
                parts = []
                cuts = sorted({0, w} | {x for x in (512, w - near) if 0 < x < w})
                parts = list(zip(cuts, cuts[1:]))
                for a, (z, e) in enumerate(parts):
                    if g == 0:
                        m = open_row[:, SEQ - w + z:SEQ - w + e]
                    elif z >= w - near:
                        dve.wait_ge(s_mb, i + 1)
                        m = mb[i % 2][:, h, 2 * P - w + z:2 * P - w + e]
                    else:
                        m = U[:, at[i] + z:at[i] + e]
                    zb = z // 512
                    dve.tensor_tensor_reduce(out=S[k][:, z:e], in0=pS[k][zb][:, z - 512 * zb:e - 512 * zb], in1=m,
                                             scale=MLA_SCALE if g == 0 else DSA_SCALE, scalar=NEG, op0=ALU.add, op1=ALU.max,
                                             accum_out=mxp[:, k, a:a + 1]).then_inc(s_mx, 1)
                    nmx[0] += 1
                dve.wait_ge(s_mx, nmx[0])
                dve.tensor_reduce(mx[:, n % 4, 0:1], mxp[:, k, 0:len(parts)], AX.X, ALU.max, negate=True).then_inc(s_nm, 1)

            def norm(n):
                i, g, h = items[n]
                dve.wait_ge(s_O, n + 1)
                dve.reciprocal(rs[:, n % 2:n % 2 + 1], mx[:, n % 4, 1:2]).then_inc(s_st, 1)
                dve.wait_ge(s_st, n + 1)
                if g == 0 and h == 0 and i >= 2:
                    dve.wait_ge(s_out[i % 2], 16 * (i // 2))
                dve.tensor_scalar(O[i % 2][:, g * 512 + h * 64:g * 512 + h * 64 + 64], pO[n % 2][:, 0:64], rs[:, n % 2:n % 2 + 1],
                                  None, ALU.mult).then_inc(s_on, 1)

            scale_and_max(0)
            for n in range(len(items)):
                if n + 1 < len(items):
                    scale_and_max(n + 1)
                evac(dve, n, 0)
                if n:
                    norm(n - 1)
            norm(len(items) - 1)


def scoped(nc):
    ctx = ExitStack()

    def sb(name, shape, dt=F32):
        return ctx.enter_context(nc.sbuf_tensor(name, shape, dt))

    def ps(name, w=512):
        return ctx.enter_context(nc.psum_tensor(name, [P, w], F32))
    return ctx, sb, ps


def stage_sample(nc, T, G, sem, sb, ps):
    pagef, SD = G["pagef"], G["SD"]
    ctx, sb1, ps1 = scoped(nc)
    with ctx:
        sample_mla(nc, T, G, sem, sb1, ps1, pagef)
    gpos, grow = sb("gpos", [P, 16]), sb("grow", [P, 16], I32)
    qb, kb, vb = sb("qb", [P, NS, 512]), sb("kb", [P, NS, 512]), sb("vb", [P, NS, 512])
    rel = sb("rel", [P, NB_REL, H])
    ctx, sb1, ps1 = scoped(nc)
    with ctx:
        sample_select(nc, T, G, sem, sb1, ps1, pagef, SD, gpos, grow, qb, kb, vb, rel)
    ctx, sb1, ps1 = scoped(nc)
    with ctx:
        sample_dsa(nc, T, G, sem, sb1, ps1, gpos, grow, qb, kb, vb, rel)


def stage_index(nc, T, G, sem, sb, ps):
    c, pages, pagef, SD = G["c"], G["pages"], G["pagef"], G["SD"]
    NP2 = NS // 2
    KI = [sb(f"KI{i}", [P, PAGE + 1, IDX]) for i in range(2)]
    qr = sb("dqr", [NS, H, 2, IDX])
    QB = sb("QB", [P, NS, 2, H])
    KT = [sb(f"KT{i}", [P, 512]) for i in range(2)]
    WB = sb("WB", [P, NP2, H])
    RL = [sb(f"RL{i}", [P, 32, H]) for i in range(2)]
    pT, pS, pq = [ps("dT0"), ps("dT1")], [ps("dS0"), ps("dS1")], ps("dq0")
    s_pg, s_q, s_w, s_pi, s_z, s_qt, s_qb, s_T, s_evd, s_eva, s_S, s_R, s_v, s_a = (
        sem("di_" + n) for n in ("pg", "q", "w", "pi", "z", "qt", "qb", "T", "evd", "eva", "S", "R", "v", "add"))
    s_k = [sem("di_k0"), sem("di_k1")]
    s_f = [sem("di_f0"), sem("di_f1")]
    idx_pages = T["cache_idx_k"][0].rearrange("n s d -> n (s d)")
    fresh = T["o11"].rearrange("l b s d -> (l b s) d")
    uses = [(pr, k) for pr in range(NP2) for k in range(17)]
    nb = lambda u: (u // 17) * 5 + (u % 17) // 4
    with nc.Block() as block:
        @block.sync
        def _(sp):
            sp.dma_start(pages[:, :], T["page_table"].rearrange("(a b) p -> (b p) a", b=2), allow_slow_non_contiguous=True).then_inc(s_pg, 16)
            qi = T["p"][SEQ:NTOK, C_QI:C_QI + 512].rearrange("b (h d) -> b h d", h=H)
            for a in range(2):
                sp.dma_start(qr[:, :, a, :], qi).then_inc(s_q, 16)
            for b in range(NS):
                sp.dma_start(WB[64 * (b % 2):64 * (b % 2) + 64, b // 2, :],
                             T["wi"][SEQ + b:SEQ + b + 1, :].to_broadcast([64, H])).then_inc(s_w, 16)
            sp.wait_ge(s_z, 1)
            for pr in range(NP2):
                if pr >= 2:
                    sp.wait_ge(s_T, 17 * (pr - 1))
                for a in range(2):
                    sp.dma_start(KI[pr % 2][64 * a + 63:64 * a + 64, PAGE, :], fresh[2 * pr + a:2 * pr + a + 1, :]).then_inc(s_f[pr % 2], 16)

        @block.gpsimd
        def _(pool):
            pool.memset(KI[0][:, PAGE, :], 0.0).then_inc(s_pi, 1)
            pool.memset(KI[1][:, PAGE, :], 0.0).then_inc(s_pi, 1)
            pool.wait_ge(s_pi, 2)
            pool.sem_inc(s_z, 1)
            pool.wait_ge(s_pg, 16)
            for pr in range(NP2):
                if pr >= 2:
                    pool.wait_ge(s_T, 17 * (pr - 1))
                pool.indirect_dma_start(out=KI[pr % 2][:, 0:PAGE, :].rearrange("p s d -> p (s d)"), out_offset=None, in_=idx_pages,
                                        in_offset=bass.IndirectOffsetOnAxis(ap=pages[:, pr:pr + 1], axis=0)).then_inc(s_k[pr % 2], 16)

        @block.tensor
        def _(pe):
            pe.wait_ge(s_q, 32)
            for h in range(H):
                m = pe.transpose(pq[:, h * NS:(h + 1) * NS], qr[:, h, :, :].rearrange("b a d -> b (a d)"), c("ident")[0:NS, 0:NS])
            m.then_inc(s_qt, 1)

            def turn(u):
                pr, k = uses[u]
                if k == 0:
                    pe.wait_ge(s_k[pr % 2], 16 * (pr // 2 + 1))
                    pe.wait_ge(s_f[pr % 2], 32 * (pr // 2 + 1))
                if u >= 2:
                    pe.wait_ge(s_eva if u % 2 else s_evd, u // 2)
                for a in range(4 if k < 16 else 1):
                    s = 8 * k + 2 * a
                    src = KI[pr % 2][:, s:min(s + 2, PAGE + 1), :].rearrange("p s d -> p (s d)")
                    m = pe.transpose(pT[u % 2][0:src.shape[1], a * P:(a + 1) * P], src, c("ident"))
                m.then_inc(s_T, 1)

            def product(u):
                pr, k = uses[u]
                pe.wait_ge(s_eva if u % 2 else s_evd, u // 2 + 1)
                b = nb(u)
                if k % 4 == 0 and b >= 2:
                    pe.wait_ge(s_R, 2 * (b - 1))
                if k < 16:
                    for a in range(4):
                        o = ((k % 4) * 4 + a) * 32
                        m = pe.matmul(pS[b % 2][:, o:o + 32], KT[u % 2][:, a * P:(a + 1) * P], QB[:, 2 * pr:2 * pr + 2, :, :],
                                      start=True, stop=True)
                else:
                    m = pe.matmul(pS[b % 2][:, 0:32], KT[u % 2][0:64, 0:P], QB[0:64, 2 * pr:2 * pr + 2, :, :], start=True, stop=True)
                m.then_inc(s_S, 1)

            turn(0)
            pe.wait_ge(s_qb, 1)
            for u in range(len(uses)):
                if u + 1 < len(uses):
                    turn(u + 1)
                product(u)

        def evac(eng, u):
            if u < len(uses):
                eng.wait_ge(s_T, u + 1)
                if u >= 2:
                    eng.wait_ge(s_S, u - 1)
                r = P if uses[u][1] < 16 else 64
                w = 512 if uses[u][1] < 16 else P
                if u % 2:
                    eng.activation(KT[1][0:r, 0:w], pT[1][0:r, 0:w], ACT.Copy).then_inc(s_eva, 1)
                else:
                    eng.tensor_copy(KT[0][0:r, 0:w], pT[0][0:r, 0:w]).then_inc(s_evd, 1)

        @block.scalar
        def _(act):
            for u, (pr, k) in enumerate(uses):
                if u % 2 == 0:
                    evac(act, u + 1)
                if k % 4 == 3 or k == 16:
                    b = nb(u)
                    act.wait_ge(s_S, u + 1)
                    if b >= 2:
                        act.wait_ge(s_a, b - 1)
                    n = 16 if k < 16 else 1
                    for half in range(2):
                        src = pS[b % 2][64 * half:64 * half + 64, 0:n * 32].rearrange("p (n q s h) -> p n q s h", q=2, s=2, h=H)
                        src = src[:, :, half, :, :] if k < 16 else src[:, :, half, 0:1, :]
                        m = 2 * n if k < 16 else 1
                        dst = RL[b % 2][64 * half:64 * half + 64, 0:m, :].rearrange("p (n s) h -> p n s h", n=n)
                        act.activation(dst, src, ACT.Relu, scale=IDX ** -0.5).then_inc(s_R, 1)

        @block.vector
        def _(dve):
            link = serial(dve, s_v)
            link(dve.memset(QB[:, :, :, :], 0.0))
            dve.wait_ge(s_pg, 16)
            link(dve.tensor_copy(pagef[:, :], pages[:, :]))
            dve.wait_ge(s_w, 16 * NS)
            link(dve.tensor_scalar(WB[:, :, :], WB[:, :, :], H ** -0.5, None, ALU.mult))
            dve.wait_ge(s_qt, 1)
            for a in range(2):
                link(dve.tensor_copy(QB[64 * a:64 * a + 64, :, a, :], pq[64 * a:64 * a + 64, 0:64].rearrange("p (h b) -> p b h", h=H)))
            dve.sem_inc(s_qb, 1)
            evac(dve, 0)
            for u, (pr, k) in enumerate(uses):
                if u % 2:
                    evac(dve, u + 1)
                if k % 4 == 3 or k == 16:
                    b = nb(u)
                    dve.wait_ge(s_R, 2 * (b + 1))
                    m = 32 if k < 16 else 1
                    r = RL[b % 2][:, 0:m, :]
                    link(dve.tensor_tensor(r, r, WB[:, pr, :].unsqueeze(1).to_broadcast([P, m, H]), ALU.mult))
                    s0 = 32 * (k // 4) if k < 16 else PAGE
                    dve.tensor_reduce(SD[:, pr, s0:s0 + m], r, AX.X, ALU.add).then_inc(s_a, 1)
            dve.wait_ge(s_a, 5 * NP2)
            link(dve.tensor_tensor(SD[:, :, PAGE], SD[:, :, PAGE], c("fresh_neg").to_broadcast([P, NP2]), ALU.add))


def sample_mla(nc, T, G, sem, sb, ps, pagef):
    c = G["c"]
    NP2, NSL = NS // 2, PAGE + 1
    Wkv = sb("dWkv", [P, H, NOPE + VD])
    NR = 11
    LC = [sb(f"LC{i}", [P, 16, KVL]) for i in range(NR)]
    LF = [sb(f"LF{i}", [P, KVL]) for i in range(2)]
    KR_ = [sb(f"KR{i}", [P, NSL, ROPE]) for i in range(2)]
    LT = [sb(f"LT{i}", [P, 512]) for i in range(3)]
    SQ = [sb(f"SQ{i}", [P, 512]) for i in range(2)]
    ssq_, num_, rop_ = ([sb(f"{n}{i}", [P, NSL, H]) for i in range(2)] for n in ("ssq", "num", "rop"))
    P16 = sb("P16", [P, NSL, 16])
    qs = sb("qs", [NS, H, QK])
    gkn = sb("gkn", [NS, NOPE])
    qr4 = sb("qr4", [NS, H, 4, ROPE])
    QG = sb("QG", [64, H, NS])
    WT = sb("WT", [64, H, P])
    QT = sb("QT", [P, NS, H])
    QR = sb("QR", [P, NP2, 4, 2, H])
    idx = sb("latidx", [P, NP2, 8], I32)
    idxf = sb("latidxf", [P, NP2, 8])
    kidx = sb("kidx", [P, NP2], I32)
    m8, m16, d16, o16 = sb("m8", [P, H]), sb("m16", [P, 2, H]), sb("d16", [16, 1]), sb("o16", [P, 16])
    o1 = sb("o1", [16, P])
    M16, sums = sb("M16", [P, 2, H]), sb("sums", [P, 2, H])
    tmp = sb("dtmp", [16, 512])
    orow = sb("orow", [NS, 512])
    epst = sb("deps", [P, 1])
    WA = sb("WA", [P, NP2, 256 + 16])
    HK = 256
    pT, pN, pO = [ps("eT0"), ps("eT1")], ps("eN"), ps("eO")
    pK = [ps("eK0", 1024), ps("eK1", 1024)]
    names = ("in", "idx", "v", "pp", "qt", "T", "evd", "eva", "KN", "sq", "red", "nrc", "z", "zi",
             "S", "rt", "mx", "am", "M", "ex", "pv", "on", "o2", "tm", "den", "g", "rr", "ot", "nc", "or")
    (s_in, s_idx, s_v, s_pp, s_qt, s_T, s_evd, s_eva, s_KN, s_sq, s_red, s_nrc, s_z, s_zi,
     s_S, s_rt, s_mx, s_am, s_M, s_ex, s_pv, s_on, s_o2, s_tm, s_den, s_g, s_rr, s_ot, s_nc, s_or) = (sem("dm_" + n) for n in names)
    s_l = [sem(f"dm_l{j}") for j in range(8)]
    s_kr, s_f = [sem("dm_kr0"), sem("dm_kr1")], [sem("dm_f0"), sem("dm_f1")]
    lat_rows = T["cache_mla_latent"][0].rearrange("n (j s) c -> (n j) (s c)", j=8)
    kr_rows = T["cache_mla_krope"][0].rearrange("n s c -> n (s c)")
    uses, kn0 = [], []
    nk = 0
    for pr in range(NP2):
        for ch in range(9):
            uses.append((pr, ch, -1, 4 if ch < 8 else 1))
            kn0.append(nk)
            for k in range(4 if ch < 8 else 1):
                uses.append((pr, ch, k, 4 if ch < 8 else 1))
                kn0.append(nk)
                nk += uses[-1][3]
    per = len(uses) // NP2
    last_use = [per * (pr + 1) - 1 for pr in range(NP2)]

    def latents(pr, slot):
        return LF[pr % 2][:, :] if slot == PAGE else LC[(8 * pr + slot // 16) % NR][:, slot % 16, :]

    def finishing(u, steps):
        pr, r = divmod(u, per)
        return [(pr - 1, k) for k in steps if k == r] if pr else []

    with nc.Block() as block:
        @block.sync
        def _(sp):
            sp.dma_start(Wkv[:, :, :], T["w_kv_up"][0].rearrange("p (h n) -> p h n", h=H)).then_inc(s_in, 16)
            qsrc = T["qm"][SEQ:NTOK, :].rearrange("b (h d) -> b h d", h=H)
            sp.dma_start(qs[:, :, :], qsrc).then_inc(s_in, 16)
            sp.dma_start(gkn[:, :], T["g_mla_kn"].to_broadcast([NS, NOPE])).then_inc(s_in, 16)
            for a in range(4):
                sp.dma_start(qr4[:, :, a, :], qsrc[:, :, NOPE:QK]).then_inc(s_in, 16)
            sp.wait_ge(s_z, 1)
            lat = T["o7"].rearrange("l b s d -> (l b s) d")
            krf = T["o8"].rearrange("l b s d -> (l b s) d")
            for pr in range(NP2):
                if pr >= 2:
                    sp.wait_ge(s_pv, pr - 1)
                for a in range(2):
                    sp.dma_start(LF[pr % 2][64 * a + 63:64 * a + 64, :], lat[2 * pr + a:2 * pr + a + 1, :]).then_inc(s_f[pr % 2], 16)
                    sp.dma_start(KR_[pr % 2][64 * a + 63:64 * a + 64, PAGE, :], krf[2 * pr + a:2 * pr + a + 1, :]).then_inc(s_f[pr % 2], 16)
            sp.wait_ge(s_or, NP2)
            sp.dma_start(T["omix"][SEQ:NTOK, 0:512], orow[:, :]).then_inc(s_g, 16)
            sp.wait_ge(s_g, 16)

        @block.gpsimd
        def _(pool):
            for i in range(2):
                pool.memset(LF[i][:, :], 0.0).then_inc(s_zi, 1)
                pool.memset(KR_[i][:, PAGE, :], 0.0).then_inc(s_zi, 1)
            pool.memset(P16[:, :, :], 0.0).then_inc(s_zi, 1)
            pool.wait_ge(s_zi, 5)
            pool.sem_inc(s_z, 1)
            pool.wait_ge(s_idx, 1)

            def ropes(pr):
                if pr >= 2:
                    pool.wait_ge(s_pv, pr - 1)
                pool.indirect_dma_start(out=KR_[pr % 2][:, 0:PAGE, :].rearrange("p s d -> p (s d)"), out_offset=None, in_=kr_rows,
                                        in_offset=bass.IndirectOffsetOnAxis(ap=kidx[:, pr:pr + 1], axis=0)).then_inc(s_kr[pr % 2], 16)

            def chunk(pr, j):
                if 8 * pr + j >= NR:
                    pool.wait_ge(s_pv, (8 * pr + j - NR) // 8 + 1)
                if pr:
                    pool.wait_ge(s_l[j], 16 * pr)
                elif j >= 2:
                    pool.wait_ge(s_l[j - 2], 16)
                pool.indirect_dma_start(out=LC[(8 * pr + j) % NR][:, :, :].rearrange("p s d -> p (s d)"), out_offset=None, in_=lat_rows,
                                        in_offset=bass.IndirectOffsetOnAxis(ap=idx[:, pr, j:j + 1], axis=0)).then_inc(s_l[j], 16)

            ropes(0)
            for j in range(8):
                chunk(0, j)
            ahead = NR - 8
            for pr in range(NP2):
                if pr + 1 < NP2:
                    ropes(pr + 1)
                    for j in range(ahead):
                        chunk(pr + 1, j)
                pool.wait_ge(s_am, pr + 1)
                pool.partition_all_reduce(M16[:, :, :].rearrange("p a h -> p (a h)"), m16[:, :, :].rearrange("p a h -> p (a h)"),
                                          P, RMAX).then_inc(s_M, 1)
                if pr + 1 < NP2:
                    for j in range(ahead, 8):
                        chunk(pr + 1, j)

        @block.tensor
        def _(pe):
            I8 = c("ident")[0:NS, 0:NS]
            pe.wait_ge(s_qt, 1)
            pe.wait_ge(s_in, 112)
            for h in range(H):
                pe.transpose(pT[0][0:64, h * NS:(h + 1) * NS], qs[:, h, 0:NOPE], I8)
                pe.transpose(pT[1][:, h * NS:(h + 1) * NS], qr4[:, h, :, :].rearrange("b a r -> b (a r)"), I8)
            for h in range(4):
                pe.transpose(pK[0][0:64, h * P:(h + 1) * P], Wkv[:, h, 0:NOPE], c("ident"))
                m = pe.transpose(pK[1][0:64, h * P:(h + 1) * P], Wkv[:, 4 + h, 0:NOPE], c("ident"))
            m.then_inc(s_pp, 1)
            pe.wait_ge(s_qt, 2)
            for h in range(H):
                m = pe.matmul(pN[:, h * NS:(h + 1) * NS], WT[:, h, :], QG[:, h, :], start=True, stop=True)
            m.then_inc(s_pp, 1)
            pe.wait_ge(s_qt, 3)

            def turn(u):
                if u >= len(uses):
                    return
                pr, ch, k, cnt = uses[u]
                if k < 0 and ch == 0:
                    pe.wait_ge(s_kr[pr % 2], 16 * (pr // 2 + 1))
                    pe.wait_ge(s_f[pr % 2], 64 * (pr // 2 + 1))
                if k == 0 and ch < 8:
                    pe.wait_ge(s_l[ch], 16 * (pr + 1))
                if u >= 2:
                    pe.wait_ge(s_eva if u % 2 else s_evd, u // 2)
                for a in range(cnt):
                    if k < 0:
                        src = KR_[pr % 2][:, 16 * ch + 4 * a:min(16 * ch + 4 * a + 4, NSL), :].rearrange("p s r -> p (s r)")
                    else:
                        src = latents(pr, 16 * ch + 4 * k + a)
                    m = pe.transpose(pT[u % 2][0:src.shape[1], a * P:(a + 1) * P], src, c("ident"))
                m.then_inc(s_T, 1)

            def products(u):
                pr, ch, k, cnt = uses[u]
                pe.wait_ge(s_eva if u % 2 else s_evd, u // 2 + 1)
                cg = pr * 9 + ch
                N = pN[:, 0:256].rearrange("p (s w) -> p s w", w=16)
                if k < 0:
                    if cg:
                        pe.wait_ge(s_nrc, cg)
                    for a in range(cnt):
                        if ch < 8:
                            m = pe.matmul(N[:, 4 * a:4 * a + 4, :], LT[u % 3][:, a * P:(a + 1) * P],
                                          QR[:, pr, :, :, :].rearrange("p s q h -> p (s q h)"), start=True, stop=True)
                        else:
                            m = pe.matmul(N[:, 0, :], LT[u % 3][0:ROPE, 0:P],
                                          QR[0:ROPE, pr, 0, :, :].rearrange("p q h -> p (q h)"), start=True, stop=True)
                else:
                    for a in range(cnt):
                        kn = kn0[u] + a
                        if kn >= 2:
                            pe.wait_ge(s_nc, 2 * (kn - 1))
                        key = LT[u % 3][:, a * P:(a + 1) * P]
                        pe.matmul(pK[kn % 2][:, 0:HK + 16], key, WA[:, pr, :], start=True, stop=True)
                        pe.matmul(pK[kn % 2][:, 512:512 + HK], key, Wkv[:, 4:8, 0:NOPE], start=True, stop=True).then_inc(s_KN, 1)
                if k < 0:
                    m.then_inc(s_rr, 1)

            def finish(pr, step):
                if step == 7:
                    if pr:
                        pe.wait_ge(s_or, pr)
                    pe.wait_ge(s_ex, 2 * (pr + 1))
                    for k in range(NSL):
                        m = pe.matmul(pO[0:16, 0:P], P16[:, k, :], latents(pr, k), start=(k == 0), stop=(k == NSL - 1))
                    m.then_inc(s_pv, 1)
                    pe.wait_ge(s_mx, 3 * pr + 3)
                    pe.matmul(pO[0:16, P:P + 1], sums[:, :, :].rearrange("p a h -> p (a h)"), c("ones")[:, 0:1], start=True, stop=True).then_inc(s_den, 1)
                elif step == 9:
                    pe.wait_ge(s_on, 2 * pr + 1)
                    pe.transpose(pO[:, 2 * P:2 * P + 16], o1[:, :], c("ident")[0:16, 0:16]).then_inc(s_ot, 1)
                elif step == 11:
                    pe.wait_ge(s_on, 2 * pr + 2)
                    pe.matmul(pO[0:16, :], o16[:, :], Wkv[:, :, NOPE:], start=True, stop=True).then_inc(s_o2, 1)
                elif step == 13:
                    pe.wait_ge(s_tm, pr + 1)
                    pe.matmul(pO[0:NS, :], c("to_pair")[0:16, pr * NS:(pr + 1) * NS], tmp[:, :], start=True, stop=True).then_inc(s_rt, 1)

            turn(0)
            for u in range(len(uses)):
                turn(u + 1)
                products(u)
                for pr, step in finishing(u, (7, 9, 11, 13)):
                    finish(pr, step)
            for step in (7, 9, 11, 13):
                finish(NP2 - 1, step)

        def evac(eng, u):
            if u >= len(uses):
                return
            pr, ch, k, cnt = uses[u]
            eng.wait_ge(s_T, u + 1)
            if u >= 3:
                v = u - 3
                if uses[v][2] < 0:
                    eng.wait_ge(s_rr, sum(1 for x in uses[:v + 1] if x[2] < 0))
                else:
                    eng.wait_ge(s_KN, kn0[v] + uses[v][3])
            r = ROPE if (k < 0 and ch == 8) else P
            if u % 2:
                eng.activation(LT[u % 3][0:r, 0:cnt * P], pT[1][0:r, 0:cnt * P], ACT.Copy).then_inc(s_eva, 1)
            else:
                eng.tensor_copy(LT[u % 3][0:r, 0:cnt * P], pT[0][0:r, 0:cnt * P]).then_inc(s_evd, 1)

        @block.scalar
        def _(act):
            act.wait_ge(s_qt, 3)

            def exps(pr):
                act.wait_ge(s_mx, 3 * pr + 2)
                if pr:
                    act.wait_ge(s_pv, pr)
                for a in range(2):
                    r = slice(64 * a, 64 * a + 64)
                    act.activation(P16[r, :, 8 * a:8 * a + 8], num_[pr % 2][r, :, :], ACT.Exp).then_inc(s_ex, 1)

            for u, (pr, ch, k, cnt) in enumerate(uses):
                if u % 2 == 0:
                    evac(act, u + 1)
                if k >= 0:
                    for a in range(cnt):
                        kn = kn0[u] + a
                        act.wait_ge(s_KN, kn + 1)
                        if kn >= 2:
                            act.wait_ge(s_red, kn - 1)
                        act.activation(SQ[kn % 2][:, :].rearrange("p (a n) -> p a n", a=2),
                                       pK[kn % 2][:, :].rearrange("p (a n) -> p a n", a=2)[:, :, 0:HK], ACT.Square).then_inc(s_sq, 1)
                if u in last_use:
                    act.wait_ge(s_red, kn0[u] + cnt)
                    act.activation(ssq_[pr % 2][:, :, :], ssq_[pr % 2][:, :, :], ACT.Sqrt, scale=1.0 / NOPE, bias=epst[:, 0:1]).then_inc(s_S, 1)
                for q, _ in finishing(u, (5,)):
                    exps(q)
            exps(NP2 - 1)

        @block.vector
        def _(dve):
            link = serial(dve, s_v)
            dve.wait_ge(s_in, 112)
            link(dve.memset(epst[:, :], EPS))
            link(dve.memset(sums[:, :, :], 0.0))
            link(dve.tensor_scalar(idxf[:, :, :], pagef[:, :].unsqueeze(2).to_broadcast([P, NP2, 8]), 8.0, None, ALU.mult))
            link(dve.tensor_tensor(idx[:, :, :], idxf[:, :, :], c("iota")[:, 0:8].unsqueeze(1).to_broadcast([P, NP2, 8]), ALU.add))
            link(dve.tensor_copy(kidx[:, :], pagef[:, :]))
            dve.sem_inc(s_idx, 1)
            link(dve.tensor_tensor(qs[:, :, 0:NOPE], qs[:, :, 0:NOPE], gkn[:, :].unsqueeze(1).to_broadcast([NS, H, NOPE]), ALU.mult))
            dve.sem_inc(s_qt, 1)
            link(dve.memset(QR[:, :, :, :, :], 0.0))
            dve.wait_ge(s_pp, 1)
            link(dve.tensor_copy(QG[:, :, :], pT[0][0:64, 0:64].rearrange("p (h b) -> p h b", h=H)))
            for a in range(4):
                r = slice(32 * a, 32 * a + 32)
                link(dve.tensor_copy(QR[r, :, a, :, :], pT[1][r, 0:64].rearrange("p (h n q) -> p n q h", h=H, q=2)))
            for a in range(2):
                link(dve.tensor_copy(WT[:, 4 * a:4 * a + 4, :], pK[a][0:64, 0:512].rearrange("p (h c) -> p h c", h=4)))
            dve.sem_inc(s_qt, 1)
            dve.wait_ge(s_pp, 2)
            for pr in range(NP2):
                link(dve.tensor_copy(WA[:, pr, 0:HK].rearrange("p (h d) -> p h d", h=4), Wkv[:, 0:4, 0:NOPE]))
            link(dve.tensor_copy(QT[:, :, :], pN[:, 0:64].rearrange("p (h b) -> p b h", h=H)))
            for pr in range(NP2):
                link(dve.tensor_copy(WA[:, pr, HK:HK + 16], QT[:, 2 * pr:2 * pr + 2, :].rearrange("p b h -> p (b h)")))
            dve.sem_inc(s_qt, 1)

            def finish(pr, step):
                ssq, num, rop = ssq_[pr % 2], num_[pr % 2], rop_[pr % 2]
                if step == 1:
                    dve.wait_ge(s_S, pr + 1)
                    dve.wait_ge(s_nc, 2 * NSL * (pr + 1))
                    link(dve.reciprocal(ssq[:, :, :], ssq[:, :, :]))
                    link(dve.tensor_tensor(num[:, :, :], num[:, :, :], ssq[:, :, :], ALU.mult))
                elif step == 2:
                    link(dve.tensor_tensor(num[:, :, :], num[:, :, :], rop[:, :, :], ALU.add))
                    link(dve.tensor_scalar(num[:, :, :], num[:, :, :], MLA_SCALE, None, ALU.mult))
                elif step == 3:
                    link(dve.tensor_scalar(num[:, PAGE, :], num[:, PAGE, :], c("fresh_neg"), None, ALU.add))
                    dve.tensor_reduce(m8[:, :], num[:, :, :].rearrange("p s h -> p h s"), AX.X, ALU.max).then_inc(s_mx, 1)
                    dve.wait_ge(s_mx, 3 * pr + 1)
                    for a in range(2):
                        link(dve.tensor_scalar(m16[:, a, :], m8[:, :], c("half_neg")[:, a:a + 1], None, ALU.add))
                    dve.sem_inc(s_am, 1)
                elif step == 4:
                    dve.wait_ge(s_M, pr + 1)
                    for a in range(2):
                        r = slice(64 * a, 64 * a + 64)
                        m = dve.tensor_tensor(num[r, :, :], num[r, :, :], M16[r, a, :].unsqueeze(1).to_broadcast([64, NSL, H]), ALU.subtract)
                        if a == 0:
                            link(m)
                        else:
                            m.then_inc(s_mx, 1)
                elif step == 6:
                    dve.wait_ge(s_ex, 2 * (pr + 1))
                    for a in range(2):
                        r = slice(64 * a, 64 * a + 64)
                        link(dve.tensor_reduce(sums[r, a, :], P16[r, :, 8 * a:8 * a + 8].rearrange("p s h -> p h s"), AX.X, ALU.add))
                    dve.sem_inc(s_mx, 1)
                elif step == 8:
                    dve.wait_ge(s_den, pr + 1)
                    link(dve.reciprocal(d16[:, :], pO[0:16, P:P + 1]))
                    dve.tensor_scalar(o1[:, :], pO[0:16, 0:P], d16[:, 0:1], None, ALU.mult).then_inc(s_on, 1)
                elif step == 10:
                    dve.wait_ge(s_ot, pr + 1)
                    dve.tensor_copy(o16[:, :], pO[:, 2 * P:2 * P + 16]).then_inc(s_on, 1)
                elif step == 12:
                    dve.wait_ge(s_o2, pr + 1)
                    dve.tensor_tensor(tmp[:, :], pO[0:16, :], c("own_head")[0:16, :], ALU.mult).then_inc(s_tm, 1)
                elif step == 14:
                    dve.wait_ge(s_rt, pr + 1)
                    if pr == 0:
                        dve.tensor_copy(orow[:, :], pO[0:NS, :]).then_inc(s_or, 1)
                    else:
                        dve.wait_ge(s_or, pr)
                        dve.tensor_tensor(orow[:, :], orow[:, :], pO[0:NS, :], ALU.add).then_inc(s_or, 1)

            STEPS = (1, 2, 3, 4, 6, 8, 10, 12, 14)
            evac(dve, 0)
            for u, (pr, ch, k, cnt) in enumerate(uses):
                ssq, num, rop = ssq_[pr % 2], num_[pr % 2], rop_[pr % 2]
                if u % 2 == 1:
                    evac(dve, u + 1)
                if k >= 0:
                    for a in range(cnt):
                        kn = kn0[u] + a
                        dve.wait_ge(s_sq, kn + 1)
                        for half in range(2):
                            r = slice(64 * half, 64 * half + 64)
                            dve.tensor_copy(num[r, 16 * ch + 4 * k + a, :], pK[kn % 2][r, HK + 8 * half:HK + 8 * half + 8]).then_inc(s_nc, 1)
                        dve.tensor_reduce(ssq[:, 16 * ch + 4 * k + a, :], SQ[kn % 2][:, :].rearrange("p (h d) -> p h d", h=H),
                                          AX.X, ALU.add).then_inc(s_red, 1)
                else:
                    cg = pr * 9 + ch
                    n = 16 if ch < 8 else 1
                    dve.wait_ge(s_rr, cg + 1)
                    N = pN[:, 0:256].rearrange("p (s w) -> p s w", w=16)
                    for a in range(2):
                        r = slice(64 * a, 64 * a + 64)
                        link(dve.tensor_copy(rop[r, 16 * ch:16 * ch + n, :], N[r, 0:n, 8 * a:8 * a + 8]))
                    dve.sem_inc(s_nrc, 1)
                for q, step in finishing(u, STEPS):
                    finish(q, step)
            for step in STEPS:
                finish(NP2 - 1, step)


def sample_select(nc, T, G, sem, sb, ps, pagef, SD, gpos, grow, qb, kb, vb, rel):
    c = G["c"]
    NP2, NSL = NS // 2, PAGE + 1
    NPOOL = T["cache_idx_k"].shape[1]
    junk = sb("zj", [P, NP2, NSL], BF16)
    thr = G["thr"]
    cnt, need, pre = (sb("z" + n, [P, NP2]) for n in ("cnt", "need", "pre"))
    eq, rank, ones = sb("zeq", [P, NP2, NSL]), sb("zrank", [P, NP2, NSL]), sb("zones", [P, NSL])
    hi, lo = sb("zhi", [P, NP2, NSL]), sb("zlo", [P, NP2, NSL])
    ri, rj = sb("zri", [P, NP2, NSL], I32), sb("zrj", [P, NP2, NSL], I32)
    A_ = [sb(f"zA{i}", [P, NSL, 32]) for i in range(2)]
    B_ = [sb(f"zB{i}", [P, NSL, 2, 16]) for i in range(2)]
    key, row = sb("zkey", [P, NSL]), sb("zrow", [P, NSL])
    lst = sb("zlst", [32, NP2, 32])
    ld = [sb("zld0", [16, P]), sb("zld1", [16, P])]
    gr = sb("zgr", [P, 16])
    pC, pL, pG = ps("zC"), ps("zL"), ps("zG")
    s_b, s_v, s_c, s_p, s_ab, s_l, s_lc, s_o, s_i, s_t = (sem("dz_" + n) for n in ("b", "v", "c", "p", "ab", "l", "lc", "o", "i", "t"))
    with nc.Block() as block:
        @block.tensor
        def _(pe):
            def total(n, w):
                pe.wait_ge(s_c, n + 1)
                pe.matmul(pC[:, 0:NP2], c(w), cnt[:, :], start=True, stop=True).then_inc(s_p, 1)
            total(0, "same_half")
            total(1, "before_half")
            total(2, "before_half")
            for pr in range(NP2):
                pe.wait_ge(s_ab, pr + 1)
                for s in range(NSL):
                    m = pe.matmul(pL[0:32, pr * 32:(pr + 1) * 32], A_[pr % 2][:, s, :], B_[pr % 2][:, s, :, :].rearrange("p a b -> p (a b)"),
                                  start=(s == 0), stop=(s == NSL - 1))
                m.then_inc(s_l, 1)
            pe.wait_ge(s_i, 32)
            pe.transpose(pG[:, 0:16], ld[0][:, :], c("ident")[0:16, 0:16])
            pe.transpose(pG[:, 16:32], ld[1][:, :], c("ident")[0:16, 0:16]).then_inc(s_t, 1)

        @block.sync
        def _(sp):
            kf, vf = T["o9"].rearrange("l b s h d -> (l b s) (h d)"), T["o10"].rearrange("l b s h d -> (l b s) (h d)")
            for src, dst in ((T["qd"][SEQ:NTOK, :], qb), (kf, kb), (vf, vb)):
                for b in range(NS):
                    sp.dma_start(dst[:, b, :], src[b:b + 1, :].to_broadcast([P, 512])).then_inc(s_b, 16)
            sp.dma_start(rel[:, :, :].rearrange("p k h -> p (k h)"),
                         T["rel_bias"].rearrange("(o k) h -> o (k h)", o=1).to_broadcast([P, NB_REL * H])).then_inc(s_b, 16)
            sp.wait_ge(s_lc, 1)
            for a, n in enumerate(("dpos", "drow")):
                sp.dma_start(T[n].rearrange("n a b -> a n b"), lst[:, :, 16 * a:16 * a + 16]).then_inc(s_o, 16)
            sp.wait_ge(s_o, 32)
            for a, n in enumerate(("dpos", "drow")):
                sp.dma_start(ld[a][:, :], T[n].rearrange("n (s h a) b -> (n s h) (a b)", s=2, h=2)).then_inc(s_i, 16)
            sp.wait_ge(s_b, 16 * 25)

        @block.vector
        def _(dve):
            link = serial(dve, s_v)

            def count(op, by):
                for pr in range(NP2):
                    x = by if isinstance(by, float) else by[:, pr:pr + 1]
                    link(dve.tensor_scalar(junk[:, pr, :], SD[:, pr, :], x, 0.0, op, ALU.add, accum_out=cnt[:, pr:pr + 1]))

            link(dve.memset(ones[:, :], 1.0))
            count(ALU.is_gt, thr)
            dve.sem_inc(s_c, 1)
            dve.wait_ge(s_p, 1)
            link(dve.tensor_scalar(need[:, :], pC[:, 0:NP2], -1.0, float(TOPK), ALU.mult, ALU.add))
            for pr in range(NP2):
                link(dve.tensor_scalar(eq[:, pr, :], SD[:, pr, :], thr[:, pr:pr + 1], None, ALU.is_equal))
                link(dve.tensor_tensor_scan(rank[:, pr, :], ones[:, :], eq[:, pr, :], 0.0, ALU.mult, ALU.add))
            link(dve.tensor_copy(cnt[:, :], rank[:, :, NSL - 1]))
            dve.sem_inc(s_c, 1)
            dve.wait_ge(s_p, 2)
            link(dve.tensor_tensor(need[:, :], need[:, :], pC[:, 0:NP2], ALU.subtract))
            for pr in range(NP2):
                link(dve.scalar_tensor_tensor(out=eq[:, pr, :], in0=rank[:, pr, :], scalar=need[:, pr:pr + 1], in1=eq[:, pr, :],
                                              op0=ALU.is_le, op1=ALU.mult))
                link(dve.scalar_tensor_tensor(out=eq[:, pr, :], in0=SD[:, pr, :], scalar=thr[:, pr:pr + 1], in1=eq[:, pr, :],
                                              op0=ALU.is_gt, op1=ALU.add))
                link(dve.tensor_tensor_scan(rank[:, pr, :], ones[:, :], eq[:, pr, :], 0.0, ALU.mult, ALU.add))
            link(dve.tensor_copy(cnt[:, :], rank[:, :, NSL - 1]))
            dve.sem_inc(s_c, 1)
            dve.wait_ge(s_p, 3)
            link(dve.tensor_copy(pre[:, :], pC[:, 0:NP2]))
            link(dve.tensor_scalar(pre[:, :], pre[:, :], 1023.0, None, ALU.add))
            for pr in range(NP2):
                link(dve.scalar_tensor_tensor(out=rank[:, pr, :], in0=rank[:, pr, :], scalar=pre[:, pr:pr + 1], in1=eq[:, pr, :],
                                              op0=ALU.add, op1=ALU.mult))
            link(dve.tensor_scalar(ri[:, :, :], rank[:, :, :], -1024.0, None, ALU.add))
            link(dve.tensor_scalar(rj[:, :, :], ri[:, :, :], 4, None, ALU.arith_shift_right))
            link(dve.tensor_copy(hi[:, :, :], rj[:, :, :]))
            link(dve.tensor_scalar(hi[:, :, :], hi[:, :, :], c("half32"), None, ALU.add))
            link(dve.tensor_scalar(rj[:, :, :], ri[:, :, :], 15, None, ALU.bitwise_and))
            link(dve.tensor_copy(lo[:, :, :], rj[:, :, :]))
            link(dve.memset(key[:, :], float(PAGE)))
            link(dve.tensor_copy(key[:, 0:PAGE], c("iota")))
            for pr in range(NP2):
                A, B = A_[pr % 2], B_[pr % 2]
                link(dve.scalar_tensor_tensor(out=row[:, :], in0=ones[:, :], scalar=pagef[:, pr:pr + 1], in1=ones[:, :], op0=ALU.mult, op1=ALU.mult))
                link(dve.tensor_scalar(row[:, :], row[:, :], float(PAGE), None, ALU.mult))
                link(dve.tensor_tensor(row[:, :], row[:, :], key[:, :], ALU.add))
                if pr >= 2:
                    dve.wait_ge(s_l, pr - 1)
                link(dve.tensor_tensor(A[:, :, :], hi[:, pr, :].unsqueeze(2).to_broadcast([P, NSL, 32]),
                                       c("iota")[:, 0:32].unsqueeze(1).to_broadcast([P, NSL, 32]), ALU.is_equal))
                link(dve.tensor_tensor(B[:, :, 0, :], lo[:, pr, :].unsqueeze(2).to_broadcast([P, NSL, 16]),
                                       c("iota")[:, 0:16].unsqueeze(1).to_broadcast([P, NSL, 16]), ALU.is_equal))
                link(dve.tensor_tensor(B[:, :, 1, :], B[:, :, 0, :], row[:, :].unsqueeze(2).to_broadcast([P, NSL, 16]), ALU.mult))
                link(dve.tensor_scalar(row[:, :], c("page_of").to_broadcast([P, NSL]), float(PAGE), None, ALU.mult))
                link(dve.tensor_tensor(row[:, :], row[:, :], key[:, :], ALU.add))
                link(dve.tensor_tensor(B[:, :, 0, :], B[:, :, 0, :], row[:, :].unsqueeze(2).to_broadcast([P, NSL, 16]), ALU.mult))
                dve.sem_inc(s_ab, 1)
            dve.wait_ge(s_l, NP2)
            dve.tensor_copy(lst[:, :, :].rearrange("p a b -> p (a b)"), pL[0:32, 0:NP2 * 32]).then_inc(s_lc, 1)
            dve.wait_ge(s_t, 1)
            link(dve.tensor_copy(gpos[:, :], pG[:, 0:16]))
            link(dve.tensor_scalar(gr[:, :], pG[:, 16:32], float(NPOOL * PAGE - 1), None, ALU.min))
            link(dve.tensor_copy(grow[:, :], gr[:, :]))


def sample_dsa(nc, T, G, sem, sb, ps, gpos, grow, qb, kb, vb, rel):
    c = G["c"]
    KS, VS = sb("KS", [P, 16, 512]), sb("VS", [P, 16, 512])
    rd = sb("rdd", [P, NB_REL - 1, H])
    M = sb("yM", [P, 16, NB_REL - 1])
    M2 = sb("yM2", [P, 16, NB_REL - 1])
    dist, isf, notf = sb("dist", [P, 16]), sb("isf", [P, 16]), sb("notf", [P, 16])
    S, sf = sb("yS", [P, 16, H]), sb("sf", [P, NS, H])
    PN, PF = sb("PN", [P, 16, H]), sb("PF", [P, 16, H])
    mx, mh = sb("ymx", [P, 16, H]), sb("ymh", [P, NS, H])
    prod = [sb("prod0", [P, 512]), sb("prod1", [P, 512])]
    tmp = [sb("ytmp0", [H, 512]), sb("ytmp1", [H, 512])]
    den = sb("yden", [H, NS])
    orow = sb("yorow", [NS, 512])
    pO, pD, pR = [ps("yO0"), ps("yO1")], ps("yD"), ps("yR")
    s_vv, s_v, s_m, s_M, s_p, s_e, s_o, s_n, s_r, s_c, s_st, s_dn = (
        sem("dy_" + n) for n in ("vv", "v", "m", "M", "p", "e", "o", "n", "r", "c", "st", "dn"))
    s_k1 = [sem(f"dy_k{j}") for j in range(16)]
    k_rows = T["cache_dsa_k"][0].rearrange("n s h d -> (n s) (h d)")
    v_rows = T["cache_dsa_v"][0].rearrange("n s h d -> (n s) (h d)")
    with nc.Block() as block:
        @block.sync
        def _(sp):
            sp.wait_ge(s_c, 1)
            sp.dma_start(T["omix"][SEQ:NTOK, 512:1024], orow[:, :]).then_inc(s_st, 16)
            sp.wait_ge(s_st, 16)

        @block.gpsimd
        def _(pool):
            for j in range(16):
                pool.indirect_dma_start(out=KS[:, j, :], out_offset=None, in_=k_rows,
                                        in_offset=bass.IndirectOffsetOnAxis(ap=grow[:, j:j + 1], axis=0)).then_inc(s_k1[j], 16)
            for j in range(16):
                pool.indirect_dma_start(out=VS[:, j, :], out_offset=None, in_=v_rows,
                                        in_offset=bass.IndirectOffsetOnAxis(ap=grow[:, j:j + 1], axis=0)).then_inc(s_vv, 16)
            pool.wait_ge(s_m, 1)
            pool.partition_all_reduce(mx[:, :, :].rearrange("p j h -> p (j h)"), S[:, :, :].rearrange("p j h -> p (j h)"), P, RMAX).then_inc(s_M, 1)

        @block.scalar
        def _(act):
            act.wait_ge(s_m, 2)
            act.activation(S[:, :, :], S[:, :, :], ACT.Exp).then_inc(s_e, 1)

        @block.vector
        def _(dve):
            link = serial(dve, s_v)
            link(dve.tensor_scalar(dist[:, :], gpos[:, :], -1.0, float(PAST), ALU.mult, ALU.add))
            link(dve.tensor_scalar(isf[:, :], gpos[:, :], float(PAST), None, ALU.is_equal))
            link(dve.tensor_scalar(notf[:, :], isf[:, :], -1.0, 1.0, ALU.mult, ALU.add))
            link(dve.tensor_tensor(rd[:, :, :], rel[:, 1:NB_REL, :], rel[:, 0:NB_REL - 1, :], ALU.subtract))
            n = NB_REL - 1
            link(dve.tensor_tensor(M[:, :, :], dist[:, :].unsqueeze(2).to_broadcast([P, 16, n]),
                                   c("rel_from").unsqueeze(1).to_broadcast([P, 16, n]), ALU.is_ge))
            for h in range(H):
                link(dve.tensor_tensor(M2[:, :, :], M[:, :, :], rd[:, :, h].unsqueeze(1).to_broadcast([P, 16, n]), ALU.mult))
                link(dve.tensor_reduce(mx[:, :, h], M2[:, :, :], AX.X, ALU.add))
            link(dve.tensor_tensor(mx[:, :, :], mx[:, :, :], rel[:, 0, :].unsqueeze(1).to_broadcast([P, 16, H]), ALU.add))
            for b in range(NS):
                link(dve.tensor_tensor(prod[0][:, :], kb[:, b, :], qb[:, b, :], ALU.mult))
                link(dve.tensor_reduce(sf[:, b, :], prod[0][:, :].rearrange("p (h d) -> p h d", h=H), AX.X, ALU.add))
            for j in range(16):
                dve.wait_ge(s_k1[j], 16)
                link(dve.tensor_tensor(prod[j % 2][:, :], KS[:, j, :], qb[:, j // 2, :], ALU.mult))
                link(dve.tensor_reduce(S[:, j, :], prod[j % 2][:, :].rearrange("p (h d) -> p h d", h=H), AX.X, ALU.add))
                link(dve.tensor_scalar(S[:, j, :], S[:, j, :], notf[:, j:j + 1], None, ALU.mult))
                link(dve.scalar_tensor_tensor(out=S[:, j, :], in0=sf[:, j // 2, :], scalar=isf[:, j:j + 1], in1=S[:, j, :],
                                              op0=ALU.mult, op1=ALU.add))
            link(dve.scalar_tensor_tensor(out=S[:, :, :], in0=S[:, :, :], scalar=DSA_SCALE, in1=mx[:, :, :], op0=ALU.mult, op1=ALU.add))
            dve.sem_inc(s_m, 1)
            dve.wait_ge(s_M, 1)
            m4 = mx[:, :, :].rearrange("p (b a) h -> p b a h", a=2)
            link(dve.tensor_tensor(mh[:, :, :], m4[:, :, 0, :], m4[:, :, 1, :], ALU.max))
            s4 = S[:, :, :].rearrange("p (b a) h -> p b a h", a=2)
            link(dve.tensor_tensor(s4, s4, mh[:, :, :].unsqueeze(2).to_broadcast([P, NS, 2, H]), ALU.subtract))
            dve.sem_inc(s_m, 1)
            dve.wait_ge(s_e, 1)
            link(dve.tensor_tensor(PN[:, :, :], S[:, :, :], notf[:, :].unsqueeze(2).to_broadcast([P, 16, H]), ALU.mult))
            link(dve.tensor_tensor(PF[:, :, :], S[:, :, :], isf[:, :].unsqueeze(2).to_broadcast([P, 16, H]), ALU.mult))
            dve.sem_inc(s_p, 1)
            dve.wait_ge(s_dn, 1)
            link(dve.reciprocal(den[:, :], pD[0:H, 0:NS]))
            for b in range(NS):
                dve.wait_ge(s_o, b + 1)
                if b >= 2:
                    dve.wait_ge(s_r, b - 1)
                dve.scalar_tensor_tensor(out=tmp[b % 2][:, :], in0=pO[b % 2][0:H, :], scalar=den[:, b:b + 1], in1=c("own_head")[0:H, :],
                                         op0=ALU.mult, op1=ALU.mult).then_inc(s_n, 1)
            dve.wait_ge(s_r, NS)
            dve.tensor_copy(orow[:, :], pR[0:NS, :]).then_inc(s_c, 1)

        @block.tensor
        def _(pe):
            pe.wait_ge(s_p, 1)
            for b in range(NS):
                for a in range(2):
                    m = pe.matmul(pD[0:H, b:b + 1], S[:, 2 * b + a, :], c("ones")[:, 0:1], start=(a == 0), stop=(a == 1))
            m.then_inc(s_dn, 1)
            pe.wait_ge(s_vv, 256)

            def fold(b):
                pe.wait_ge(s_n, b + 1)
                pe.matmul(pR[0:NS, :], c("to_row")[0:H, b * NS:(b + 1) * NS], tmp[b % 2][:, :], start=(b == 0), stop=(b == NS - 1)).then_inc(s_r, 1)

            for b in range(NS):
                if b >= 2:
                    pe.wait_ge(s_n, b - 1)
                for a in range(2):
                    j = 2 * b + a
                    pe.matmul(pO[b % 2][0:H, :], PN[:, j, :], VS[:, j, :], start=(a == 0), stop=False)
                    m = pe.matmul(pO[b % 2][0:H, :], PF[:, j, :], vb[:, b, :], start=False, stop=(a == 1))
                m.then_inc(s_o, 1)
                if b:
                    fold(b - 1)
            fold(NS - 1)


TOKP = (NT + 1) * P


def stage_out(nc, T, G, sem, sb, ps):
    c = G["c"]
    Wo = sb("Wo", [P, KD, D])
    Wr = sb("Wr", [P, KD, NE])
    mod = {n: (sb("r_" + n, [P, D]), sb("rs_" + n, [NS, D])) for n in ("ga", "sf", "cf")}
    gf = sb("gfr", [P, D])
    mi = [sb(f"mi{i}", [P, D]) for i in range(2)]
    xi = [sb(f"xi{i}", [P, D]) for i in range(2)]
    x1 = [sb(f"x1{i}", [P, D]) for i in range(2)]
    h2 = [sb(f"h2{i}", [P, D]) for i in range(2)]
    mT = [sb(f"mT{i}", [P, KD, P]) for i in range(2)]
    hT = sb("hT", [P, KD, P])
    junk, st, epst = sb("ojunk", [P, D]), sb("ost", [P, 3, NT + 1]), sb("oeps", [P, 1])
    lg = G["lg"]
    pT, pY, pR = [ps(f"oT{i}") for i in range(4)], [ps("oY0"), ps("oY1")], ps("oR")
    names = ("m", "mt", "mte", "y", "x1", "ss", "rt", "h", "ht", "hte", "r", "lg", "v", "z")
    s_m, s_mt, s_mte, s_y, s_x1, s_ss, s_rt, s_h, s_ht, s_hte, s_r, s_lg, s_v, s_z = (sem("ou_" + n) for n in names)
    s_in, s_xi, s_st = [sem("ou_i0"), sem("ou_i1")], [sem("ou_xi0"), sem("ou_xi1")], [sem("ou_s0"), sem("ou_s1")]
    s_w = [sem("ou_w0"), sem("ou_w1")]
    xp, xs = T["x_prompt"][0], T["x_sample"].rearrange("b s d -> (b s) d")
    with nc.Block() as block:
        @block.sync
        def _(sp):
            def constants():
                for j, n in ((2, "ga"), (3, "sf"), (4, "cf")):
                    sp.dma_start(mod[n][0][:, :], T["mod"][NS:NC9, j * D:(j + 1) * D].to_broadcast([P, D])).then_inc(s_m, 16)
                    sp.dma_start(mod[n][1][:, :], T["mod"][0:NS, j * D:(j + 1) * D]).then_inc(s_m, 16)
                sp.dma_start(gf[:, :], T["g_ffn_norm"].to_broadcast([P, D])).then_inc(s_m, 16)
                sp.dma_start(Wr[:, :, :], T["w_router"][0].rearrange("(k p) n -> p k n", p=P)).then_inc(s_m, 16)

            for t, R in tiles():
                if t >= 2:
                    sp.wait_ge(s_mt, 2 * (t - 1))
                sp.dma_start(mi[t % 2][0:R, :], T["omix"][t * P:t * P + R, :]).then_inc(s_in[t % 2], 16)
                if t == 0:
                    for n in range(2):
                        sp.dma_start(Wo[:, :, n * 512:(n + 1) * 512], T["w_out"][0, :, n * 512:(n + 1) * 512]
                                     .rearrange("(k p) n -> p k n", p=P)).then_inc(s_w[n], 16)
                if t >= 2:
                    sp.wait_ge(s_x1, 2 * (t - 1))
                sp.dma_start(xi[t % 2][0:R, :], token_rows(xp, xs, t)).then_inc(s_xi[t % 2], 16)
                if t == 1:
                    constants()

        @block.gpsimd
        def _(pool):
            for t, R in tiles():
                pool.wait_ge(s_h, t + 1)
                if t == NT:
                    R2 = P
                else:
                    R2 = R
                pool.dma_start(T["x1"][t * P:t * P + R, :], x1[t % 2][0:R, :]).then_inc(s_st[t % 2], 16)
                pool.dma_start(T["h2"][t * P:t * P + R2, :], h2[t % 2][0:R2, :]).then_inc(s_st[t % 2], 16)
            pool.wait_ge(s_st[0], 32 * 5)
            pool.wait_ge(s_st[1], 32 * 4)

        @block.tensor
        def _(pe):
            def turn_mix(t, R):
                pe.wait_ge(s_in[t % 2], 16 * (t // 2 + 1))
                if t:
                    pe.wait_ge(s_mte, 2 * t)
                for k in range(KD):
                    m = pe.transpose(pT[k // 4][:, (k % 4) * P:(k % 4) * P + R], mi[t % 2][0:R, k * P:(k + 1) * P], c("ident")[0:R, 0:R])
                    if k % 4 == 3:
                        m.then_inc(s_mt, 1)

            def out(t, R):
                pe.wait_ge(s_mte, 2 * (t + 1))
                if t:
                    pe.wait_ge(s_x1, 2 * t)
                for n in range(2):
                    if t == 0:
                        pe.wait_ge(s_w[n], 16)
                    for k in range(KD):
                        m = pe.matmul(pY[n][0:R, :], mT[t % 2][:, k, 0:R], Wo[:, k, n * 512:(n + 1) * 512], start=(k == 0), stop=(k == KD - 1))
                    m.then_inc(s_y, 1)

            def route(t, R):
                pe.wait_ge(s_h, t + 1)
                if t:
                    pe.wait_ge(s_hte, 2 * t)
                for k in range(KD):
                    m = pe.transpose(pT[2 + k // 4][:, (k % 4) * P:(k % 4) * P + R], h2[t % 2][0:R, k * P:(k + 1) * P], c("ident")[0:R, 0:R])
                    if k % 4 == 3:
                        m.then_inc(s_ht, 1)
                pe.wait_ge(s_hte, 2 * (t + 1))
                if t:
                    pe.wait_ge(s_lg, t)
                for k in range(KD):
                    m = pe.matmul(pR[0:R, 0:NE], hT[:, k, 0:R], Wr[:, k, :], start=(k == 0), stop=(k == KD - 1))
                m.then_inc(s_r, 1)

            turn_mix(*tiles()[0])
            for t, R in tiles():
                if t < NT:
                    turn_mix(*tiles()[t + 1])
                out(t, R)
                if t:
                    route(*tiles()[t - 1])
            route(*tiles()[NT])

        @block.scalar
        def _(act):
            def mt(t, R):
                for n in range(2):
                    act.wait_ge(s_mt, 2 * t + n + 1)
                    if t >= 2:
                        act.wait_ge(s_y, 2 * (t - 1))
                    act.activation(mT[t % 2][:, 4 * n:4 * n + 4, 0:R], pT[n][:, :].rearrange("p (k r) -> p k r", k=4)[:, :, 0:R], ACT.Copy).then_inc(s_mte, 1)

            def ht(t, R):
                for n in range(2):
                    act.wait_ge(s_ht, 2 * t + n + 1)
                    if t:
                        act.wait_ge(s_r, t)
                    act.activation(hT[:, 4 * n:4 * n + 4, 0:R], pT[2 + n][:, :].rearrange("p (k r) -> p k r", k=4)[:, :, 0:R], ACT.Copy).then_inc(s_hte, 1)

            act.wait_ge(s_z, 1)
            mt(*tiles()[0])
            for t, R in tiles():
                if t < NT:
                    mt(*tiles()[t + 1])
                if t:
                    ht(*tiles()[t - 1])
                act.wait_ge(s_x1, 2 * (t + 1))
                if t:
                    act.wait_ge(s_ss, t)
                act.activation(junk[0:R, :], x1[t % 2][0:R, :], ACT.Square, accum_out=st[0:R, 0, t:t + 1]).then_inc(s_ss, 1)
                act.wait_ge(s_ss, t + 1)
                act.activation(st[0:R, 1, t:t + 1], st[0:R, 0, t:t + 1], ACT.Sqrt, scale=1.0 / D, bias=epst[0:R, 0:1]).then_inc(s_rt, 1)
            ht(*tiles()[NT])

        @block.vector
        def _(dve):
            link = serial(dve, s_v)
            link(dve.memset(epst[:, :], EPS))
            dve.sem_inc(s_z, 1)
            link(dve.memset(lg[:, :, :], 0.0))
            dve.wait_ge(s_m, 128)
            A = mod["cf"]
            for a, R in ((0, P), (1, NS)):
                link(dve.scalar_tensor_tensor(out=A[a][0:R, :], in0=A[a][0:R, :], scalar=1.0, in1=gf[0:R, :], op0=ALU.add, op1=ALU.mult))
            for t, R in tiles():
                a = 0 if t < NT else 1
                if t >= 2:
                    dve.wait_ge(s_st[t % 2], 32 * (t // 2))
                    dve.wait_ge(s_ht, 2 * (t - 1))
                if t == NT:
                    link(dve.memset(h2[t % 2][:, :], 0.0))
                dve.wait_ge(s_xi[t % 2], 16 * (t // 2 + 1))
                for n in range(2):
                    sl = slice(n * 512, (n + 1) * 512)
                    dve.wait_ge(s_y, 2 * t + n + 1)
                    link(dve.tensor_tensor(x1[t % 2][0:R, sl], pY[n][0:R, :], mod["ga"][a][0:R, sl], ALU.mult))
                    dve.tensor_tensor(x1[t % 2][0:R, sl], x1[t % 2][0:R, sl], xi[t % 2][0:R, sl], ALU.add).then_inc(s_x1, 1)
                if t:
                    dve.wait_ge(s_r, t)
                    dve.tensor_copy(lg[0:P, t - 1, :], pR[0:P, 0:NE]).then_inc(s_lg, 1)
                dve.wait_ge(s_rt, t + 1)
                link(dve.reciprocal(st[0:R, 2, t:t + 1], st[0:R, 1, t:t + 1]))
                link(dve.scalar_tensor_tensor(out=h2[t % 2][0:R, :], in0=x1[t % 2][0:R, :], scalar=st[0:R, 2, t:t + 1], in1=A[a][0:R, :],
                                              op0=ALU.mult, op1=ALU.mult))
                dve.tensor_tensor(h2[t % 2][0:R, :], h2[t % 2][0:R, :], mod["sf"][a][0:R, :], ALU.add).then_inc(s_h, 1)
            dve.wait_ge(s_r, NT + 1)
            dve.tensor_copy(lg[0:NS, NT, :], pR[0:NS, 0:NE]).then_inc(s_lg, 1)


def stage_dispatch(nc, T, G, sem, sb, ps):
    c, lg = G["c"], G["lg"]
    NTT = NT + 1
    sh = [P, NTT, NE]
    SC, BI, S1, S2, SEL, GT, SV = (sb("g" + n, sh) for n in ("SC", "BI", "S1", "S2", "SEL", "GT", "SV"))
    br, ones, tot, car, pre = sb("gbr", [P, NE]), sb("gone", [P, NE]), sb("gtot", sh), sb("gcar", sh), sb("gpre", sh)
    m1, m2, cn, gr = (sb("g" + n, [P, NTT, NG]) for n in ("m1", "m2", "cn", "gr"))
    pw, pe2 = sb("gpw", [P, NTT, NG, NG]), sb("gpe", [P, NTT, NG, NG])
    top, need, sums = sb("gtop", [P, NTT, 8]), sb("gneed", [P, NTT]), sb("gsum", [P, NTT])
    nb, nbi, be = sb("gnb", [P, NE]), sb("gnbi", [P, NE], I32), sb("gbe", [P, NE])
    eb, npair = sb("geb", [P, 3]), sb("gnpair", [P, 1], I32)
    tokf = sb("gtokf", [P, NTT])
    slotf, posf, blkf = (sb("g" + n, [P, NTT, 8]) for n in ("slotf", "posf", "blkf"))
    slot, part = sb("gslot", [P, NTT, 8], I32), sb("gpart", [P, NTT, 8], I32)
    A = [sb(f"gA{i}", [P, TK, P]) for i in range(NTT)]
    B = [sb(f"gB{i}", [P, TK, NBLK]) for i in range(NTT)]
    pA, pC, pZ = (ps(f"g{n}") for n in "ACZ")
    pB, pD, pE, pL = pZ[:, 0:64], pZ[:, 64:128], pZ[:, 128:256], pZ[:, 256:256 + NBLK]
    WG, WD = sb("hWG", [P, KD, 2 * DE]), sb("hWD", [P, 2, D])
    X, Y = [sb(f"hX{i}", [P, D]) for i in range(2)], [sb(f"hY{i}", [P, D]) for i in range(2)]
    XT, AT = [sb(f"hXT{i}", [P, KD, P]) for i in range(2)], [sb(f"hAT{i}", [P, 2, P]) for i in range(2)]
    sg, gu, av = ([sb(f"h{n}{i}", [P, w]) for i in range(2)] for n, w in (("sg", DE), ("gu", 2 * DE), ("av", DE)))
    pX, pG, pH, pY = ps("hT"), ps("hG"), ps("hA"), [ps("hO0"), ps("hO1")]
    s_hw, s_hxt, s_hxe, s_hgu, s_hsg, s_ha1, s_ha, s_hat, s_hate, s_hy, s_hye = (
        sem("hs_" + n) for n in ("w", "xt", "xe", "gu", "sg", "a1", "a", "at", "ate", "y", "ye"))
    s_hwd, s_hx, s_hst = sem("hs_wd"), [sem("hs_x0"), sem("hs_x1")], [sem("hs_st0"), sem("hs_st1")]
    names = ("in", "v", "sg", "sel", "cnt", "eb", "AB", "lt", "m")
    s_in, s_v, s_sg, s_sel, s_cnt, s_eb, s_AB, s_lt, s_m = (sem("gd_" + n) for n in names)
    W = NTT * NE
    f = lambda a: a[:, :, :].rearrange("p t e -> p (t e)")
    with nc.Block() as block:
        @block.sync
        def _(sp):
            sp.dma_start(br[:, :], T["b_router"].to_broadcast([P, NE])).then_inc(s_in, 16)

            def load(m):
                if m >= 2:
                    sp.wait_ge(s_hxt, 2 * (m - 1))
                sp.dma_start(X[m % 2][:, :], T["h2"][m * P:(m + 1) * P, :]).then_inc(s_hx[m % 2], 16)

            def store(m):
                sp.wait_ge(s_hye, 2 * (m + 1))
                sp.dma_start(T["ysh"][m * P:(m + 1) * P, :], Y[m % 2][:, :]).then_inc(s_hst[m % 2], 16)

            load(0)
            sp.dma_start(WG[:, :, :], T["w_s_gu"][0].rearrange("(k p) n -> p k n", p=P)).then_inc(s_hw, 16)
            load(1)
            sp.dma_start(WD[:, :, :], T["w_s_down"][0].rearrange("(k p) n -> p k n", p=P)).then_inc(s_hwd, 16)
            for m in range(2, NTT + 3):
                if m < NTT:
                    load(m)
                if m >= 3:
                    store(m - 3)
            for i in range(2):
                sp.wait_ge(s_hst[i], 16 * ((NTT + 1 - i) // 2))

        @block.scalar
        def _(act):
            act.activation(SC[:, :, :], lg[:, :, :], ACT.Sigmoid).then_inc(s_sg, 1)

            def take_x(m):
                if m < NTT:
                    for n in range(2):
                        act.wait_ge(s_hxt, 2 * m + n + 1)
                        if m >= 2:
                            act.wait_ge(s_hgu, m - 1)
                        act.activation(XT[m % 2][:, 4 * n:4 * n + 4, :], pX[:, :].rearrange("p (k r) -> p k r", k=4), ACT.Copy).then_inc(s_hxe, 1)

            def take_gu(m):
                act.wait_ge(s_hgu, m + 1)
                if m >= 2:
                    act.wait_ge(s_ha, m - 1)
                act.activation(sg[m % 2][:, :], pG[:, 0:DE], ACT.Sigmoid).then_inc(s_hsg, 1)
                act.activation(gu[m % 2][:, :], pG[:, :], ACT.Copy).then_inc(s_hsg, 1)

            def take_a(m):
                act.wait_ge(s_hat, m + 1)
                if m >= 2:
                    act.wait_ge(s_hy, 2 * (m - 1))
                act.activation(AT[m % 2][:, :, :], pH[:, 0:2 * P].rearrange("p (k r) -> p k r", k=2), ACT.Copy).then_inc(s_hate, 1)

            def take_y(m):
                if m >= 2:
                    act.wait_ge(s_hst[m % 2], 16 * (m // 2))
                for n in range(2):
                    act.wait_ge(s_hy, 2 * m + n + 1)
                    act.activation(Y[m % 2][:, n * 512:(n + 1) * 512], pY[n][:, :], ACT.Copy).then_inc(s_hye, 1)

            take_x(0)
            for m in range(NTT + 1):
                take_x(m + 1)
                if m:
                    take_a(m - 1)
                if m < NTT:
                    take_gu(m)
                if m:
                    take_y(m - 1)

        @block.gpsimd
        def _(pool):
            for m in range(NTT):
                pool.wait_ge(s_hsg, 2 * m + 2)
                pool.tensor_tensor(sg[m % 2][:, :], sg[m % 2][:, :], gu[m % 2][:, 0:DE], ALU.mult).then_inc(s_ha1, 1)
                pool.wait_ge(s_ha1, m + 1)
                if m >= 2:
                    pool.wait_ge(s_hat, m - 1)
                pool.tensor_tensor(av[m % 2][:, :], sg[m % 2][:, :], gu[m % 2][:, DE:2 * DE], ALU.mult).then_inc(s_ha, 1)

        @block.tensor
        def _(pe):
            def turn_x(m, n):
                if m >= NTT:
                    return
                if n == 0:
                    pe.wait_ge(s_hx[m % 2], 16 * (m // 2 + 1))
                if 2 * m + n:
                    pe.wait_ge(s_hxe, 2 * m + n)
                for k in range(4):
                    mm = pe.transpose(pX[:, k * P:(k + 1) * P], X[m % 2][:, (4 * n + k) * P:(4 * n + k + 1) * P], c("ident"))
                mm.then_inc(s_hxt, 1)

            def gate_up(m, n):
                if m >= NTT:
                    return
                if n == 0:
                    if m == 0:
                        pe.wait_ge(s_hw, 16)
                    else:
                        pe.wait_ge(s_hsg, 2 * m)
                pe.wait_ge(s_hxe, 2 * m + n + 1)
                for k in range(4 * n, 4 * n + 4):
                    mm = pe.matmul(pG[:, :], XT[m % 2][:, k, :], WG[:, k, :], start=(k == 0), stop=(k == KD - 1))
                if n:
                    mm.then_inc(s_hgu, 1)

            def turn_a(m):
                pe.wait_ge(s_ha, m + 1)
                if m:
                    pe.wait_ge(s_hate, m)
                for k in range(2):
                    mm = pe.transpose(pH[:, k * P:(k + 1) * P], av[m % 2][:, k * P:(k + 1) * P], c("ident"))
                mm.then_inc(s_hat, 1)

            def down(m):
                pe.wait_ge(s_hate, m + 1)
                if m == 0:
                    pe.wait_ge(s_hwd, 16)
                for n in range(2):
                    if m:
                        pe.wait_ge(s_hye, 2 * (m - 1) + n + 1)
                    for k in range(2):
                        mm = pe.matmul(pY[n][:, :], AT[m % 2][:, k, :], WD[:, k, n * 512:(n + 1) * 512], start=(k == 0), stop=(k == 1))
                    mm.then_inc(s_hy, 1)

            def counts():
                pe.wait_ge(s_sel, 1)
                for w, (p0, p1) in (("ones", (pA[:, :], pB)), ("before", (pC[:, :], pD))):
                    pe.matmul(p0, c(w), f(SEL)[:, 0:512], start=True, stop=True)
                    mm = pe.matmul(p1, c(w), f(SEL)[:, 512:W], start=True, stop=True)
                mm.then_inc(s_cnt, 1)

            def lists():
                pe.wait_ge(s_eb, 1)
                pe.transpose(pE[0:3, :], eb[:, :], c("ident"))
                for t in range(NTT):
                    pe.wait_ge(s_AB, t + 1)
                    for k in range(TK):
                        mm = pe.matmul(pL, A[t][:, k, :], B[t][:, k, :], start=(t == 0 and k == 0), stop=(t == NT and k == TK - 1))
                mm.then_inc(s_lt, 1)

            turn_x(0, 0)
            turn_x(0, 1)
            for m in range(NTT + 1):
                turn_x(m + 1, 0)
                gate_up(m, 0)
                turn_x(m + 1, 1)
                if m:
                    turn_a(m - 1)
                gate_up(m, 1)
                if m:
                    down(m - 1)
                if m == 1:
                    counts()
                if m == NTT - 2:
                    lists()

        @block.vector
        def _(dve):
            link = serial(dve, s_v)
            link(dve.memset(ones[:, :], 1.0))
            link(dve.tensor_scalar(tokf[:, :], c("iota")[:, 0:NTT], float(P), c("part"), ALU.mult, ALU.add))
            dve.wait_ge(s_in, 16)
            dve.wait_ge(s_sg, 1)
            link(dve.tensor_tensor(BI[:, :, :], SC[:, :, :], br[:, :].unsqueeze(1).to_broadcast(sh), ALU.add))
            g4 = lambda a: a[:, :, :].rearrange("p t (g e) -> p t g e", g=NG)
            bc = lambda a: a[:, :, :].unsqueeze(3).to_broadcast([P, NTT, NG, NE // NG])
            link(dve.tensor_reduce(m1[:, :, :], g4(BI), AX.X, ALU.max))
            link(dve.tensor_tensor(g4(S1), g4(BI), bc(m1), ALU.is_equal))
            link(dve.tensor_reduce(cn[:, :, :], g4(S1), AX.X, ALU.add))
            link(dve.scalar_tensor_tensor(out=S1[:, :, :], in0=S1[:, :, :], scalar=NEG, in1=BI[:, :, :], op0=ALU.mult, op1=ALU.add))
            link(dve.tensor_reduce(m2[:, :, :], g4(S1), AX.X, ALU.max))
            link(dve.tensor_scalar(cn[:, :, :], cn[:, :, :], 2.0, -1.0, ALU.is_ge, ALU.add))
            link(dve.scalar_tensor_tensor(out=cn[:, :, :], in0=cn[:, :, :], scalar=-NEG, in1=m1[:, :, :], op0=ALU.mult, op1=ALU.add))
            link(dve.tensor_tensor(m2[:, :, :], m2[:, :, :], cn[:, :, :], ALU.max))
            link(dve.tensor_tensor(m1[:, :, :], m1[:, :, :], m2[:, :, :], ALU.add))
            mine = m1[:, :, :].unsqueeze(3).to_broadcast([P, NTT, NG, NG])
            other = m1[:, :, :].unsqueeze(2).to_broadcast([P, NTT, NG, NG])
            link(dve.tensor_tensor(pw[:, :, :, :], other, mine, ALU.is_gt))
            link(dve.tensor_tensor(pe2[:, :, :, :], other, mine, ALU.is_equal))
            lower = c("lower8").rearrange("p (a b) -> p a b", a=NG).unsqueeze(1).to_broadcast([P, NTT, NG, NG])
            link(dve.tensor_tensor(pe2[:, :, :, :], pe2[:, :, :, :], lower, ALU.mult))
            link(dve.tensor_tensor(pw[:, :, :, :], pw[:, :, :, :], pe2[:, :, :, :], ALU.add))
            link(dve.tensor_reduce(gr[:, :, :], pw[:, :, :, :], AX.X, ALU.add))
            link(dve.tensor_scalar(gr[:, :, :], gr[:, :, :], float(TKG), -1.0, ALU.is_lt, ALU.add))
            link(dve.tensor_scalar(gr[:, :, :], gr[:, :, :], -NEG, None, ALU.mult))
            link(dve.tensor_tensor(g4(BI), g4(BI), bc(gr), ALU.add))
            for t in range(NTT):
                link(dve.max(top[:, t, :], BI[:, t, :]))
            t6 = top[:, :, TK - 1:TK].to_broadcast(sh)
            link(dve.tensor_tensor(S1[:, :, :], BI[:, :, :], t6, ALU.is_gt))
            link(dve.tensor_tensor(S2[:, :, :], BI[:, :, :], t6, ALU.is_equal))
            link(dve.tensor_reduce(need[:, :], S1[:, :, :], AX.X, ALU.add))
            link(dve.tensor_scalar(need[:, :], need[:, :], -1.0, float(TK), ALU.mult, ALU.add))
            for t in range(NTT):
                link(dve.tensor_tensor_scan(SV[:, t, :], ones[:, :], S2[:, t, :], 0.0, ALU.mult, ALU.add))
            link(dve.tensor_tensor(SV[:, :, :], SV[:, :, :], need[:, :].unsqueeze(2).to_broadcast(sh), ALU.is_le))
            link(dve.tensor_tensor(S2[:, :, :], S2[:, :, :], SV[:, :, :], ALU.mult))
            link(dve.tensor_tensor(S1[:, :, :], S1[:, :, :], S2[:, :, :], ALU.add))
            link(dve.tensor_tensor(SEL[:, :, :], S1[:, :, :], c("is_token").unsqueeze(2).to_broadcast(sh), ALU.mult))
            dve.sem_inc(s_sel, 1)
            link(dve.tensor_tensor(GT[:, :, :], SC[:, :, :], S1[:, :, :], ALU.mult))
            link(dve.tensor_reduce(sums[:, :], GT[:, :, :], AX.X, ALU.add))
            link(dve.reciprocal(sums[:, :], sums[:, :]))
            link(dve.tensor_tensor(GT[:, :, :], GT[:, :, :], sums[:, :].unsqueeze(2).to_broadcast(sh), ALU.mult))
            link(dve.tensor_scalar(GT[:, :, :], GT[:, :, :], ROUTED_SCALE, None, ALU.mult))
            dve.wait_ge(s_cnt, 1)
            link(dve.tensor_copy(f(tot)[:, 0:512], pA[:, :]))
            link(dve.tensor_copy(f(tot)[:, 512:W], pB))
            link(dve.tensor_copy(f(pre)[:, 0:512], pC[:, :]))
            link(dve.tensor_copy(f(pre)[:, 512:W], pD))
            link(dve.memset(car[:, 0, :], 0.0))
            for t in range(1, NTT):
                link(dve.tensor_tensor(car[:, t, :], car[:, t - 1, :], tot[:, t - 1, :], ALU.add))
            link(dve.tensor_tensor(nb[:, :], car[:, NTT - 1, :], tot[:, NTT - 1, :], ALU.add))
            link(dve.tensor_scalar(nbi[:, :], nb[:, :], float(P - 1), None, ALU.add))
            link(dve.tensor_scalar(nbi[:, :], nbi[:, :], 7, None, ALU.arith_shift_right))
            link(dve.tensor_copy(nb[:, :], nbi[:, :]))
            link(dve.tensor_tensor_scan(be[:, :], ones[:, :], nb[:, :], 0.0, ALU.mult, ALU.add))
            link(dve.tensor_scalar(S1[:, 0, :], be[:, :], c("part"), 0.0, ALU.is_le, ALU.add, accum_out=eb[:, 0:1]))
            link(dve.tensor_scalar(eb[:, 0:1], eb[:, 0:1], float(NE - 1), None, ALU.min))
            link(dve.tensor_copy(eb[:, 1:2], be[:, NE - 1:NE]))
            link(dve.tensor_scalar(npair[:, :], be[:, NE - 1:NE], 1.0, None, ALU.add))
            link(dve.tensor_scalar(npair[:, :], npair[:, :], 1, None, ALU.arith_shift_right))
            link(dve.tensor_copy(eb[:, 2:3], npair[:, :]))
            dve.sem_inc(s_eb, 1)
            link(dve.tensor_tensor(nb[:, :], be[:, :], nb[:, :], ALU.subtract))
            link(dve.tensor_scalar(nb[:, :], nb[:, :], float(P), 1.0, ALU.mult, ALU.add))
            link(dve.tensor_tensor(SV[:, :, :], pre[:, :, :], car[:, :, :], ALU.add))
            link(dve.tensor_tensor(SV[:, :, :], SV[:, :, :], nb[:, :].unsqueeze(1).to_broadcast(sh), ALU.add))
            link(dve.tensor_tensor(SV[:, :, :], SV[:, :, :], SEL[:, :, :], ALU.mult))
            for t in range(NTT):
                link(dve.max(slotf[:, t, :], SV[:, t, :]))
            link(dve.tensor_scalar(slot[:, :, :], slotf[:, :, :], -1.0, None, ALU.add))
            link(dve.tensor_scalar(part[:, :, :], slot[:, :, :], P - 1, None, ALU.bitwise_and))
            link(dve.tensor_copy(posf[:, :, :], part[:, :, :]))
            link(dve.tensor_scalar(part[:, :, :], slot[:, :, :], 7, None, ALU.arith_shift_right))
            link(dve.tensor_copy(blkf[:, :, :], part[:, :, :]))
            for t in range(NTT):
                dve.tensor_tensor(A[t][:, :, :], c("iota").unsqueeze(1).to_broadcast([P, TK, P]),
                                  posf[:, t, 0:TK].unsqueeze(2).to_broadcast([P, TK, P]), ALU.is_equal)
                for k in range(TK):
                    m = dve.tensor_scalar(B[t][:, k, :], c("iota")[:, 0:NBLK], blkf[:, t, k:k + 1], tokf[:, t:t + 1], ALU.is_equal, ALU.mult)
                m.then_inc(s_AB, 1)
            for k in range(TK):
                link(dve.tensor_tensor(S2[:, :, :], SV[:, :, :], slotf[:, :, k:k + 1].to_broadcast(sh), ALU.is_equal))
                link(dve.tensor_tensor(S2[:, :, :], S2[:, :, :], GT[:, :, :], ALU.mult))
                link(dve.tensor_reduce(G["gate"][:, :, k], S2[:, :, :], AX.X, ALU.add))
            link(dve.tensor_scalar(slotf[:, :, :], slotf[:, :, :], -1.0, 0.0, ALU.add, ALU.max))
            link(dve.tensor_copy(G["slot"][:, :, :], slotf[:, :, :]))
            dve.wait_ge(s_lt, 1)
            link(dve.tensor_copy(G["expert"][:, :], pE[0:3, :]))
            link(dve.tensor_copy(G["list"][:, :], pL))
    with nc.Block() as block:
        @block.sync
        def _(sp):
            for j in range(2):
                sp.dma_start(G["nblk"][0:1, j:j + 1], G["expert"][1 + j:2 + j, 0:1]).then_inc(s_m, 16)
            sp.wait_ge(s_m, 32)


def stage_routed(nc, T, G, sem, sb, ps):
    c, pre, n_pairs = G["c"], "ex_", NBLK // 2
    GU0, Y0, XT0 = 4, 7, 7
    WG = [sb(f"{pre}WG{i}", [P, KD, 2 * DE]) for i in range(4)]
    WD = [sb(f"{pre}WD{i}", [P, 2, D]) for i in range(4)]
    X = [sb(f"{pre}X{i}", [P, D]) for i in range(4)]
    XT = [sb(f"{pre}XT{i}", [P, KD, P]) for i in range(2)]
    sg = [sb(f"{pre}sg{i}", [P, DE]) for i in range(2)]
    av = [sb(f"{pre}av{i}", [P, DE]) for i in range(2)]
    AT = [sb(f"{pre}AT{i}", [P, 2, P]) for i in range(2)]
    Y = [sb(f"{pre}Y{i}", [P, D]) for i in range(2)]
    ix = [sb(f"{pre}ix{i}", [P, 1], I32) for i in range(4)]
    pX, pG, pA, pY = [ps(pre + "pX0"), ps(pre + "pX1")], [ps(pre + "pG0"), ps(pre + "pG1")], ps(pre + "pA"), [ps(pre + "pY0"), ps(pre + "pY1")]
    names = ("ix", "xt", "xe", "gu", "sg", "a1", "a", "at", "ate", "y", "ye", "k")
    s_ix, s_xt, s_xe, s_gu, s_sg, s_a1, s_a, s_at, s_ate, s_y, s_ye, s_k = (sem(pre + n) for n in names)
    s_w, s_wd, s_x = ([sem(f"{pre}{n}{i}") for i in range(4)] for n in ("w", "wd", "x"))
    s_st = [sem(f"{pre}st{i}") for i in range(2)]
    s_z, s_zd = sem(pre + "z"), sem(pre + "zd")
    zero = sb(pre + "zero", [P, D])
    out = T["yblk"]

    def run(eng, pair):
        used = eng.value_load(G["nblk"][0:1, 0:1], min_val=0, max_val=NBLK)
        with eng.Fori(0, n_pairs // 2) as i:
            for q in range(2):
                with eng.If(i * 4 + 2 * q < used):
                    pair(i, q)

    with nc.Block() as block:
        @block.sync
        def _(sp):
            def weights(i, q):
                for u in range(2):
                    b = 2 * q + u
                    e = sp.value_load(G["expert"][0:1, bass.ds(i * 4 + b, 1)], min_val=0, max_val=NE - 1)
                    sp.wait_ge(s_gu, i * 4 + b + 1)
                    sp.dma_start(WG[b][:, :, :], T["w_e_gu"][0, bass.ds(e, 1)].rearrange("a (k p) n -> p (a k) n", p=P)).then_inc(s_w[b], 16)
                    sp.wait_ge(s_y, (i * 4 + b) * 2 + 1)
                    sp.dma_start(WD[b][:, :, :], T["w_e_down"][0, bass.ds(e, 1)].rearrange("a (k p) n -> p (a k) n", p=P)).then_inc(s_wd[b], 16)
            used = sp.value_load(G["nblk"][0:1, 0:1], min_val=0, max_val=NBLK)
            sp.wait_ge(s_z, 1)
            with sp.Fori(0, n_pairs // 2) as i:
                for q in range(2):
                    with sp.If(i * 4 + 2 * q < used):
                        weights(i, q)
                for q in range(2):
                    with sp.If((n_pairs - 1 - q - i * 2) * 2 >= used):
                        sp.dma_start(out.rearrange("(q u p) d -> q p u d", u=2, p=P)[bass.ds(n_pairs - 1 - q - i * 2, 1)]
                                     .rearrange("a p u d -> p (a u) d"),
                                     zero[:, :].unsqueeze(1).to_broadcast([P, 2, D])).then_inc(s_zd, 16)
                        sp.wait_ge(s_zd, (i * 2 + q) * 16 + 16)
                        sp.sem_inc(s_z, 1)

        @block.gpsimd
        def _(pool):
            def gather(i, q):
                for u in range(2):
                    b = 2 * q + u
                    pool.wait_ge(s_xt, (i * 4 + b) * 2 + 1)
                    pool.tensor_copy(ix[b][:, :], G["list"][:, bass.ds(i * 4 + b, 1)]).then_inc(s_ix, 1)
                    pool.wait_ge(s_ix, i * 4 + b + 1)
                    pool.sem_inc(s_k, 1)
                    pool.indirect_dma_start(out=X[b][:, :], out_offset=None, in_=T["h2"],
                                            in_offset=bass.IndirectOffsetOnAxis(ap=ix[b][:, 0:1], axis=0)).then_inc(s_x[b], 16)
            run(pool, gather)

        @block.tensor
        def _(pe):
            for s, start in ((s_xt, XT0), (s_gu, GU0), (s_at, 1), (s_y, Y0)):
                pe.sem_inc(s, start)

            def pair(i, q):
                n0 = i * 4 + 2 * q

                def turn_x(u, n):
                    if n == 0:
                        pe.wait_ge(s_x[2 * q + u], i * 16 + 16)
                    pe.wait_ge(s_xe, (n0 + u) * 2 + n + 1)
                    for k in range(4):
                        m = pe.transpose(pX[n][:, k * P:(k + 1) * P], X[2 * q + u][:, (4 * n + k) * P:(4 * n + k + 1) * P], c("ident"))
                    m.then_inc(s_xt, 1)

                def gate_up(u, n):
                    w = 2 * q + u
                    if n == 0:
                        pe.wait_ge(s_w[w], i * 16 + 16)
                        pe.wait_ge(s_a, n0 + 1)
                    pe.wait_ge(s_xe, (n0 + u) * 2 + n + 1 + 2)
                    for k in range(4 * n, 4 * n + 4):
                        m = pe.matmul(pG[u][:, :], XT[u][:, k, :], WG[w][:, k, :], start=(k == 0), stop=(k == KD - 1))
                    if n:
                        m.then_inc(s_gu, 1)

                def turn_a(u):
                    pe.wait_ge(s_a, n0 + u + 1 + 1)
                    pe.wait_ge(s_ate, n0 + u + 1)
                    for k in range(2):
                        m = pe.transpose(pA[:, k * P:(k + 1) * P], av[u][:, k * P:(k + 1) * P], c("ident"))
                    m.then_inc(s_at, 1)

                def down(u, n):
                    w = 2 * q + u
                    if n == 0:
                        pe.wait_ge(s_ate, n0 + u + 1 + 1)
                        pe.wait_ge(s_wd[w], i * 16 + 16)
                    pe.wait_ge(s_ye, (n0 + u) * 2 + n + 1)
                    for k in range(2):
                        m = pe.matmul(pY[n][:, :], AT[u][:, k, :], WD[w][:, k, n * 512:(n + 1) * 512], start=(k == 0), stop=(k == 1))
                    m.then_inc(s_y, 1)

                turn_x(0, 0)
                turn_x(0, 1)
                gate_up(0, 0)
                turn_x(1, 0)
                gate_up(0, 1)
                turn_x(1, 1)
                gate_up(1, 0)
                turn_a(0)
                gate_up(1, 1)
                down(0, 0)
                turn_a(1)
                down(0, 1)
                down(1, 0)
                down(1, 1)
            run(pe, pair)

        @block.scalar
        def _(act):
            act.sem_inc(s_ye, 2)
            act.sem_inc(s_ate, 1)
            for u in range(2):
                act.dma_start(T["pad"][u:u + 1, :], c("iota")[0:1, :]).then_inc(s_st[u], 16)

            def pair(i, q):
                n0 = i * 4 + 2 * q

                def sigmoid(u):
                    act.wait_ge(s_gu, n0 + u + 1 + GU0)
                    act.wait_ge(s_a1, n0 + 1)
                    act.activation(sg[u][:, :], pG[u][:, 0:DE], ACT.Sigmoid).then_inc(s_sg, 1)

                def take_a(u):
                    act.wait_ge(s_at, n0 + u + 1 + 1)
                    act.wait_ge(s_y, n0 * 2 + Y0)
                    act.activation(AT[u][:, :, :], pA[:, 0:2 * P].rearrange("p (k r) -> p k r", k=2), ACT.Copy).then_inc(s_ate, 1)

                def take_y(u, n):
                    act.wait_ge(s_y, (n0 + u) * 2 + n + 1 + Y0)
                    if n == 0:
                        act.wait_ge(s_st[u], (i * 2 + q) * 16 + 16)
                    act.activation(Y[u][:, n * 512:(n + 1) * 512], pY[n][:, :], ACT.Copy).then_inc(s_ye, 1)

                sigmoid(0)
                take_a(0)
                sigmoid(1)
                take_y(0, 0)
                take_a(1)
                take_y(0, 1)
                take_y(1, 0)
                take_y(1, 1)
                for u in range(2):
                    act.wait_ge(s_ye, (n0 + u) * 2 + 2 + 2)
                    act.dma_start(out.rearrange("(t p) d -> t p d", p=P)[bass.ds(n0 + u, 1)].rearrange("a p d -> p (a d)"),
                                  Y[u][:, :]).then_inc(s_st[u], 16)
            run(act, pair)

        @block.vector
        def _(dve):
            dve.sem_inc(s_xe, 2)
            dve.sem_inc(s_a1, 1)
            dve.sem_inc(s_a, 1)
            dve.memset(zero[:, :], 0.0).then_inc(s_z, 1)

            def pair(i, q):
                n0 = i * 4 + 2 * q
                for u in range(2):
                    for n in range(2):
                        dve.wait_ge(s_xt, (n0 + u) * 2 + n + 1 + XT0)
                        dve.wait_ge(s_gu, n0 + u - 2 + 1 + GU0)
                        dve.tensor_copy(XT[u][:, 4 * n:4 * n + 4, :], pX[n][:, :].rearrange("p (k r) -> p k r", k=4)).then_inc(s_xe, 1)
                for u in range(2):
                    dve.wait_ge(s_sg, n0 + u + 1)
                    dve.tensor_tensor(sg[u][:, :], sg[u][:, :], pG[u][:, 0:DE], ALU.mult).then_inc(s_a1, 1)
                    dve.wait_ge(s_a1, n0 + u + 1 + 1)
                    dve.wait_ge(s_at, n0 + 1)
                    dve.tensor_tensor(av[u][:, :], sg[u][:, :], pG[u][:, DE:2 * DE], ALU.mult).then_inc(s_a, 1)
            run(dve, pair)
    with nc.Block() as block:
        @block.sync
        def _(sp):
            pairs = sp.value_load(G["nblk"][0:1, 1:2], min_val=1, max_val=n_pairs)
            for u in range(2):
                sp.wait_ge(s_st[u], pairs * 16 + 16)
            sp.sem_inc(s_z, 1)


def stage_combine(nc, T, G, sem, sb, ps):
    acc = [sb(f"cacc{i}", [P, D]) for i in range(2)]
    x1 = [sb(f"cx1{i}", [P, D]) for i in range(2)]
    E = [sb(f"cE{i}", [P, TK, D]) for i in range(2)]
    gf, gfs = sb("cgf", [P, D]), sb("cgfs", [NS, D])
    s_m, s_v, s_r = sem("cb_m"), sem("cb_v"), sem("cb_r")
    s_in, s_e, s_o = ([sem(f"cb_{n}{i}") for i in range(2)] for n in ("in", "e", "o"))
    y_p, y_s = T["o0"][0], T["o1"].rearrange("b s d -> (b s) d")
    with nc.Block() as block:
        @block.sync
        def _(sp):
            sp.dma_start(gf[:, :], T["mod"][NS:NC9, 5 * D:6 * D].to_broadcast([P, D])).then_inc(s_m, 16)
            sp.dma_start(gfs[:, :], T["mod"][0:NS, 5 * D:6 * D]).then_inc(s_m, 16)
            for t, R in tiles():
                if t >= 2:
                    sp.wait_ge(s_o[t % 2], 16 * (t // 2))
                sp.dma_start(acc[t % 2][0:R, :], T["ysh"][t * P:t * P + R, :]).then_inc(s_in[t % 2], 16)
                sp.dma_start(x1[t % 2][0:R, :], T["x1"][t * P:t * P + R, :]).then_inc(s_in[t % 2], 16)

        @block.gpsimd
        def _(pool):
            for t, R in tiles():
                if t >= 2:
                    pool.wait_ge(s_r, t - 1)
                for k in range(TK):
                    pool.indirect_dma_start(out=E[t % 2][0:R, k, :], out_offset=None, in_=T["yblk"],
                                            in_offset=bass.IndirectOffsetOnAxis(ap=G["slot"][0:R, t, k:k + 1], axis=0)).then_inc(s_e[t % 2], 16)

        @block.scalar
        def _(act):
            for t, R in tiles():
                act.wait_ge(s_r, t + 1)
                act.dma_start(token_rows(y_p, y_s, t), acc[t % 2][0:R, :]).then_inc(s_o[t % 2], 16)
            act.wait_ge(s_o[0], 16 * 5)
            act.wait_ge(s_o[1], 16 * 4)

        @block.vector
        def _(dve):
            link = serial(dve, s_v)
            dve.wait_ge(s_m, 32)
            for t, R in tiles():
                a = acc[t % 2][0:R, :]
                dve.wait_ge(s_in[t % 2], 32 * (t // 2 + 1))
                dve.wait_ge(s_e[t % 2], 16 * TK * (t // 2 + 1))
                for k in range(TK):
                    link(dve.scalar_tensor_tensor(out=a, in0=E[t % 2][0:R, k, :], scalar=G["gate"][0:R, t, k:k + 1], in1=a,
                                                  op0=ALU.mult, op1=ALU.add))
                link(dve.tensor_tensor(a, a, gf[:, :] if t < NT else gfs[:, :], ALU.mult))
                dve.tensor_tensor(a, a, x1[t % 2][0:R, :], ALU.add).then_inc(s_r, 1)


_INS = ['x_prompt', 'x_sample', 'cache_mla_latent', 'cache_mla_krope', 'cache_dsa_k', 'cache_dsa_v', 'cache_idx_k',
        'page_table', 'c_prompt', 'c_sample', 'rel_bias', 'w_ada', 'b_ada', 'g_attn_norm', 'w_in', 'g_q_lora', 'w_q_up',
        'g_kv_lora', 'w_kv_up', 'g_mla_qn', 'g_mla_qr', 'g_mla_kn', 'g_mla_kr', 'g_dsa_q', 'g_dsa_k', 'w_out', 'g_ffn_norm',
        'w_router', 'b_router', 'w_e_gu', 'w_e_down', 'w_s_gu', 'w_s_down']
_OUTS = [(1, SEQ, D), (NS, 1, D), (1, 1, SEQ, KVL), (1, 1, SEQ, ROPE), (1, 1, SEQ, H, 64), (1, 1, SEQ, H, 64),
         (1, 1, SEQ, IDX), (1, NS, 1, KVL), (1, NS, 1, ROPE), (1, NS, 1, H, 64), (1, NS, 1, H, 64), (1, NS, 1, IDX)]
_SCRATCH = {"mod": (NC9, 6 * D), "p": (NTOK, D_IN), "wi": (NTOK, H), "vm": (NTOK, 512), "vd": (NTOK, 512), "qm": (NTOK, H * QK),
            "qd": (NTOK, 512), "qmT": (H, QK, NTOK), "kmT": (H, QK, NTOK), "tdT": (13, P, NTOK), "mixT": (D, NTOK), "x1": (NTOK, D),
            "h2": ((NT + 1) * P, D), "yblk": (SLOTS, D), "ysh": ((NT + 1) * P, D), "score": (SEQ, SEQ), "omix": (NTOK, D), "pad": (2, P),
            "dpos": (NS // 2, 32, 16), "drow": (NS // 2, 32, 16)}


def kernel(**inputs):
    import concourse.bacc as _bacc
    from concourse.bass_utils import run_bass_kernel_spmd as _run

    nc = _bacc.Bacc("TRN2", target_bir_lowering=False, num_devices=1)
    arrays, T = {}, {}

    def give(name, a):
        a = np.ascontiguousarray(a)
        arrays[f"in_{name}"] = a
        T[name] = nc.dram_tensor(f"in_{name}", a.shape, mybir.dt.from_np(a.dtype), kind="ExternalInput").ap()

    for name in _INS:
        give(name, inputs[name])
    give("const", CONST)
    give("rope", rope_table())
    for name, shape in _SCRATCH.items():
        T[name] = nc.dram_tensor(f"s_{name}", shape, F32).ap()
    for i, shape in enumerate(_OUTS):
        T[f"o{i}"] = nc.dram_tensor(f"out_{i}", shape, F32, kind="ExternalOutput").ap()
    build(nc, T)
    r = _run(nc, [arrays], core_ids=[0])
    return tuple(r.results[0][f"out_{i}"] for i in range(len(_OUTS)))
```
